# Optimizing a Trainium2 kernel written in Bass

```python
import jax, jax.numpy as jnp
from jax import lax
import numpy as np
import math

D_MODEL = 1024
BATCH = 1
SEQ = 256
DEPTH = 2

CHUNK = 64
N_META = 16
CONV_WIDTH = 31
POOL_WINDOWS = (2, 4, 8, 16)
N_POOL_GROUPS = len(POOL_WINDOWS)
POOL_GROUP = D_MODEL // N_POOL_GROUPS
D_FF = 2816
N_EXPERTS = 8
TOP_K = 2
D_FF_EXPERT = 3584
N_MIX_A = (DEPTH + 1) // 2
N_MIX_B = DEPTH // 2
N_DENSE = (DEPTH + 1) // 2
N_MOE = DEPTH // 2
RMS_EPS = 1e-6
LN_EPS = 1e-5


def rms_norm(x, g):
    xf = x.astype(jnp.float32)
    y = xf * lax.rsqrt(jnp.mean(xf * xf, axis=-1, keepdims=True) + RMS_EPS)
    return y.astype(x.dtype) * g

def layer_norm(x, g, b):
    xf = x.astype(jnp.float32)
    mu = jnp.mean(xf, axis=-1, keepdims=True)
    var = jnp.mean(jnp.square(xf - mu), axis=-1, keepdims=True)
    y = (xf - mu) * lax.rsqrt(var + LN_EPS)
    return y.astype(x.dtype) * g + b

def conformer_conv(h, w_pw1, b_pw1, w_dw, b_dw, ln_g, ln_b, w_pw2, b_pw2):
    u = h @ w_pw1 + b_pw1
    a, gate = jnp.split(u, 2, axis=-1)
    u = a * jax.nn.sigmoid(gate)
    u = lax.conv_general_dilated(
        u, w_dw[:, None, :].astype(u.dtype),
        window_strides=(1,), padding=((CONV_WIDTH - 1, 0),),
        dimension_numbers=("NWC", "WIO", "NWC"),
        feature_group_count=D_MODEL) + b_dw
    u = jax.nn.silu(layer_norm(u, ln_g, ln_b))
    return u @ w_pw2 + b_pw2

def multiscale_pool(h, w_group, scale):
    B, L, _ = h.shape
    hg = h.reshape(B, L, N_POOL_GROUPS, POOL_GROUP).astype(jnp.float32)
    pos = jnp.arange(L)
    outs = []
    for gi, w in enumerate(POOL_WINDOWS):
        xg = hg[:, :, gi, :]
        cs = jnp.cumsum(xg, axis=1)
        cs_shift = jnp.pad(cs, ((0, 0), (w, 0), (0, 0)))[:, :L]
        count = jnp.minimum(pos + 1, w).astype(jnp.float32)[None, :, None]
        outs.append((cs - cs_shift) / count - xg)
    pooled = jnp.stack(outs, axis=2).astype(h.dtype)
    mixed = jnp.einsum("blgc,gcd->blgd", pooled, w_group)
    return mixed.reshape(B, L, D_MODEL) * scale

def swiglu(h, w_gate, w_up, w_down):
    return (jax.nn.silu(h @ w_gate) * (h @ w_up)) @ w_down

def moe_swiglu(h, w_router, e_gate, e_up, e_down):
    logits = (h @ w_router).astype(jnp.float32)
    top_vals, top_idx = lax.top_k(logits, TOP_K)
    top_w = jax.nn.softmax(top_vals, axis=-1)
    combine = jnp.sum(jax.nn.one_hot(top_idx, N_EXPERTS, dtype=jnp.float32)
                      * top_w[..., None], axis=-2).astype(h.dtype)
    y = jnp.zeros_like(h)
    for e in range(N_EXPERTS):
        y = y + combine[..., e:e + 1] * swiglu(h, e_gate[e], e_up[e], e_down[e])
    return y

def first_inputs(seed: int = 0) -> dict:
    key = jax.random.key(seed)
    ks = iter(jax.random.split(key, 32))
    D = D_MODEL

    def nrm(shape, fan_in):
        return jax.random.normal(next(ks), shape, jnp.float32) * (fan_in ** -0.5)

    def gain(shape):
        return 1.0 + 0.05 * jax.random.normal(next(ks), shape, jnp.float32)

    def bias(shape):
        return 0.02 * jax.random.normal(next(ks), shape, jnp.float32)

    return {
        "x": jax.random.normal(next(ks), (BATCH, SEQ, D), jnp.float32),
        "meta_tokens": jax.random.normal(next(ks), (N_META, D), jnp.float32),
        "conv_w_pw1": nrm((N_MIX_A, D, 2 * D), D),
        "conv_b_pw1": bias((N_MIX_A, 2 * D)),
        "conv_w_dw": nrm((N_MIX_A, CONV_WIDTH, D), CONV_WIDTH),
        "conv_b_dw": bias((N_MIX_A, D)),
        "conv_ln_g": gain((N_MIX_A, D)),
        "conv_ln_b": bias((N_MIX_A, D)),
        "conv_w_pw2": nrm((N_MIX_A, D, D), D),
        "conv_b_pw2": bias((N_MIX_A, D)),
        "pool_w_group": nrm((N_MIX_B, N_POOL_GROUPS, POOL_GROUP, POOL_GROUP), POOL_GROUP),
        "pool_scale": gain((N_MIX_B, D)),
        "ffn_w_gate": nrm((N_DENSE, D, D_FF), D),
        "ffn_w_up": nrm((N_DENSE, D, D_FF), D),
        "ffn_w_down": nrm((N_DENSE, D_FF, D), D_FF),
        "moe_w_router": nrm((N_MOE, D, N_EXPERTS), D),
        "moe_w_gate": nrm((N_MOE, N_EXPERTS, D, D_FF_EXPERT), D),
        "moe_w_up": nrm((N_MOE, N_EXPERTS, D, D_FF_EXPERT), D),
        "moe_w_down": nrm((N_MOE, N_EXPERTS, D_FF_EXPERT, D), D_FF_EXPERT),
        "mix_norm_g": gain((DEPTH, D)),
        "ffn_norm_g": gain((DEPTH, D)),
        "final_norm_g": gain((D,)),
    }

def first_block(x, meta_tokens,
              conv_w_pw1, conv_b_pw1, conv_w_dw, conv_b_dw, conv_ln_g, conv_ln_b,
              conv_w_pw2, conv_b_pw2,
              pool_w_group, pool_scale,
              ffn_w_gate, ffn_w_up, ffn_w_down,
              moe_w_router, moe_w_gate, moe_w_up, moe_w_down,
              mix_norm_g, ffn_norm_g, final_norm_g):
    B = x.shape[0]
    meta = jnp.broadcast_to(meta_tokens[None].astype(x.dtype), (B, N_META, D_MODEL))
    h = jnp.concatenate([meta, x], axis=1)

    for i in range(DEPTH):
        j = i // 2
        hn = rms_norm(h, mix_norm_g[i])
        if i % 2 == 0:
            h = h + conformer_conv(hn, conv_w_pw1[j], conv_b_pw1[j], conv_w_dw[j],
                                   conv_b_dw[j], conv_ln_g[j], conv_ln_b[j],
                                   conv_w_pw2[j], conv_b_pw2[j])
        else:
            h = h + multiscale_pool(hn, pool_w_group[j], pool_scale[j])
        hn = rms_norm(h, ffn_norm_g[i])
        if i % 2 == 0:
            h = h + swiglu(hn, ffn_w_gate[j], ffn_w_up[j], ffn_w_down[j])
        else:
            h = h + moe_swiglu(hn, moe_w_router[j], moe_w_gate[j], moe_w_up[j], moe_w_down[j])

    h = h[:, N_META:]
    return rms_norm(h, final_norm_g)


DEPTH_2 = 1

HEAD_DIM = 64
NSA_HEADS = 8
NSA_KV_GROUPS = 2
NSA_HPG = NSA_HEADS // NSA_KV_GROUPS
NSA_WIDTH = NSA_HEADS * HEAD_DIM
NSA_KV_WIDTH = NSA_KV_GROUPS * HEAD_DIM
CMP_LEN = 32
CMP_STRIDE = 16
CMP_HIDDEN = 2 * HEAD_DIM
SLC_BLOCK = 64
SLC_TOPN = 16
WINDOW = 512
MOBA_HEADS = 8
MOBA_WIDTH = MOBA_HEADS * HEAD_DIM
MOBA_BLOCK = 256
MOBA_TOPK = 3
TOTAL_HEADS = NSA_HEADS + MOBA_HEADS
Q_CHUNK = 32
COL_WIDTHS = (NSA_WIDTH, 6 * NSA_KV_WIDTH, 3 * NSA_HEADS, NSA_WIDTH, 3 * MOBA_WIDTH, MOBA_WIDTH, 2 * D_MODEL)
IN_COLS = NSA_WIDTH + 6 * NSA_KV_WIDTH + 3 * NSA_HEADS + NSA_WIDTH + 3 * MOBA_WIDTH + MOBA_WIDTH + 2 * D_MODEL


def rms_norm_2(x, g):
    xf = x.astype(jnp.float32)
    y = xf * lax.rsqrt(jnp.mean(xf * xf, axis=-1, keepdims=True) + RMS_EPS)
    return (y * g.astype(jnp.float32)).astype(x.dtype)

def alibi_slopes(n):
    return jnp.asarray((2.0 ** (-8.0 * np.arange(1, n + 1) / n)).astype(np.float32))

def masked_softmax(s, mask):
    s = jnp.where(mask, s, -jnp.inf)
    m = jnp.max(s, axis=-1, keepdims=True)
    m = jnp.where(jnp.isfinite(m), m, 0.0)
    p = jnp.where(mask, jnp.exp(s - m), 0.0)
    return p / jnp.maximum(jnp.sum(p, axis=-1, keepdims=True), 1e-30)

def cmp_to_slc_matrix(n_cmp, n_slc):
    cs = np.arange(n_cmp) * CMP_STRIDE
    ce = cs + CMP_LEN - 1
    ss = np.arange(n_slc) * SLC_BLOCK
    se = ss + SLC_BLOCK - 1
    return ((cs[:, None] <= se[None, :]) & (ce[:, None] >= ss[None, :])).astype(np.float32)

def compress(k, pe, w1, w2):
    S = k.shape[2]
    n_cmp = (S - CMP_LEN) // CMP_STRIDE + 1
    idx = np.arange(n_cmp)[:, None] * CMP_STRIDE + np.arange(CMP_LEN)[None, :]
    blocks = k[:, :, idx] + pe
    h = jax.nn.silu(jnp.einsum('bgnld,lde->bgne', blocks, w1))
    return jnp.einsum('bgne,ef->bgnf', h, w2)

def nsa_attention(q, kc, vc, ks, vs, kw, vw, gates, slopes):
    B, G, P, S, hd = q.shape
    n_cmp = kc.shape[2]
    n_slc = S // SLC_BLOCK
    k_sel = min(SLC_TOPN, n_slc)
    scale = hd ** -0.5
    cmp_end = jnp.asarray(np.arange(n_cmp) * CMP_STRIDE + CMP_LEN - 1, jnp.int32)
    overlap = jnp.asarray(cmp_to_slc_matrix(n_cmp, n_slc))
    ks_b = ks.reshape(B, G, n_slc, SLC_BLOCK, hd)
    vs_b = vs.reshape(B, G, n_slc, SLC_BLOCK, hd)
    kw_p = jnp.pad(kw, ((0, 0), (0, 0), (WINDOW, 0), (0, 0)))
    vw_p = jnp.pad(vw, ((0, 0), (0, 0), (WINDOW, 0), (0, 0)))
    bi = jnp.arange(B)[:, None, None, None]
    gi = jnp.arange(G)[None, :, None, None]
    blk = jnp.arange(n_slc)
    in_blk = jnp.arange(SLC_BLOCK)
    win_off = jnp.arange(WINDOW + Q_CHUNK) - WINDOW
    sl = slopes.astype(jnp.float32)[None, :, :, None, None]

    def chunk(ci):
        c0 = ci * Q_CHUNK
        t = c0 + jnp.arange(Q_CHUNK)
        qc = lax.dynamic_slice_in_dim(q, c0, Q_CHUNK, axis=3)
        g = lax.dynamic_slice_in_dim(gates, c0, Q_CHUNK, axis=4)
        dist = t[:, None] - cmp_end[None, :]
        s = jnp.einsum('bgpqd,bgnd->bgpqn', qc, kc).astype(jnp.float32) * scale - sl * dist.astype(jnp.float32)
        p_cmp = masked_softmax(s, dist >= 0)
        o_cmp = jnp.einsum('bgpqn,bgnd->bgpqd', p_cmp.astype(vc.dtype), vc)
        imp = jnp.einsum('bgpqn,nj->bgqj', p_cmp, overlap)
        cur = t // SLC_BLOCK
        causal_blk = blk[None, :] <= cur[:, None]
        forced = (blk[None, :] == 0) | (blk[None, :] == cur[:, None]) | (blk[None, :] == cur[:, None] - 1)
        imp = jnp.where(forced, jnp.inf, imp)
        imp = jnp.where(causal_blk, imp, -jnp.inf)
        _, sel = lax.top_k(imp, k_sel)
        kg = ks_b[bi, gi, sel]
        vg = vs_b[bi, gi, sel]
        pos = (sel[..., None] * SLC_BLOCK + in_blk).reshape(B, G, 1, Q_CHUNK, k_sel * SLC_BLOCK)
        dist = t[:, None] - pos
        s = jnp.einsum('bgpqd,bgqkld->bgpqkl', qc, kg).reshape(B, G, P, Q_CHUNK, k_sel * SLC_BLOCK)
        s = s.astype(jnp.float32) * scale - sl * dist.astype(jnp.float32)
        p = masked_softmax(s, dist >= 0).astype(vg.dtype).reshape(B, G, P, Q_CHUNK, k_sel, SLC_BLOCK)
        o_slc = jnp.einsum('bgpqkl,bgqkld->bgpqd', p, vg)
        kwin = lax.dynamic_slice_in_dim(kw_p, c0, WINDOW + Q_CHUNK, axis=2)
        vwin = lax.dynamic_slice_in_dim(vw_p, c0, WINDOW + Q_CHUNK, axis=2)
        posw = c0 + win_off
        dist = t[:, None] - posw[None, :]
        mask = (posw[None, :] >= 0) & (dist >= 0) & (dist < WINDOW)
        s = jnp.einsum('bgpqd,bgkd->bgpqk', qc, kwin).astype(jnp.float32) * scale - sl * dist.astype(jnp.float32)
        p = masked_softmax(s, mask).astype(vwin.dtype)
        o_win = jnp.einsum('bgpqk,bgkd->bgpqd', p, vwin)
        return g[0][..., None] * o_cmp + g[1][..., None] * o_slc + g[2][..., None] * o_win

    out = lax.map(chunk, jnp.arange(S // Q_CHUNK))
    return out.transpose(1, 0, 4, 2, 3, 5).reshape(B, S, G * P * hd)

def moba_attention(q, k, v, slopes):
    B, H, S, hd = q.shape
    nb = -(-S // MOBA_BLOCK)
    pad = nb * MOBA_BLOCK - S
    kb = jnp.pad(k, ((0, 0), (0, 0), (0, pad), (0, 0))).reshape(B, H, nb, MOBA_BLOCK, hd)
    vb = jnp.pad(v, ((0, 0), (0, 0), (0, pad), (0, 0))).reshape(B, H, nb, MOBA_BLOCK, hd)
    kbar = jnp.mean(kb.astype(jnp.float32), axis=3)
    k_sel = min(MOBA_TOPK, nb)
    scale = hd ** -0.5
    bi = jnp.arange(B)[:, None, None, None]
    hi = jnp.arange(H)[None, :, None, None]
    offs = jnp.arange(MOBA_BLOCK)
    blocks = jnp.arange(nb)
    sl = slopes.astype(jnp.float32)[None, :, None, None]

    def chunk(ci):
        c0 = ci * Q_CHUNK
        t = c0 + jnp.arange(Q_CHUNK)
        cur = c0 // MOBA_BLOCK
        qc = lax.dynamic_slice_in_dim(q, c0, Q_CHUNK, axis=2)
        gate = jnp.einsum('bhqd,bhnd->bhqn', qc.astype(jnp.float32), kbar)
        gate = jnp.where(blocks < cur, gate, -jnp.inf)
        _, sel = lax.top_k(gate, k_sel)
        valid = sel < cur
        kg = kb[bi, hi, sel]
        vg = vb[bi, hi, sel]
        ko = lax.dynamic_index_in_dim(kb, cur, axis=2, keepdims=False)
        vo = lax.dynamic_index_in_dim(vb, cur, axis=2, keepdims=False)
        n_sel = k_sel * MOBA_BLOCK
        s_sel = jnp.einsum('bhqd,bhqkld->bhqkl', qc, kg).reshape(B, H, Q_CHUNK, n_sel)
        s_own = jnp.einsum('bhqd,bhld->bhql', qc, ko)
        s = jnp.concatenate([s_sel, s_own], axis=-1).astype(jnp.float32) * scale
        pos_sel = (sel[..., None] * MOBA_BLOCK + offs).reshape(B, H, Q_CHUNK, n_sel)
        pos_own = jnp.broadcast_to(cur * MOBA_BLOCK + offs, (B, H, Q_CHUNK, MOBA_BLOCK))
        pos = jnp.concatenate([pos_sel, pos_own], axis=-1)
        dist = t[:, None] - pos
        mask_sel = jnp.broadcast_to(valid[..., None], (B, H, Q_CHUNK, k_sel, MOBA_BLOCK)).reshape(B, H, Q_CHUNK, n_sel)
        mask = jnp.concatenate([mask_sel, dist[..., n_sel:] >= 0], axis=-1)
        s = s - sl * dist.astype(jnp.float32)
        p = masked_softmax(s, mask).astype(v.dtype)
        p_sel = p[..., :n_sel].reshape(B, H, Q_CHUNK, k_sel, MOBA_BLOCK)
        p_own = p[..., n_sel:]
        return jnp.einsum('bhqkl,bhqkld->bhqd', p_sel, vg) + jnp.einsum('bhql,bhld->bhqd', p_own, vo)

    out = lax.map(chunk, jnp.arange(S // Q_CHUNK))
    return out.transpose(1, 0, 3, 2, 4).reshape(B, S, H * hd)

def hybrid_layer(x, norm_pre, w_in, pe_k, w1_k, w2_k, pe_v, w1_v, w2_v, w_a, w_b, w_o, norm_post):
    B, S, _ = x.shape
    G, P, hd = NSA_KV_GROUPS, NSA_HPG, HEAD_DIM
    u = rms_norm_2(x, norm_pre)
    proj = u @ w_in
    splits = [int(c) for c in np.cumsum(COL_WIDTHS)[:-1]]
    q_a, kv_a, g_a, z_a, qkv_b, z_b, merge = jnp.split(proj, splits, axis=-1)
    slopes = alibi_slopes(TOTAL_HEADS)
    q_a = q_a.reshape(B, S, G, P, hd).transpose(0, 2, 3, 1, 4)
    kv_a = kv_a.reshape(B, S, 6, G, hd).transpose(2, 0, 3, 1, 4)
    kc = compress(kv_a[0], pe_k, w1_k, w2_k)
    vc = compress(kv_a[1], pe_v, w1_v, w2_v)
    gates_a = jax.nn.sigmoid(g_a).reshape(B, S, 3, G, P).transpose(2, 0, 3, 4, 1)
    o_a = nsa_attention(q_a, kc, vc, kv_a[2], kv_a[3], kv_a[4], kv_a[5], gates_a,
                        slopes[0::2].reshape(G, P))
    y_a = o_a * jax.nn.silu(z_a)
    qkv_b = qkv_b.reshape(B, S, 3, MOBA_HEADS, hd).transpose(2, 0, 3, 1, 4)
    o_b = moba_attention(qkv_b[0], qkv_b[1], qkv_b[2], slopes[1::2])
    y_b = o_b * jax.nn.silu(z_b)
    gate_a, gate_b = jnp.split(merge, 2, axis=-1)
    m = jax.nn.sigmoid(gate_a) * (y_a @ w_a) + jax.nn.sigmoid(gate_b) * (y_b @ w_b)
    return x + rms_norm_2(m @ w_o, norm_post)

def second_inputs(seed: int = 0) -> dict:
    key = jax.random.key(seed)
    ks = jax.random.split(key, 13)

    def nrm(k, shape, s):
        return jax.random.normal(k, shape, jnp.float32) * s

    return {
        'x': nrm(ks[0], (BATCH, SEQ, D_MODEL), 1.0),
        'norm_pre': 1.0 + nrm(ks[1], (DEPTH_2, D_MODEL), 0.1),
        'w_in': nrm(ks[2], (DEPTH_2, D_MODEL, IN_COLS), D_MODEL ** -0.5),
        'cmp_pe_k': nrm(ks[3], (DEPTH_2, CMP_LEN, HEAD_DIM), 0.1),
        'cmp_w1_k': nrm(ks[4], (DEPTH_2, CMP_LEN, HEAD_DIM, CMP_HIDDEN), (CMP_LEN * HEAD_DIM) ** -0.5),
        'cmp_w2_k': nrm(ks[5], (DEPTH_2, CMP_HIDDEN, HEAD_DIM), CMP_HIDDEN ** -0.5),
        'cmp_pe_v': nrm(ks[6], (DEPTH_2, CMP_LEN, HEAD_DIM), 0.1),
        'cmp_w1_v': nrm(ks[7], (DEPTH_2, CMP_LEN, HEAD_DIM, CMP_HIDDEN), (CMP_LEN * HEAD_DIM) ** -0.5),
        'cmp_w2_v': nrm(ks[8], (DEPTH_2, CMP_HIDDEN, HEAD_DIM), CMP_HIDDEN ** -0.5),
        'w_branch_a': nrm(ks[9], (DEPTH_2, NSA_WIDTH, D_MODEL), NSA_WIDTH ** -0.5),
        'w_branch_b': nrm(ks[10], (DEPTH_2, MOBA_WIDTH, D_MODEL), MOBA_WIDTH ** -0.5),
        'w_o': nrm(ks[11], (DEPTH_2, D_MODEL, D_MODEL), D_MODEL ** -0.5),
        'norm_post': 1.0 + nrm(ks[12], (DEPTH_2, D_MODEL), 0.1),
    }

def second_block(x, norm_pre, w_in, cmp_pe_k, cmp_w1_k, cmp_w2_k, cmp_pe_v, cmp_w1_v, cmp_w2_v,
              w_branch_a, w_branch_b, w_o, norm_post):
    h = x
    for l in range(DEPTH_2):
        h = hybrid_layer(h, norm_pre[l], w_in[l], cmp_pe_k[l], cmp_w1_k[l], cmp_w2_k[l],
                         cmp_pe_v[l], cmp_w1_v[l], cmp_w2_v[l], w_branch_a[l], w_branch_b[l],
                         w_o[l], norm_post[l])
    return h


DEPTH_3 = 1

LRU_W = 256
LRU_BLOCKS = 4
LRU_BLOCK_W = LRU_W // LRU_BLOCKS
LRU_C = 8.0
CONV_W = 4
MLSTM_HEADS = 4
MLSTM_HEAD_DIM = 64
MLSTM_W = MLSTM_HEADS * MLSTM_HEAD_DIM
MLSTM_CHUNK = 64
SB_HEADS = 4
SB_HEAD_DIM = 64
SB_W = SB_HEADS * SB_HEAD_DIM
SB_BLOCK = 128
FF = ((8 * D_MODEL // 3 + 255) // 256) * 256
EPS = 1e-6

SPLIT_SIZES = (LRU_W, LRU_W, 2 * MLSTM_W, MLSTM_W, MLSTM_W, MLSTM_HEADS, MLSTM_HEADS,
               SB_W, SB_W, SB_W, D_MODEL, D_MODEL, D_MODEL)
IN_COLS_3 = sum(SPLIT_SIZES)


def rmsnorm(x, g):
    xf = x.astype(jnp.float32)
    y = xf * lax.rsqrt(jnp.mean(xf * xf, axis=-1, keepdims=True) + EPS)
    return (y * g.astype(jnp.float32)).astype(x.dtype)

def causal_dwconv(x, w):
    K, C = w.shape
    return lax.conv_general_dilated(
        x, w.astype(x.dtype)[:, None, :], window_strides=(1,), padding=[(K - 1, 0)],
        dimension_numbers=("NWC", "WIO", "NWC"), feature_group_count=C)

def to_heads(t, n_heads):
    B, S, W = t.shape
    return t.reshape(B, S, n_heads, W // n_heads).transpose(0, 2, 1, 3)

def from_heads(t):
    B, H, S, d = t.shape
    return t.transpose(0, 2, 1, 3).reshape(B, S, H * d)

def rg_lru(xb, wa, ba, wx, bx, lam):
    B, S, W = xb.shape
    xf = xb.astype(jnp.float32)
    xh = xf.reshape(B, S, LRU_BLOCKS, LRU_BLOCK_W)
    r = jax.nn.sigmoid(jnp.einsum('bsgi,gij->bsgj', xh, wa.astype(jnp.float32)).reshape(B, S, W)
                       + ba.astype(jnp.float32))
    i = jax.nn.sigmoid(jnp.einsum('bsgi,gij->bsgj', xh, wx.astype(jnp.float32)).reshape(B, S, W)
                       + bx.astype(jnp.float32))
    log_a = -LRU_C * r * jax.nn.softplus(-lam.astype(jnp.float32))
    a = jnp.exp(log_a)
    u = jnp.sqrt(-jnp.expm1(2.0 * log_a)) * (i * xf)

    def combine(left, right):
        a1, b1 = left
        a2, b2 = right
        return a1 * a2, a2 * b1 + b2

    _, h = lax.associative_scan(combine, (a, u), axis=1)
    return h.astype(xb.dtype)

def mlstm_chunkwise(q, k, v, i_pre, f_pre):
    B, H, S, dk = q.shape
    dv = v.shape[-1]
    L = MLSTM_CHUNK
    nc = S // L
    out_dtype = v.dtype
    q = q.astype(jnp.float32)
    k = k.astype(jnp.float32) * (dk ** -0.5)
    v = v.astype(jnp.float32)
    logi = i_pre.astype(jnp.float32)
    logf = jax.nn.log_sigmoid(f_pre.astype(jnp.float32))

    def chunks(t):
        return jnp.moveaxis(t.reshape((B, H, nc, L) + t.shape[3:]), 2, 0)

    tril = jnp.tril(jnp.ones((L, L), dtype=bool))

    def step(carry, inp):
        C, n, m = carry
        qc, kc, vc, ic, fc = inp
        b = jnp.cumsum(fc, axis=-1)
        D = jnp.where(tril, b[..., :, None] - b[..., None, :] + ic[..., None, :], -jnp.inf)
        m_inter = b + m[..., None]
        m_t = jnp.maximum(jnp.max(D, axis=-1), m_inter)
        P = jnp.exp(D - m_t[..., None]) * jnp.einsum('bhtk,bhsk->bhts', qc, kc)
        decay = jnp.exp(m_inter - m_t)
        num = (jnp.einsum('bhts,bhsv->bhtv', P, vc)
               + decay[..., None] * jnp.einsum('bhvk,bhtk->bhtv', C, qc))
        den = jnp.sum(P, axis=-1) + decay * jnp.einsum('bhk,bhtk->bht', n, qc)
        h = num / jnp.maximum(jnp.abs(den), jnp.exp(-m_t))[..., None]
        bL = b[..., -1]
        g = bL[..., None] - b + ic
        m_new = jnp.maximum(bL + m, jnp.max(g, axis=-1))
        wts = jnp.exp(g - m_new[..., None])
        carry_decay = jnp.exp(bL + m - m_new)
        C = carry_decay[..., None, None] * C + jnp.einsum('bhs,bhsv,bhsk->bhvk', wts, vc, kc)
        n = carry_decay[..., None] * n + jnp.einsum('bhs,bhsk->bhk', wts, kc)
        return (C, n, m_new), h

    init = (jnp.zeros((B, H, dv, dk), jnp.float32), jnp.zeros((B, H, dk), jnp.float32),
            jnp.zeros((B, H), jnp.float32))
    _, hs = lax.scan(step, init, (chunks(q), chunks(k), chunks(v), chunks(logi), chunks(logf)))
    return jnp.moveaxis(hs, 0, 2).reshape(B, H, S, dv).astype(out_dtype)

def stick_breaking_attention(q, k, v):
    B, H, S, d = q.shape
    nb = S // SB_BLOCK
    scale = 1.0 / math.sqrt(d)
    loc = jnp.arange(SB_BLOCK)
    diag_mask = loc[None, :] < loc[:, None]
    outs = []
    for bi in range(nb):
        nk = bi + 1
        lk_len = nk * SB_BLOCK
        qblk = q[:, :, bi * SB_BLOCK:(bi + 1) * SB_BLOCK]
        kk = k[:, :, :lk_len]
        vv = v[:, :, :lk_len]
        z = jnp.einsum('bhqd,bhsd->bhqs', qblk, kk).astype(jnp.float32) * scale
        causal = jnp.concatenate(
            [jnp.ones((SB_BLOCK, lk_len - SB_BLOCK), dtype=bool), diag_mask], axis=1)
        log_keep = jnp.where(causal, jax.nn.log_sigmoid(-z), 0.0)
        intra = lax.cumsum(log_keep.reshape(B, H, SB_BLOCK, nk, SB_BLOCK), axis=4, reverse=True)
        bsum = intra[..., 0]
        inter = lax.cumsum(bsum, axis=3, reverse=True) - bsum
        R = (intra + inter[..., None]).reshape(B, H, SB_BLOCK, lk_len)
        A = jnp.where(causal, jnp.exp(z + R), 0.0)
        outs.append(jnp.einsum('bhqs,bhsd->bhqd', A.astype(v.dtype), vv))
    return jnp.concatenate(outs, axis=2)

def third_inputs(seed: int = 0) -> dict:
    key = jax.random.key(seed)
    ks = jax.random.split(key, 24)
    f32 = jnp.float32
    D = D_MODEL

    def nrm(k, shape, fan_in):
        return jax.random.normal(k, shape, f32) * (fan_in ** -0.5)

    a0 = jax.random.uniform(ks[8], (DEPTH_3, LRU_W), f32, 0.9, 0.999)
    s0 = a0 ** (1.0 / LRU_C)
    lru_lambda = jnp.log(s0) - jnp.log1p(-s0)
    fg_b = (jnp.linspace(3.0, 6.0, MLSTM_HEADS, dtype=f32)[None, :]
            + 0.1 * jax.random.normal(ks[11], (DEPTH_3, MLSTM_HEADS), f32))
    return {
        "x": jax.random.normal(ks[0], (BATCH, SEQ, D), f32),
        "norm_mix_g": 1.0 + 0.02 * jax.random.normal(ks[1], (DEPTH_3, D), f32),
        "w_in": nrm(ks[2], (DEPTH_3, D, IN_COLS_3), D),
        "conv_lru_w": nrm(ks[3], (DEPTH_3, CONV_W, LRU_W), CONV_W),
        "lru_wa": nrm(ks[4], (DEPTH_3, LRU_BLOCKS, LRU_BLOCK_W, LRU_BLOCK_W), LRU_BLOCK_W),
        "lru_ba": 0.02 * jax.random.normal(ks[5], (DEPTH_3, LRU_W), f32),
        "lru_wx": nrm(ks[6], (DEPTH_3, LRU_BLOCKS, LRU_BLOCK_W, LRU_BLOCK_W), LRU_BLOCK_W),
        "lru_bx": 0.02 * jax.random.normal(ks[7], (DEPTH_3, LRU_W), f32),
        "lru_lambda": lru_lambda,
        "conv_mlstm_w": nrm(ks[9], (DEPTH_3, CONV_W, 2 * MLSTM_W), CONV_W),
        "mlstm_ig_b": 0.1 * jax.random.normal(ks[10], (DEPTH_3, MLSTM_HEADS), f32),
        "mlstm_fg_b": fg_b,
        "w_out_lru": nrm(ks[12], (DEPTH_3, LRU_W, D), LRU_W),
        "w_out_mlstm": nrm(ks[13], (DEPTH_3, MLSTM_W, D), MLSTM_W),
        "w_out_sb": nrm(ks[14], (DEPTH_3, SB_W, D), SB_W),
        "w_o": nrm(ks[15], (DEPTH_3, D, D), D),
        "norm_ffn_g": 1.0 + 0.02 * jax.random.normal(ks[16], (DEPTH_3, D), f32),
        "w_ffn_in": nrm(ks[17], (DEPTH_3, D, 2 * FF), D),
        "w_ffn_out": nrm(ks[18], (DEPTH_3, FF, D), FF),
        "final_norm_g": 1.0 + 0.02 * jax.random.normal(ks[19], (D,), f32),
    }

def third_block(x, norm_mix_g, w_in, conv_lru_w, lru_wa, lru_ba, lru_wx, lru_bx, lru_lambda,
              conv_mlstm_w, mlstm_ig_b, mlstm_fg_b, w_out_lru, w_out_mlstm, w_out_sb, w_o,
              norm_ffn_g, w_ffn_in, w_ffn_out, final_norm_g):
    split_points = np.cumsum(SPLIT_SIZES)[:-1].tolist()
    for l in range(DEPTH_3):
        h = rmsnorm(x, norm_mix_g[l])
        proj = h @ w_in[l]
        (lru_x, lru_gate, m_qk, m_v, m_o, m_i, m_f,
         s_q, s_k, s_v, g_a, g_b, g_c) = jnp.split(proj, split_points, axis=-1)

        xa = causal_dwconv(lru_x, conv_lru_w[l])
        ya = rg_lru(xa, lru_wa[l], lru_ba[l], lru_wx[l], lru_bx[l], lru_lambda[l])
        ya = (ya * jax.nn.gelu(lru_gate)) @ w_out_lru[l]

        qk = jax.nn.silu(causal_dwconv(m_qk, conv_mlstm_w[l]))
        mq, mk = jnp.split(qk, 2, axis=-1)
        i_pre = (m_i + mlstm_ig_b[l]).transpose(0, 2, 1)
        f_pre = (m_f + mlstm_fg_b[l]).transpose(0, 2, 1)
        hb = mlstm_chunkwise(to_heads(mq, MLSTM_HEADS), to_heads(mk, MLSTM_HEADS),
                             to_heads(m_v, MLSTM_HEADS), i_pre, f_pre)
        yb = (jax.nn.sigmoid(m_o) * from_heads(hb)) @ w_out_mlstm[l]

        hc = stick_breaking_attention(to_heads(s_q, SB_HEADS), to_heads(s_k, SB_HEADS),
                                      to_heads(s_v, SB_HEADS))
        yc = from_heads(hc) @ w_out_sb[l]

        merged = (jax.nn.sigmoid(g_a) * ya + jax.nn.sigmoid(g_b) * yb
                  + jax.nn.sigmoid(g_c) * yc)
        x = x + merged @ w_o[l]

        hf = rmsnorm(x, norm_ffn_g[l])
        gate, up = jnp.split(hf @ w_ffn_in[l], 2, axis=-1)
        x = x + (jax.nn.silu(gate) * up) @ w_ffn_out[l]
    return rmsnorm(x, final_norm_g)


def setup_inputs(seed=0):
    out = dict(first_inputs(seed))
    for name, value in second_inputs(seed + 1).items():
        if name != "x":
            out[name + "_2"] = value
    for name, value in third_inputs(seed + 2).items():
        if name != "x":
            out[name + "_3"] = value
    return out


def reference(
    x, meta_tokens, conv_w_pw1, conv_b_pw1, conv_w_dw, conv_b_dw, conv_ln_g, conv_ln_b,
    conv_w_pw2, conv_b_pw2, pool_w_group, pool_scale, ffn_w_gate, ffn_w_up, ffn_w_down,
    moe_w_router, moe_w_gate, moe_w_up, moe_w_down, mix_norm_g, ffn_norm_g, final_norm_g,
    norm_pre_2, w_in_2, cmp_pe_k_2, cmp_w1_k_2, cmp_w2_k_2, cmp_pe_v_2, cmp_w1_v_2, cmp_w2_v_2,
    w_branch_a_2, w_branch_b_2, w_o_2, norm_post_2, norm_mix_g_3, w_in_3, conv_lru_w_3,
    lru_wa_3, lru_ba_3, lru_wx_3, lru_bx_3, lru_lambda_3, conv_mlstm_w_3, mlstm_ig_b_3,
    mlstm_fg_b_3, w_out_lru_3, w_out_mlstm_3, w_out_sb_3, w_o_3, norm_ffn_g_3, w_ffn_in_3,
    w_ffn_out_3, final_norm_g_3,
):
    x = first_block(
        x, meta_tokens, conv_w_pw1, conv_b_pw1, conv_w_dw, conv_b_dw, conv_ln_g, conv_ln_b,
        conv_w_pw2, conv_b_pw2, pool_w_group, pool_scale, ffn_w_gate, ffn_w_up, ffn_w_down,
        moe_w_router, moe_w_gate, moe_w_up, moe_w_down, mix_norm_g, ffn_norm_g, final_norm_g,
    )
    x = second_block(
        x, norm_pre_2, w_in_2, cmp_pe_k_2, cmp_w1_k_2, cmp_w2_k_2, cmp_pe_v_2, cmp_w1_v_2,
        cmp_w2_v_2, w_branch_a_2, w_branch_b_2, w_o_2, norm_post_2,
    )
    return third_block(
        x, norm_mix_g_3, w_in_3, conv_lru_w_3, lru_wa_3, lru_ba_3, lru_wx_3, lru_bx_3,
        lru_lambda_3, conv_mlstm_w_3, mlstm_ig_b_3, mlstm_fg_b_3, w_out_lru_3, w_out_mlstm_3,
        w_out_sb_3, w_o_3, norm_ffn_g_3, w_ffn_in_3, w_ffn_out_3, final_norm_g_3,
    )


_drawn_inputs = setup_inputs


def setup_inputs(seed=0):
    import zlib

    import numpy as np

    out = dict(_drawn_inputs(seed))
    spreads = {}
    factors = {'cmp_pe_k_2': 8.0,
     'norm_mix_g_3': 5.151,
     'lru_ba_3': 26.22,
     'lru_bx_3': 8.0,
     'mlstm_ig_b_3': 64.0,
     'norm_ffn_g_3': 5.549,
     'final_norm_g_3': 7.673}
    for name, (base, spread) in spreads.items():
        noise = np.random.default_rng([zlib.crc32(name.encode()), seed]).standard_normal(out[name].shape)
        drawn = base * np.exp(spread * noise) if base else spread * noise
        out[name] = __import__('jax').numpy.asarray(drawn.astype(out[name].dtype))
    for name, factor in factors.items():
        out[name] = (out[name] * factor).astype(out[name].dtype)
    return out
```

```python
from contextlib import ExitStack

import numpy as np
import concourse.bass as bass
from concourse import mybir

F32 = mybir.dt.float32
U32 = mybir.dt.uint32
ALU = mybir.AluOpType
ACT = mybir.ActivationFunctionType
AX = mybir.AxisListType

P = 128
D = 1024
KD = D // P
META = 16
SEQ = 256
T0 = META + SEQ
CONVW = 31
FF = 2816
KF = FF // P
E_FF = 3584
KE = E_FF // P
NE = 8
WIDE = 256
CH = 12
RING = 7
PE_TAPS = 16
NEG = -1.0e30
EPS = 1e-6
LN_EPS = 1e-5
CMP_N = 15

VECS = [
    ("b_pw1", 16), ("w_dw", KD * CONVW), ("b_dw", 8), ("ln_g", 8), ("ln_b", 8), ("b_pw2", 8),
    ("pool_scale", 8), ("mix_g0", 8), ("mix_g1", 8), ("ffn_g0", 8), ("ffn_g1", 8), ("final_g", 8),
    ("pre_g", 8), ("post_g", 8), ("mix3_g", 8), ("ffn3_g", 8), ("final3_g", 8),
    ("conv3", 6 * 4), ("lru_ba", 2), ("lru_bx", 2), ("lru_lam", 2), ("ig_b", 1), ("fg_b", 1),
    ("router", KD * NE), ("w_gates", KD * 24), ("w_if", KD * 8), ("w2k", 64), ("w2v", 64),
    ("pek", 32), ("pev", 32), ("lru_wa", 2 * 64), ("lru_wx", 2 * 64),
]
VOFF = {}
NV = 0
for _name, _n in VECS:
    VOFF[_name] = NV
    NV += _n

STAGES = [
    ("pw1", 8 * KD), ("pw2", 4 * KD), ("ffn0_in", KF * KD), ("ffn0_out", 4 * KF), ("pool", 8), ("pad", 4),
    ("moe", NE * (KE * KD + 4 * KE)),
    ("w_in2", 23 * KD), ("cmp", 32), ("branch", 4 * KD), ("w_o2", 4 * KD),
    ("w_in3", 21 * KD), ("outs3", 4 * 6), ("w_o3", 4 * KD), ("ffn3_in", KF * KD), ("ffn3_out", 4 * KF),
]
BOFF = {}
NBLK = 0
for _name, _n in STAGES:
    BOFF[_name] = NBLK
    NBLK += _n
NCH = -(-NBLK // (CH * RING)) * RING
assert BOFF["moe"] % CH == 0
MOE_BLK = KE * KD + 4 * KE
MOE_CH = MOE_BLK // CH
assert MOE_BLK % CH == 0 and MOE_CH % RING == 0


def nsa_slope(g, p):
    return float(np.float32(2.0 ** (-8.0 * (2 * (4 * g + p) + 1) / 16)))


def moba_slope(h):
    return float(np.float32(2.0 ** (-8.0 * (2 * h + 2) / 16)))


def program(nc, w_stream, vec_in, h_in, out):
    with ExitStack() as ctx:
        def sb(name, shape, dt=F32):
            return ctx.enter_context(nc.sbuf_tensor(name, shape, dt))

        def sem(name):
            return ctx.enter_context(nc.semaphore(name))

        ps = ctx.enter_context(nc.psum_tensor("ps", [P, 8, 512], F32))
        ring = sb("ring", [P, RING, CH * WIDE])
        vec = sb("vec", [P, NV])
        h = sb("h", [P, KD, T0])
        x = sb("x", [P, KD, SEQ])
        hn = sb("hn", [P, KD, T0])
        sq = sb("sq", [P, KD, T0])
        big = sb("big", [P, 12032])
        scr = sb("scr", [P, 5120])
        gate_sb = sb("gate_sb", [P, 2, T0])
        up_sb = sb("up_sb", [P, 2, SEQ])
        var = sb("var", [P, T0])
        rstd = sb("rstd", [P, T0])
        ident = sb("ident", [P, P])
        ones = sb("ones", [P, 2 * P])
        tri = sb("tri", [P, P])
        sel = sb("sel", [8, 8, P])
        alibi = sb("alibi", [P, 2 * P])
        cbias = sb("cbias", [P, 2, 16])
        tmask = sb("tmask", [P, 3 * P])
        smask = sb("smask", [P, 3 * P])
        iota8 = sb("iota8", [P, 8])
        small = sb("small", [P, 512])
        idx_u = sb("idx_u", [P, 2, 8], U32)

        def vcol(name, j=0, n=1, rows=P):
            return vec[0:rows, VOFF[name] + j:VOFF[name] + j + n]

        conv_u = big[:, 0:KD * 302].rearrange("p (k t) -> p k t", k=KD)
        conv_y = big[:, 2432:2432 + KD * T0].rearrange("p (k t) -> p k t", k=KD)
        diag = big[:, 4608:4608 + 2 * PE_TAPS * P].rearrange("p (b t c) -> p b t c", b=2, c=P)
        hid0 = big[:, 0:KF * T0].rearrange("p (k t) -> p k t", k=KF)
        pool_a = big[:, 6000:6000 + 2 * T0].rearrange("p (k t) -> p k t", k=2)
        pool_b = big[:, 6600:6600 + 2 * T0].rearrange("p (k t) -> p k t", k=2)
        hid = big[:, 0:KE * SEQ].rearrange("p (k t) -> p k t", k=KE)
        comb_b = big[:, 7168:7168 + NE * SEQ].rearrange("p (e t) -> p e t", e=NE)
        proj = big[:, 0:40 * SEQ].rearrange("p (k t) -> p k t", k=40)
        vtok = big[:, 10240:10240 + 1536].rearrange("p (t c) -> p t c", t=2)
        mean = gate_sb[:, 0, :]
        zo = proj[:, 0:8, :]
        sq256 = sq[:, :, 0:SEQ]
        hn256 = hn[:, :, 0:SEQ]
        soft = scr[:, 0:2048].rearrange("p (b a k) -> p b a k", b=2, a=4)
        probT = scr[:, 2048:2048 + 2560].rearrange("p (u c) -> p u c", u=5)
        part = scr[:, 0:1536].rearrange("p (b n k) -> p b n k", b=2, n=3)
        logit = small[:, 0:16].rearrange("p (t e) -> p t e", t=2)
        top = small[:, 16:32].rearrange("p (t e) -> p t e", t=2)
        top_i = small[:, 32:48].rearrange("p (t e) -> p t e", t=2)
        gap = small[:, 48:64].rearrange("p (t e) -> p t e", t=2)
        comb = small[:, 64:80].rearrange("p (t e) -> p t e", t=2)
        comb1 = small[:, 80:96].rearrange("p (t e) -> p t e", t=2)
        cmp_h = small[:, 128:192].rearrange("p (n c) -> p n c", n=4)
        cmp_k = small[:, 192:208]
        cmp_v = small[:, 256:384]
        gates = small[:, 384:432]
        stats = small[:, 432:464].rearrange("p (b n c) -> p b n c", b=2, n=4)
        ccol = small[:, 464:472]
        lam = small[:, 472:488].rearrange("p (n c) -> p n c", n=8)
        cmp_pe = small[:, 488:490]
        v3 = big[:, 10240:10240 + 1024].rearrange("p (t c) -> p t c", t=2)
        crow, mrow, floor = (big[0:4, 11264 + 256 * n:11520 + 256 * n] for n in range(3))
        irow, frow = (big[0:4, 9728 + 256 * n:9984 + 256 * n] for n in range(2))
        arow, brow = up_sb[0:4, 0, :], up_sb[0:4, 1, :]
        hflat = h[:, :, :].rearrange("p k t -> p (k t)")
        cin = hflat[:, 0:6 * 259].rearrange("p (k t) -> p k t", k=6)
        cpad = cin[:, :, 0:3]
        sb_lk = big[:, 0:1536].rearrange("p (h c) -> p h c", h=4)
        sb_w = sq[:, :, :].rearrange("p k t -> p (k t)")[:, 0:1536].rearrange("p (h c) -> p h c", h=4)
        zs = hn[:, :, :].rearrange("p k t -> p (k t)")[:, 0:1536].rearrange("p (h c) -> p h c", h=4)
        decay = zs
        xa = scr[:, 0:512].rearrange("p (k t) -> p k t", k=2)
        qk3 = scr[:, 512:1536].rearrange("p (k t) -> p k t", k=4)
        y3 = scr[:, 1536:3072].rearrange("p (k t) -> p k t", k=6)
        lru_t = scr[:, 3072:5120].rearrange("p (n k t) -> p n k t", n=4, k=2)
        part3 = scr[:, 3072:3072 + 1536].rearrange("p (b n k) -> p b n k", b=2, n=3)

        chunk_landed = [sem(f"chunk_landed{s}") for s in range(RING)]
        chunk_begun = sem("chunk_begun")
        S = {}
        for n in """vec_landed h_landed consts_ready pool_step dve_step act_step
                    sq_ready sum_done var_ready std_ready normed
                    pw1_done glu_sig glu_done diag_ready conv_done conv_ready mean_done xc_ready ln_ready
                    ln_silu pw2_done h1_ready ffn_gu ffn_sig ffn_hid ffn_down ffn_out
                    pooled pool_done x_ready router_done gap_ready gap_exp comb_ready combT_done combT_ready
                    combb_done combb_ready moe_gu moe_sig moe_up moe_hid moe_down moe_out
                    in2_done in2_act in2_dve gl_done gates_ready cmp_h_done cmp_pe_ready cmp_h_ready cmp_kv_done
                    cmp_kv_ready score_done s_ready exp_ready prob_ready turn_done turned pv_done y_ready
                    br_done br_part br_ready wo2_done wo2_ready
                    in3_done in3_act in3_dve if_done conv3_ready qk_silu lru_g_done lru_sig lam_exp lam_ln
                    lru_loga lru_a lru_f lru_sqrt lru_y lru_in gelu_ready
                    gate_in gate_ln c_ready cT_done cT_ready m_floor_in m_floor mb_done mb_ready ml_s_done ml_exp
                    ml_p ml_nd_done fl_done fl_ready mh_ready
                    sb_z_done sb_zs sb_ln sb_lk sb_r_done sb_arg sb_a sb_o_done sb_y
                    out3_done out3_part merged wo3_done x3_ready out_done""".split():
            S[n] = sem(n)

        block = ctx.enter_context(nc.Block())

        jobs = [("nsa", i, g) for i in range(2) for g in range(2)] + \
               [("moba", i, hh) for i in range(2) for hh in range(2)]
        subs = []
        for j, (kind, i, g) in enumerate(jobs):
            for br in (("cmp", "slc", "win") if kind == "nsa" else ("moba",)):
                subs.append((j, kind, i, g, br))
        turns = [1 if br == "cmp" else i + 1 for (_, _, i, _, br) in subs]
        turns_before = [sum(turns[:s]) for s in range(len(subs) + 1)]
        job_last_turn = {}
        for s, (j, *_r) in enumerate(subs):
            job_last_turn[j] = turns_before[s + 1]
        prob_slot = {"cmp": 4, "slc": 0, "win": 2, "moba": 0}

        QA, KC, VC, KS, KW, ZA, QB, KB, ZB, MG = 0, 4, 5, 6, 7, 8, 12, 16, 20, 24
        L_X, M_QK, L_G, M_O, S_Q, S_K, G3 = 0, 2, 6, 8, 10, 12, 14
        taker2 = ["dve"] * 4 + ["act"] * 2 + ["dve"] * 4 + ["act"] * 10 + ["dve"] * 3
        taker3 = ["dve"] * 3 + ["act"] * 2 + ["dve"] * 2 + ["act"] * 12 + ["dve"] * 2

        def taken(taker, stage, p):
            return S[f"{stage}_{taker[p]}"], taker[:p + 1].count(taker[p])

        @block.sync
        def _(sp):
            for s in range(RING):
                sp.dma_start(ring[:, s, :], w_stream[s]).then_inc(chunk_landed[s], 16)
            with sp.Fori(1, NCH // RING) as r:
                for s in range(RING):
                    sp.wait_ge(chunk_begun, r * RING + (s - RING + 2))
                    sp.dma_start(ring[:, s, :], w_stream[r * RING + s]).then_inc(chunk_landed[s], 16)
            sp.wait_ge(S["normed"], 8 * 11)
            sp.dma_start(out, hn256).then_inc(S["out_done"], 16)
            sp.wait_ge(S["out_done"], 16)

        @block.tensor
        def _(pe):
            bank_owner = {}
            at_chunk = [-1]

            def claim(b):
                if b in bank_owner:
                    pe.wait_ge(*bank_owner.pop(b))

            def block_of(b):
                c = b // CH
                first = c != at_chunk[0]
                if first:
                    assert c == at_chunk[0] + 1
                    at_chunk[0] = c
                    pe.wait_ge(chunk_landed[c % RING], 16 * (c // RING + 1))
                return ring[:, c % RING, (b % CH) * WIDE:(b % CH + 1) * WIDE], first

            def begun(first, mm):
                if first:
                    mm.then_inc(chunk_begun, 1)

            def pair(b0, kt, src, t, bank, done, inputs=None):
                claim(bank)
                claim(bank + 1)
                for k in range(kt):
                    if inputs is not None:
                        inputs(k)
                    w, first = block_of(b0 + k)
                    for half in range(2):
                        mm = pe.matmul(ps[:, bank + half, 0:t], w[:, half * P:half * P + P], src(k),
                                       start=(k == 0), stop=(k == kt - 1))
                        if half == 0:
                            begun(first, mm)
                        if k == kt - 1:
                            mm.then_inc(done, 1)

            def token_pair(b0, src, bank, done):
                claim(bank)
                claim(bank + 1)
                for k in range(KD):
                    w, first = block_of(b0 + k)
                    for t in range(2):
                        mm = pe.matmul(ps[:, bank + t, 0:WIDE], src[:, k, t * P:(t + 1) * P], w,
                                       start=(k == 0), stop=(k == KD - 1))
                        if t == 0:
                            begun(first, mm)
                        if k == KD - 1:
                            mm.then_inc(done, 1)

            def sum_squares(i, t):
                for k in range(KD):
                    pe.wait_ge(S["sq_ready"], 8 * i + k + 1)
                    mm = pe.matmul(ps[:, 7, 0:t], ones[:, 0:P], sq[:, k, 0:t], start=(k == 0), stop=(k == KD - 1))
                mm.then_inc(S["sum_done"], 1)

            def after_norm(i):
                return lambda k: pe.wait_ge(S["normed"], 8 * i + k + 1)

            pe.wait_ge(S["consts_ready"], 1)
            pe.wait_ge(S["vec_landed"], 16)
            sum_squares(0, T0)

            def conv_tile(j):
                pe.wait_ge(S["glu_done"], j + 1)
                pe.wait_ge(S["diag_ready"], PE_TAPS * (j + 1))
                claim(6)
                for tap in range(PE_TAPS):
                    mm = pe.matmul(ps[:, 6, 0:T0], diag[:, j % 2, tap, :], conv_u[:, j, tap:tap + T0],
                                   start=(tap == 0), stop=(tap == PE_TAPS - 1))
                mm.then_inc(S["conv_done"], 1)
                bank_owner[6] = (S["conv_ready"], j + 1)

            for j in range(8):
                b = 2 * (j % 3)
                pair(BOFF["pw1"] + j * KD, KD, lambda k: hn[:, k, :], T0, b, S["pw1_done"],
                     after_norm(0) if j == 0 else None)
                bank_owner[b] = (S["glu_done"], j + 1)
                bank_owner[b + 1] = (S["glu_sig"], j + 1)
                if j >= 1:
                    conv_tile(j - 1)
            conv_tile(7)
            for k in range(KD):
                pe.wait_ge(S["conv_ready"], k + 1)
                mm = pe.matmul(ps[:, 7, 0:T0], ones[:, 0:P], conv_y[:, k, :], start=(k == 0), stop=(k == KD - 1))
            mm.then_inc(S["mean_done"], 1)
            sum_squares(1, T0)
            for j in range(4):
                b = 2 * (j % 3)
                pair(BOFF["pw2"] + j * KD, KD, lambda k: sq[:, k, :], T0, b, S["pw2_done"],
                     (lambda k: pe.wait_ge(S["ln_silu"], k + 1)) if j == 0 else None)
                bank_owner[b] = (S["h1_ready"], 2 * j + 1)
                bank_owner[b + 1] = (S["h1_ready"], 2 * j + 2)

            def ffn(n, norm_i, t, hidden, b_in, b_out):
                sum_squares(norm_i, t)
                for p in range(KF):
                    b = 2 * (p % 3)
                    pair(b_in + p * KD, KD, lambda k: hn[:, k, 0:t], t, b, S["ffn_gu"],
                         after_norm(norm_i) if p == 0 else None)
                    bank_owner[b] = (S["ffn_sig"], n * KF + p + 1)
                    bank_owner[b + 1] = (S["ffn_hid"], n * KF + p + 1)
                for j in range(4):
                    b = 2 * (j % 3)
                    pair(b_out + j * KF, KF, lambda k: hidden[:, k, 0:t], t, b, S["ffn_down"],
                         (lambda k: pe.wait_ge(S["ffn_hid"], n * KF + k + 1)) if j == 0 else None)
                    bank_owner[b] = (S["ffn_out"], 8 * n + 2 * j + 1)
                    bank_owner[b + 1] = (S["ffn_out"], 8 * n + 2 * j + 2)

            ffn(0, 2, T0, hid0, BOFF["ffn0_in"], BOFF["ffn0_out"])
            sum_squares(3, T0)
            for g in range(4):
                b = 2 * (g % 3)
                pe.wait_ge(S["pooled"], g + 1)
                pair(BOFF["pool"] + 2 * g, 2, lambda k: sq256[:, 2 * g + k, :], SEQ, b, S["pool_done"])
                bank_owner[b] = (S["x_ready"], 2 * g + 1)
                bank_owner[b + 1] = (S["x_ready"], 2 * g + 2)
            sum_squares(4, SEQ)
            pe.wait_ge(S["normed"], 8 * 5)
            for t in range(2):
                for k in range(KD):
                    mm = pe.matmul(ps[:, 6, t * NE:(t + 1) * NE], hn[:, k, t * P:(t + 1) * P],
                                   vcol("router", k * NE, NE), start=(k == 0), stop=(k == KD - 1))
            mm.then_inc(S["router_done"], 1)
            pe.wait_ge(S["comb_ready"], 1)
            for t in range(2):
                mm = pe.transpose(ps[0:NE, 7, t * P:(t + 1) * P], comb[:, t, :], ident[:, :])
            mm.then_inc(S["combT_done"], 1)
            pe.wait_ge(S["combT_ready"], 1)
            for e in range(NE):
                claim(e // 2)
                mm = pe.matmul(ps[:, e // 2, (e % 2) * SEQ:(e % 2 + 1) * SEQ], sel[0:NE, e, :],
                               up_sb[0:NE, 0, :], start=True, stop=True)
                mm.then_inc(S["combb_done"], 1)
            bank_owner.clear()
            pe.wait_ge(S["combb_ready"], 4)
            pe.wait_ge(S["x_ready"], 8)
            c0 = BOFF["moe"] // CH
            assert at_chunk[0] == c0 - 1
            with pe.Fori(0, NE) as e:
                pe.wait_ge(S["moe_out"], e * 8 + 1)
                blk = [0, -1]

                def moe_block():
                    b, blk[0] = blk[0], blk[0] + 1
                    c = b // CH
                    first = c != blk[1]
                    blk[1] = c
                    s = (c0 + c) % RING
                    if first:
                        pe.wait_ge(chunk_landed[s], e * (16 * (MOE_CH // RING)) + 16 * ((c0 + c) // RING + 1))
                    return ring[:, s, (b % CH) * WIDE:(b % CH + 1) * WIDE], first

                def moe_pair(kt, src, bank, done):
                    for k in range(kt):
                        w, first = moe_block()
                        for half in range(2):
                            mm = pe.matmul(ps[:, bank + half, 0:SEQ], w[:, half * P:half * P + P], src[:, k, 0:SEQ],
                                           start=(k == 0), stop=(k == kt - 1))
                            if half == 0:
                                begun(first, mm)
                            if k == kt - 1:
                                mm.then_inc(done, 1)

                for p in range(KE):
                    if p >= 3:
                        pe.wait_ge(S["moe_sig"], e * KE + (p - 2))
                        pe.wait_ge(S["moe_up"], e * KE + (p - 2))
                    moe_pair(KD, hn, 2 * (p % 3), S["moe_gu"])
                pe.wait_ge(S["moe_hid"], e * KE + KE)
                for j in range(4):
                    if j == 3:
                        pe.wait_ge(S["moe_out"], e * 8 + 3)
                    moe_pair(KE, hid, 2 * (j % 3), S["moe_down"])
            at_chunk[0] = c0 + NE * MOE_CH - 1
            pe.wait_ge(S["moe_out"], 8 * NE + 1)

            sum_squares(5, SEQ)
            sum_squares(6, SEQ)
            for p in range(23):
                b = 2 * (p % 3)
                if p < 20:
                    pair(BOFF["w_in2"] + p * KD, KD, lambda k: hn256[:, k, :], SEQ, b, S["in2_done"],
                         after_norm(6) if p == 0 else None)
                else:
                    token_pair(BOFF["w_in2"] + p * KD, hn256, b, S["in2_done"])
                bank_owner[b] = bank_owner[b + 1] = taken(taker2, "in2", p)
            for t in range(2):
                for k in range(KD):
                    mm = pe.matmul(ps[:, 6, t * 24:(t + 1) * 24], hn256[:, k, t * P:(t + 1) * P],
                                   vcol("w_gates", k * 24, 24), start=(k == 0), stop=(k == KD - 1))
            mm.then_inc(S["gl_done"], 1)
            pe.wait_ge(S["in2_act"], taker2.count("act"))
            pe.wait_ge(S["in2_dve"], taker2.count("dve"))
            bank_owner.clear()
            for kv in range(2):
                src = proj[:, KC + kv, :]
                pe_off = VOFF["pev" if kv else "pek"]
                for l in range(32):
                    w, first = block_of(BOFF["cmp"] + 16 * kv + l // 2)
                    for g in range(2):
                        lo = 64 * g
                        lw = w[lo:lo + 64, (l % 2) * P:(l % 2) * P + P]
                        mm = pe.matmul(ps[:, 2 * kv + g, 0:CMP_N], lw,
                                       src[lo:lo + 64, l:l + 16 * (CMP_N - 1) + 1:16],
                                       start=(l == 0), stop=(l == 31))
                        begun(g == 0 and l % 2 == 0 and first, mm)
                    mm = pe.matmul(ps[:, 4 + kv, 0:1], w[0:64, (l % 2) * P:(l % 2) * P + P],
                                   vec[0:64, pe_off + l:pe_off + l + 1], start=(l == 0), stop=(l == 31))
                mm.then_inc(S["cmp_h_done"], 1)
            for kv in range(2):
                pe.wait_ge(S["cmp_h_ready"], 2 * kv + 2)
                for g in range(2):
                    hidc = cmp_h[:, 2 * kv + g, 0:CMP_N]
                    if kv == 0:
                        mm = pe.matmul(ps[64 * g:64 * g + 64, 6, 64:64 + CMP_N], vcol("w2k", 0, 64), hidc,
                                       start=True, stop=True)
                    else:
                        mm = pe.matmul(ps[0:CMP_N, 7, 64 * g:64 * g + 64], hidc, vcol("w2v", 0, 64),
                                       start=True, stop=True)
            mm.then_inc(S["cmp_kv_done"], 1)
            pe.wait_ge(S["cmp_kv_ready"], 2)
            pe.wait_ge(S["gates_ready"], 1)

            def scores(s):
                j, kind, i, g, br = subs[s]
                if s >= 2:
                    pe.wait_ge(S["s_ready"], s - 1)
                n = CMP_N if br == "cmp" else (i + 1) * P
                for p in range(4):
                    bank = 2 * (s % 2) + p % 2
                    if kind == "nsa":
                        lo = 64 * g
                        q = proj[lo:lo + 64, QA + p, i * P:(i + 1) * P]
                        key = cmp_k[lo:lo + 64, 0:CMP_N] if br == "cmp" else \
                            proj[lo:lo + 64, KS if br == "slc" else KW, 0:n]
                    else:
                        hd = 4 * g + p
                        lo = 64 * (hd % 2)
                        q = proj[lo:lo + 64, QB + hd // 2, i * P:(i + 1) * P]
                        key = proj[lo:lo + 64, KB + hd // 2, 0:n]
                    mm = pe.matmul(ps[:, bank, (p // 2) * 256:(p // 2) * 256 + n], q, key, start=True, stop=True)
                mm.then_inc(S["score_done"], 1)

            def turn(s):
                j, kind, i, g, br = subs[s]
                pe.wait_ge(S["prob_ready"], s + 1)
                for kt in range(turns[s]):
                    u = turns_before[s] + kt
                    if u >= 2:
                        pe.wait_ge(S["turned"], u - 1)
                    for p in range(4):
                        if br == "cmp":
                            mm = pe.transpose(ps[0:CMP_N, 4 + u % 2, p * P:(p + 1) * P],
                                              soft[:, s % 2, p, 0:CMP_N], ident[:, :])
                        else:
                            mm = pe.transpose(ps[:, 4 + u % 2, p * P:(p + 1) * P],
                                              soft[:, s % 2, p, kt * P:(kt + 1) * P], ident[:, :])
                    mm.then_inc(S["turn_done"], 1)

            def values(j):
                kind, i, g = jobs[j]
                pe.wait_ge(S["turned"], job_last_turn[j])
                if j >= 2:
                    pe.wait_ge(S["y_ready"], j - 1)
                for p in range(4):
                    if kind == "nsa":
                        o = ps[64 * g:64 * g + 64, 6 + j % 2, p * P:(p + 1) * P]
                        terms = [(cmp_v[0:CMP_N, 64 * g:64 * g + 64], probT[0:CMP_N, 4, p * P:(p + 1) * P])]
                        for br in (0, 1):
                            terms += [(vtok[:, kt, br * P + 64 * g:br * P + 64 * g + 64],
                                       probT[:, 2 * br + kt, p * P:(p + 1) * P]) for kt in range(i + 1)]
                    else:
                        hd = 4 * g + p
                        lo = 64 * (hd % 2)
                        o = ps[lo:lo + 64, 6 + j % 2, (p // 2) * P:(p // 2 + 1) * P]
                        terms = [(vtok[:, kt, 256 + 64 * hd:256 + 64 * hd + 64],
                                  probT[:, kt, p * P:(p + 1) * P]) for kt in range(i + 1)]
                    for n, (lw, r) in enumerate(terms):
                        mm = pe.matmul(o, lw, r, start=(n == 0), stop=(n == len(terms) - 1))
                mm.then_inc(S["pv_done"], 1)

            scores(0)
            for s in range(len(subs)):
                if s + 1 < len(subs):
                    scores(s + 1)
                turn(s)
                if s + 1 == len(subs) or subs[s + 1][0] != subs[s][0]:
                    values(subs[s][0])
            pe.wait_ge(S["y_ready"], 8)
            for j in range(4):
                if j >= 2:
                    pe.wait_ge(S["br_ready"], 2 * j - 2)
                for br in range(2):
                    for k in range(4):
                        w, first = block_of(BOFF["branch"] + j * KD + 4 * br + k)
                        for half in range(2):
                            mm = pe.matmul(ps[:, 4 * (j % 2) + 2 * br + half, 0:SEQ], w[:, half * P:half * P + P],
                                           sq256[:, 4 * br + k, :], start=(k == 0), stop=(k == 3))
                            begun(half == 0 and first, mm)
                mm.then_inc(S["br_done"], 1)
            pe.wait_ge(S["br_ready"], 8)
            for j in range(4):
                b = 2 * (j % 3)
                pair(BOFF["w_o2"] + j * KD, KD, lambda k: hn256[:, k, :], SEQ, b, S["wo2_done"])
                bank_owner[b] = (S["wo2_ready"], 2 * j + 1)
                bank_owner[b + 1] = (S["wo2_ready"], 2 * j + 2)
            sum_squares(7, SEQ)

            sum_squares(8, SEQ)
            for p in range(21):
                b = 2 * (p % 3)
                if p < 19:
                    pair(BOFF["w_in3"] + p * KD, KD, lambda k: hn256[:, k, :], SEQ, b, S["in3_done"],
                         after_norm(8) if p == 0 else None)
                else:
                    token_pair(BOFF["w_in3"] + p * KD, hn256, b, S["in3_done"])
                bank_owner[b] = bank_owner[b + 1] = taken(taker3, "in3", p)
            for n in range(2):
                for k in range(KD):
                    mm = pe.matmul(ps[0:4, 6, n * SEQ:(n + 1) * SEQ], vcol("w_if", k * 8 + 4 * n, 4),
                                   hn256[:, k, :], start=(k == 0), stop=(k == KD - 1))
            mm.then_inc(S["if_done"], 1)
            bank_owner.clear()
            pe.wait_ge(S["in3_act"], taker3.count("act"))
            pe.wait_ge(S["in3_dve"], taker3.count("dve"))
            for hd in range(4):
                lo = 64 * (hd % 2)
                for kt in range(2):
                    mm = pe.matmul(ps[:, hd, 256 * kt:256 * kt + SEQ - P * kt],
                                   proj[lo:lo + 64, S_K + hd // 2, kt * P:(kt + 1) * P],
                                   proj[lo:lo + 64, S_Q + hd // 2, kt * P:SEQ], start=True, stop=True)
                mm.then_inc(S["sb_z_done"], 1)
            pe.wait_ge(S["conv3_ready"], 1)
            for n, name in enumerate(("lru_wa", "lru_wx")):
                for t in range(2):
                    for lo in (0, 64):
                        mm = pe.matmul(ps[lo:lo + 64, 4 + n, t * SEQ:(t + 1) * SEQ],
                                       vec[lo:lo + 64, VOFF[name] + 64 * t:VOFF[name] + 64 * t + 64],
                                       xa[lo:lo + 64, t, :], start=True, stop=True)
            mm.then_inc(S["lru_g_done"], 1)
            pe.wait_ge(S["c_ready"], 1)
            for t in range(2):
                mm = pe.transpose(ps[:, 7, 4 * t:4 * t + 4], crow[:, t * P:(t + 1) * P], ident[0:4, 0:4])
            mm.then_inc(S["cT_done"], 1)
            for hd in range(4):
                pe.wait_ge(S["sb_lk"], hd + 1)
                pe.matmul(ps[:, hd, 0:SEQ], tri[:, :], sb_lk[:, hd, 0:SEQ], start=True, stop=False)
                pe.matmul(ps[:, hd, P:SEQ], ones[:, 0:P], sb_lk[:, hd, SEQ:3 * P], start=False, stop=True)
                mm = pe.matmul(ps[:, hd, SEQ:3 * P], tri[:, :], sb_lk[:, hd, SEQ:3 * P], start=True, stop=True)
                mm.then_inc(S["sb_r_done"], 1)
            pe.wait_ge(S["lru_sig"], 2)
            for hd in range(4):
                lo = 64 * (hd % 2)
                c0v = 256 + 64 * hd
                pe.wait_ge(S["sb_a"], hd + 1)
                o = ps[lo:lo + 64, 4, (hd // 2) * SEQ:(hd // 2 + 1) * SEQ]
                pe.matmul(o, v3[:, 0, c0v:c0v + 64], sb_w[:, hd, 0:SEQ], start=True, stop=False)
                mm = pe.matmul(o[:, P:SEQ], v3[:, 1, c0v:c0v + 64], sb_w[:, hd, SEQ:3 * P], start=False, stop=True)
            mm.then_inc(S["sb_o_done"], 1)
            pe.wait_ge(S["m_floor"], 1)
            pe.wait_ge(S["cT_ready"], 1)
            for hd in range(4):
                mm = pe.matmul(ps[:, hd // 2, (hd % 2) * SEQ:(hd % 2 + 1) * SEQ], sel[0:4, hd, :], mrow,
                               start=True, stop=True)
            mm.then_inc(S["mb_done"], 1)
            for hd in range(4):
                lo = 64 * (hd % 2)
                mm = pe.matmul(ps[lo:lo + 64, 5, (hd // 2) * SEQ:(hd // 2 + 1) * SEQ], sel[0:4, hd, 0:64],
                               floor, start=True, stop=True)
            mm.then_inc(S["fl_done"], 1)
            pe.wait_ge(S["mb_ready"], 4)
            pe.wait_ge(S["qk_silu"], 1)
            for hd in range(4):
                lo = 64 * (hd % 2)
                for kt in range(2):
                    mm = pe.matmul(ps[:, hd, 256 * kt:256 * kt + SEQ - P * kt],
                                   qk3[lo:lo + 64, 2 + hd // 2, kt * P:(kt + 1) * P],
                                   qk3[lo:lo + 64, hd // 2, kt * P:SEQ], start=True, stop=True)
                mm.then_inc(S["ml_s_done"], 1)
            for hd in range(4):
                lo = 64 * (hd % 2)
                pe.wait_ge(S["ml_p"], hd + 1)
                for bank, lws in ((6, (v3[:, 0, 64 * hd:64 * hd + 64], v3[:, 1, 64 * hd:64 * hd + 64])),
                                  (7, (ones[:, 0:64], ones[:, 0:64]))):
                    o = ps[lo:lo + 64, bank, (hd // 2) * SEQ:(hd // 2 + 1) * SEQ]
                    pe.matmul(o, lws[0], sb_w[:, hd, 0:SEQ], start=True, stop=False)
                    mm = pe.matmul(o[:, P:SEQ], lws[1], sb_w[:, hd, SEQ:3 * P], start=False, stop=True)
            mm.then_inc(S["ml_nd_done"], 1)
            pe.wait_ge(S["lru_in"], 1)
            pe.wait_ge(S["sb_y"], 1)
            pe.wait_ge(S["mh_ready"], 1)
            for j in range(4):
                pe.wait_ge(S["merged"], 2 * j)
                for br in range(3):
                    for k in range(2):
                        w, first = block_of(BOFF["outs3"] + j * 6 + 2 * br + k)
                        for half in range(2):
                            mm = pe.matmul(ps[:, 3 * half + br, 0:SEQ], w[:, half * P:half * P + P],
                                           y3[:, 2 * br + k, :], start=(k == 0), stop=(k == 1))
                            begun(half == 0 and first, mm)
                mm.then_inc(S["out3_done"], 1)
            pe.wait_ge(S["merged"], 8)
            for j in range(4):
                b = 2 * (j % 3)
                pair(BOFF["w_o3"] + j * KD, KD, lambda k: hn256[:, k, :], SEQ, b, S["wo3_done"])
                bank_owner[b] = (S["x3_ready"], 2 * j + 1)
                bank_owner[b + 1] = (S["x3_ready"], 2 * j + 2)
            ffn(1, 9, SEQ, hid, BOFF["ffn3_in"], BOFF["ffn3_out"])
            sum_squares(10, SEQ)
            for c in range(at_chunk[0] + 1, NCH):
                pe.wait_ge(chunk_landed[c % RING], 16 * (c // RING + 1))

        @block.scalar
        def _(act):
            steps = [0]

            def step(ins):
                steps[0] += 1
                ins.then_inc(S["act_step"], 1)
                act.wait_ge(S["act_step"], steps[0])

            def norm(i, src, t, ready):
                for k in range(KD):
                    ready(k)
                    act.activation(sq[:, k, 0:t], src[:, k, 0:t], ACT.Square).then_inc(S["sq_ready"], 1)
                act.wait_ge(S["var_ready"], i + 1)
                act.activation(var[:, 0:t], var[:, 0:t], ACT.Sqrt).then_inc(S["std_ready"], 1)

            act.dma_start(h[:, :, :], h_in).then_inc(S["h_landed"], 16)
            act.dma_start(vec[:, :], vec_in).then_inc(S["vec_landed"], 16)
            act.wait_ge(S["h_landed"], 16)
            norm(0, h, T0, lambda k: None)
            act.wait_ge(S["vec_landed"], 16)
            for j in range(8):
                act.wait_ge(S["pw1_done"], 2 * j + 2)
                if j >= 2:
                    act.wait_ge(S["glu_done"], j - 1)
                act.activation(gate_sb[:, j % 2, :], ps[:, 2 * (j % 3) + 1, 0:T0], ACT.Sigmoid,
                               bias=vcol("b_pw1", 8 + j)).then_inc(S["glu_sig"], 1)
            norm(1, conv_y, T0, lambda k: act.wait_ge(S["xc_ready"], k + 1))
            for k in range(KD):
                act.wait_ge(S["normed"], 8 * 1 + k + 1)
                act.activation(sq[:, k, :], conv_y[:, k, :], ACT.Silu, bias=vcol("ln_b", k)).then_inc(S["ln_silu"], 1)
            norm(2, h, T0, lambda k: act.wait_ge(S["h1_ready"], max(k + 1, 8)))

            def ffn(n, t):
                for p in range(KF):
                    act.wait_ge(S["ffn_gu"], n * 2 * KF + 2 * p + 2)
                    if p >= 2:
                        act.wait_ge(S["ffn_hid"], n * KF + p - 1)
                    act.activation(gate_sb[:, p % 2, 0:t], ps[:, 2 * (p % 3), 0:t], ACT.Silu).then_inc(S["ffn_sig"], 1)

            ffn(0, T0)
            norm(3, h, T0, lambda k: act.wait_ge(S["ffn_out"], k + 1))
            norm(4, x, SEQ, lambda k: act.wait_ge(S["x_ready"], 8))
            act.wait_ge(S["gap_ready"], 1)
            act.activation(gap[:, :, 1:2], gap[:, :, 0:1], ACT.Exp).then_inc(S["gap_exp"], 1)
            act.wait_ge(S["combT_done"], 1)
            act.activation(up_sb[0:NE, 0, :], ps[0:NE, 7, 0:SEQ], ACT.Copy).then_inc(S["combT_ready"], 1)
            for n in range(4):
                act.wait_ge(S["combb_done"], 2 * n + 2)
                act.activation(comb_b[:, 2 * n:2 * n + 2, :],
                               ps[:, n, :].rearrange("p (e t) -> p e t", e=2), ACT.Copy).then_inc(S["combb_ready"], 1)
            with act.Fori(0, NE) as e:
                for p in range(KE):
                    act.wait_ge(S["moe_gu"], e * (2 * KE) + (2 * p + 2))
                    if p >= 2:
                        act.wait_ge(S["moe_hid"], e * KE + (p - 1))
                    act.activation(gate_sb[:, p % 2, 0:SEQ], ps[:, 2 * (p % 3), 0:SEQ], ACT.Silu)\
                       .then_inc(S["moe_sig"], 1)
            norm(5, x, SEQ, lambda k: act.wait_ge(S["moe_out"], 8 * NE - 6 + k))
            norm(6, x, SEQ, lambda k: act.wait_ge(S["normed"], 8 * 5 + k + 1))
            for p in range(20):
                if taker2[p] != "act":
                    continue
                act.wait_ge(S["in2_done"], 2 * p + 2)
                b = 2 * (p % 3)
                act.activation(proj[:, 2 * p:2 * p + 2, :], ps[:, b:b + 2, 0:SEQ],
                               ACT.Silu if 2 * p < MG else ACT.Sigmoid).then_inc(S["in2_act"], 1)
            act.wait_ge(S["gl_done"], 1)
            act.activation(gates, ps[:, 6, 0:48], ACT.Sigmoid).then_inc(S["gates_ready"], 1)
            act.wait_ge(S["cmp_pe_ready"], 1)
            for kv in range(2):
                act.wait_ge(S["cmp_pe_ready"], kv + 1)
                for g in range(2):
                    act.activation(cmp_h[:, 2 * kv + g, 0:CMP_N], ps[:, 2 * kv + g, 0:CMP_N], ACT.Silu,
                                   bias=cmp_pe[:, kv:kv + 1]).then_inc(S["cmp_h_ready"], 1)

            def exps(s):
                j, kind, i, g, br = subs[s]
                act.wait_ge(S["s_ready"], s + 1)
                n = CMP_N if br == "cmp" else (i + 1) * P
                for p in range(4):
                    ins = act.activation(soft[:, s % 2, p, 0:n], soft[:, s % 2, p, 0:n], ACT.Exp,
                                         bias=stats[:, s % 2, 1, p:p + 1], accum_out=stats[:, s % 2, 2, p:p + 1])
                ins.then_inc(S["exp_ready"], 1)

            def copies(s):
                j, kind, i, g, br = subs[s]
                for kt in range(turns[s]):
                    u = turns_before[s] + kt
                    act.wait_ge(S["turn_done"], u + 1)
                    if j >= 1:
                        act.wait_ge(S["pv_done"], j)
                    rows_n = CMP_N if br == "cmp" else P
                    act.activation(probT[0:rows_n, prob_slot[br] + kt, :], ps[0:rows_n, 4 + u % 2, :], ACT.Copy)\
                       .then_inc(S["turned"], 1)

            exps(0)
            for s in range(len(subs)):
                if s + 1 < len(subs):
                    exps(s + 1)
                copies(s)
            norm(7, zo, SEQ, lambda k: act.wait_ge(S["wo2_ready"], k + 1))
            norm(8, x, SEQ, lambda k: act.wait_ge(S["normed"], 8 * 7 + k + 1))
            for p in range(19):
                if taker3[p] != "act":
                    continue
                act.wait_ge(S["in3_done"], 2 * p + 2)
                b = 2 * (p % 3)
                act.activation(proj[:, 2 * p:2 * p + 2, :], ps[:, b:b + 2, 0:SEQ],
                               ACT.Gelu_apprx_tanh if 2 * p == L_G else ACT.Sigmoid).then_inc(S["in3_act"], 1)
            act.wait_ge(S["conv3_ready"], 2)
            act.activation(qk3, qk3, ACT.Silu).then_inc(S["qk_silu"], 1)
            act.wait_ge(S["lru_g_done"], 1)
            for n, name in enumerate(("lru_ba", "lru_bx")):
                for t in range(2):
                    ins = act.activation(lru_t[:, n, t, :], ps[:, 4 + n, t * SEQ:(t + 1) * SEQ], ACT.Sigmoid,
                                         bias=vcol(name, t))
                ins.then_inc(S["lru_sig"], 1)
            step(act.activation(lam[:, 0, :], vcol("lru_lam", 0, 2), ACT.Abs))
            act.activation(lam[:, 1, :], lam[:, 0, :], ACT.Exp, scale=-1.0).then_inc(S["lam_exp"], 1)
            act.wait_ge(S["lru_loga"], 1)
            act.activation(lru_t[:, 3, :, :], lru_t[:, 2, :, :], ACT.Exp).then_inc(S["lru_a"], 1)
            act.wait_ge(S["lru_a"], 1)
            act.activation(lru_t[:, 2, :, :], lru_t[:, 2, :, :], ACT.Tanh).then_inc(S["lru_a"], 1)
            act.wait_ge(S["lru_f"], 1)
            act.activation(lru_t[:, 2, :, :], lru_t[:, 2, :, :], ACT.Sqrt, scale=-1.0).then_inc(S["lru_sqrt"], 1)
            act.wait_ge(S["gate_in"], 1)
            step(act.activation(arow, frow, ACT.Abs))
            step(act.activation(arow, arow, ACT.Exp, scale=-1.0))
            act.activation(arow, arow, ACT.Ln, bias=1.0).then_inc(S["gate_ln"], 1)
            for hd in range(4):
                act.wait_ge(S["sb_zs"], hd + 1)
                step(act.activation(sb_lk[:, hd, :], zs[:, hd, :], ACT.Abs))
                step(act.activation(sb_lk[:, hd, :], sb_lk[:, hd, :], ACT.Exp, scale=-1.0))
                act.activation(sb_lk[:, hd, :], sb_lk[:, hd, :], ACT.Ln, bias=1.0).then_inc(S["sb_ln"], 1)
            for hd in range(4):
                act.wait_ge(S["sb_arg"], hd + 1)
                act.activation(sb_w[:, hd, :], sb_w[:, hd, :], ACT.Exp).then_inc(S["sb_a"], 1)
            act.wait_ge(S["m_floor_in"], 1)
            act.activation(floor, floor, ACT.Exp).then_inc(S["m_floor"], 1)
            act.wait_ge(S["cT_ready"], 1)
            for hd in range(4):
                act.wait_ge(S["mb_ready"], hd + 1)
                act.activation(decay[:, hd, 0:SEQ], decay[:, hd, 0:SEQ], ACT.Exp, bias=ccol[:, hd:hd + 1])
                act.activation(decay[:, hd, SEQ:3 * P], decay[:, hd, SEQ:3 * P], ACT.Exp,
                               bias=ccol[:, 4 + hd:5 + hd]).then_inc(S["ml_exp"], 1)
            act.wait_ge(S["ml_nd_done"], 1)
            act.activation(lru_t[:, 0, :, :], ps[:, 7, :].rearrange("p (k t) -> p k t", k=2), ACT.Abs)\
               .then_inc(S["fl_ready"], 1)
            norm(9, x, SEQ, lambda k: act.wait_ge(S["x3_ready"], k + 1))
            ffn(1, SEQ)
            norm(10, x, SEQ, lambda k: act.wait_ge(S["ffn_out"], 8 + k + 1))

        @block.vector
        def _(dve):
            steps = [0]

            def step(ins):
                steps[0] += 1
                ins.then_inc(S["dve_step"], 1)
                dve.wait_ge(S["dve_step"], steps[0])

            def inverse_root(i, t, eps):
                dve.wait_ge(S["sum_done"], i + 1)
                dve.tensor_scalar(var[:, 0:t], ps[:, 7, 0:t], 1.0 / D, eps, ALU.mult, ALU.add)\
                   .then_inc(S["var_ready"], 1)
                dve.wait_ge(S["std_ready"], i + 1)
                step(dve.reciprocal(rstd[:, 0:t], var[:, 0:t]))

            def norm(i, src, dst, gain, t, eps=EPS):
                inverse_root(i, t, eps)
                for k in range(KD):
                    dve.scalar_tensor_tensor(out=dst[:, k, 0:t], in0=src[:, k, 0:t], scalar=vcol(gain, k),
                                             in1=rstd[:, 0:t], op0=ALU.mult, op1=ALU.mult).then_inc(S["normed"], 1)

            dve.wait_ge(S["consts_ready"], 1)
            dve.wait_ge(S["vec_landed"], 16)
            dve.wait_ge(S["h_landed"], 16)
            step(dve.memset(conv_u[:, :, 0:CONVW - 1], 0.0))
            norm(0, h, hn, "mix_g0", T0)

            def conv_dve(j):
                dve.wait_ge(S["glu_done"], j + 1)
                for tap in range(PE_TAPS, CONVW):
                    u = conv_u[:, j, tap:tap + T0]
                    w = vcol("w_dw", j * CONVW + tap)
                    if tap == PE_TAPS:
                        step(dve.tensor_scalar(conv_y[:, j, :], u, w, None, ALU.mult))
                    else:
                        step(dve.scalar_tensor_tensor(out=conv_y[:, j, :], in0=u, scalar=w, in1=conv_y[:, j, :],
                                                      op0=ALU.mult, op1=ALU.add))
                dve.wait_ge(S["conv_done"], j + 1)
                dve.scalar_tensor_tensor(out=conv_y[:, j, :], in0=ps[:, 6, 0:T0], scalar=vcol("b_dw", j),
                                         in1=conv_y[:, j, :], op0=ALU.add, op1=ALU.add).then_inc(S["conv_ready"], 1)

            for j in range(8):
                dve.wait_ge(S["glu_sig"], j + 1)
                dve.scalar_tensor_tensor(out=conv_u[:, j, CONVW - 1:CONVW - 1 + T0], in0=ps[:, 2 * (j % 3), 0:T0],
                                         scalar=vcol("b_pw1", j), in1=gate_sb[:, j % 2, :],
                                         op0=ALU.add, op1=ALU.mult).then_inc(S["glu_done"], 1)
                if j >= 1:
                    conv_dve(j - 1)
            conv_dve(7)
            dve.wait_ge(S["mean_done"], 1)
            step(dve.tensor_scalar(mean, ps[:, 7, 0:T0], 1.0 / D, None, ALU.mult))
            for k in range(KD):
                dve.tensor_tensor(conv_y[:, k, :], conv_y[:, k, :], mean, ALU.subtract).then_inc(S["xc_ready"], 1)
            norm(1, conv_y, conv_y, "ln_g", T0, LN_EPS)
            for m in range(KD):
                dve.wait_ge(S["pw2_done"], m + 1)
                b = 2 * (m // 2 % 3) + m % 2
                dve.scalar_tensor_tensor(out=h[:, m, :], in0=ps[:, b, 0:T0], scalar=vcol("b_pw2", m),
                                         in1=h[:, m, :], op0=ALU.add, op1=ALU.add).then_inc(S["h1_ready"], 1)

            def ffn(n, norm_i, res, gain, t, hidden):
                norm(norm_i, res, hn, gain, t)
                for p in range(KF):
                    dve.wait_ge(S["ffn_sig"], n * KF + p + 1)
                    dve.tensor_tensor(hidden[:, p, 0:t], ps[:, 2 * (p % 3) + 1, 0:t], gate_sb[:, p % 2, 0:t],
                                      ALU.mult).then_inc(S["ffn_hid"], 1)
                for m in range(KD):
                    dve.wait_ge(S["ffn_down"], 8 * n + m + 1)
                    b = 2 * (m // 2 % 3) + m % 2
                    dve.tensor_tensor(res[:, m, 0:t], ps[:, b, 0:t], res[:, m, 0:t], ALU.add)\
                       .then_inc(S["ffn_out"], 1)

            ffn(0, 2, h, "ffn_g0", T0, hid0)
            norm(3, h, hn, "mix_g1", T0)
            dve.wait_ge(S["normed"], 8 * 4)
            for g in range(4):
                src, width, at = hn[:, 2 * g:2 * g + 2, :], 1, 0
                if g:
                    dve.wait_ge(S["pooled"], g)
                for dst in (pool_a, pool_b, pool_a, pool_b)[:g + 1]:
                    at += width
                    step(dve.tensor_tensor(dst[:, :, at:T0], src[:, :, at:T0], src[:, :, at - width:T0 - width],
                                           ALU.add))
                    src, width = dst, 2 * width
                dve.scalar_tensor_tensor(out=sq256[:, 2 * g:2 * g + 2, :], in0=src[:, :, META:T0],
                                         scalar=1.0 / width, in1=hn[:, 2 * g:2 * g + 2, META:T0],
                                         op0=ALU.mult, op1=ALU.subtract).then_inc(S["pooled"], 1)
            for m in range(KD):
                dve.wait_ge(S["pool_done"], m + 1)
                b = 2 * (m // 2 % 3) + m % 2
                dve.scalar_tensor_tensor(out=x[:, m, :], in0=ps[:, b, 0:SEQ], scalar=vcol("pool_scale", m),
                                         in1=h[:, m, META:T0], op0=ALU.mult, op1=ALU.add).then_inc(S["x_ready"], 1)
            norm(4, x, hn, "ffn_g1", SEQ)
            dve.wait_ge(S["router_done"], 1)
            step(dve.tensor_copy(logit, ps[:, 6, 0:2 * NE].rearrange("p (t e) -> p t e", t=2)))
            for t in range(2):
                step(dve.max(top[:, t, :], logit[:, t, :]))
                step(dve.max_index(idx_u[:, t, :], top[:, t, :], logit[:, t, :]))
            step(dve.tensor_copy(top_i, idx_u[:, :, :]))
            dve.tensor_tensor(gap[:, :, 0:1], top[:, :, 1:2], top[:, :, 0:1], ALU.subtract)\
               .then_inc(S["gap_ready"], 1)
            dve.wait_ge(S["gap_exp"], 1)
            step(dve.tensor_scalar(gap[:, :, 2:3], gap[:, :, 1:2], 1.0, None, ALU.add))
            step(dve.reciprocal(gap[:, :, 3:4], gap[:, :, 2:3]))
            step(dve.tensor_tensor(gap[:, :, 4:5], gap[:, :, 3:4], gap[:, :, 1:2], ALU.mult))
            for t in range(2):
                dve.tensor_scalar(comb1[:, t, :], iota8[:, :], top_i[:, t, 1:2], gap[:, t, 4:5],
                                  ALU.is_equal, ALU.mult)
                step(dve.tensor_scalar(comb[:, t, :], iota8[:, :], top_i[:, t, 0:1], gap[:, t, 3:4],
                                       ALU.is_equal, ALU.mult))
            dve.tensor_tensor(comb, comb, comb1, ALU.add).then_inc(S["comb_ready"], 1)
            dve.wait_ge(S["combb_ready"], 4)
            dve.memset(gap[:, :, 5:6], 0.0).then_inc(S["moe_out"], 1)
            with dve.Fori(0, NE) as e:
                for p in range(KE):
                    dve.wait_ge(S["moe_gu"], e * (2 * KE) + (2 * p + 2))
                    if p >= 2:
                        dve.wait_ge(S["moe_hid"], e * KE + (p - 1))
                    dve.tensor_tensor(up_sb[:, p % 2, :], ps[:, 2 * (p % 3) + 1, 0:SEQ], comb_b[:, e, :],
                                      ALU.mult).then_inc(S["moe_up"], 1)
                for m in range(KD):
                    dve.wait_ge(S["moe_down"], e * 8 + (m + 1))
                    b = 2 * (m // 2 % 3) + m % 2
                    dve.tensor_tensor(x[:, m, :], ps[:, b, 0:SEQ], x[:, m, :], ALU.add).then_inc(S["moe_out"], 1)
            norm(5, x, x, "final_g", SEQ)
            norm(6, x, hn, "pre_g", SEQ)
            for p in range(23):
                if taker2[p] != "dve":
                    continue
                dve.wait_ge(S["in2_done"], 2 * p + 2)
                b = 2 * (p % 3)
                if p >= 20:
                    c = p - 20
                    ins = dve.tensor_copy(vtok[:, :, c * WIDE:(c + 1) * WIDE], ps[:, b:b + 2, 0:SEQ])
                elif QA <= 2 * p < KC or QB <= 2 * p < KB:
                    ins = dve.tensor_scalar(proj[:, 2 * p:2 * p + 2, :], ps[:, b:b + 2, 0:SEQ], 0.125, None, ALU.mult)
                else:
                    ins = dve.tensor_copy(proj[:, 2 * p:2 * p + 2, :], ps[:, b:b + 2, 0:SEQ])
                ins.then_inc(S["in2_dve"], 1)
            for kv in range(2):
                dve.wait_ge(S["cmp_h_done"], kv + 1)
                dve.tensor_copy(cmp_pe[:, kv:kv + 1], ps[:, 4 + kv, 0:1]).then_inc(S["cmp_pe_ready"], 1)
            dve.wait_ge(S["cmp_kv_done"], 1)
            dve.tensor_copy(cmp_k[:, 0:CMP_N], ps[:, 6, 64:64 + CMP_N]).then_inc(S["cmp_kv_ready"], 1)
            dve.tensor_copy(cmp_v[0:CMP_N, :], ps[0:CMP_N, 7, 0:P]).then_inc(S["cmp_kv_ready"], 1)
            dve.wait_ge(S["gates_ready"], 1)

            def biased(s):
                j, kind, i, g, br = subs[s]
                dve.wait_ge(S["score_done"], s + 1)
                if s >= 2:
                    dve.wait_ge(S["turn_done"], turns_before[s - 1])
                n = CMP_N if br == "cmp" else (i + 1) * P
                for p in range(4):
                    slope = moba_slope(4 * g + p) if kind == "moba" else nsa_slope(g, p)
                    bias = cbias[:, i, 0:CMP_N] if br == "cmp" else alibi[:, 2 * P - n:2 * P]
                    ins = dve.scalar_tensor_tensor(out=soft[:, s % 2, p, 0:n], in0=bias, scalar=slope,
                                                   in1=ps[:, 2 * (s % 2) + p % 2, (p // 2) * 256:(p // 2) * 256 + n],
                                                   op0=ALU.mult, op1=ALU.add)
                step(ins)
                step(dve.tensor_reduce(stats[:, s % 2, 0, :], soft[:, s % 2, :, 0:n], AX.X, ALU.max))
                dve.tensor_scalar(stats[:, s % 2, 1, :], stats[:, s % 2, 0, :], -1.0, 1.0e20, ALU.mult, ALU.min)\
                   .then_inc(S["s_ready"], 1)

            def scaled(s):
                j, kind, i, g, br = subs[s]
                dve.wait_ge(S["exp_ready"], s + 1)
                n = CMP_N if br == "cmp" else (i + 1) * P
                step(dve.tensor_scalar(stats[:, s % 2, 3, :], stats[:, s % 2, 2, :], 1.0e-30, None, ALU.max))
                step(dve.reciprocal(stats[:, s % 2, 3, :], stats[:, s % 2, 3, :]))
                if kind == "nsa":
                    col = i * 24 + ("cmp", "slc", "win").index(br) * 8 + g * 4
                    step(dve.tensor_tensor(stats[:, s % 2, 3, :], stats[:, s % 2, 3, :], gates[:, col:col + 4],
                                           ALU.mult))
                for p in range(4):
                    ins = dve.tensor_scalar(soft[:, s % 2, p, 0:n], soft[:, s % 2, p, 0:n],
                                            stats[:, s % 2, 3, p:p + 1], None, ALU.mult)
                ins.then_inc(S["prob_ready"], 1)

            def gated(j):
                kind, i, g = jobs[j]
                dve.wait_ge(S["pv_done"], j + 1)
                q = slice(i * P, (i + 1) * P)
                if kind == "nsa":
                    lo = 64 * g
                    ins = dve.tensor_tensor(sq256[lo:lo + 64, 0:4, q],
                                            ps[lo:lo + 64, 6 + j % 2, :].rearrange("p (a t) -> p a t", a=4),
                                            proj[lo:lo + 64, ZA:ZA + 4, q], ALU.mult)
                else:
                    ins = dve.tensor_tensor(sq256[:, 4 + 2 * g:6 + 2 * g, q],
                                            ps[:, 6 + j % 2, 0:2 * P].rearrange("p (a t) -> p a t", a=2),
                                            proj[:, ZB + 2 * g:ZB + 2 * g + 2, q], ALU.mult)
                ins.then_inc(S["y_ready"], 1)

            biased(0)
            for s in range(len(subs)):
                if s + 1 < len(subs):
                    biased(s + 1)
                scaled(s)
                if s >= 1 and subs[s][0] != subs[s - 1][0]:
                    gated(subs[s - 1][0])
            gated(len(jobs) - 1)
            for m in range(KD):
                j, half = m // 2, m % 2
                dve.wait_ge(S["br_done"], j + 1)
                if m >= 2:
                    dve.wait_ge(S["br_ready"], m - 1)
                for br in range(2):
                    ins = dve.tensor_tensor(part[:, m % 2, br, :], ps[:, 4 * (j % 2) + 2 * br + half, 0:SEQ],
                                            proj[:, MG + 8 * br + m, :], ALU.mult)
                ins.then_inc(S["br_part"], 1)
            for m in range(KD):
                dve.wait_ge(S["wo2_done"], m + 1)
                b = 2 * (m // 2 % 3) + m % 2
                dve.tensor_copy(zo[:, m, :], ps[:, b, 0:SEQ]).then_inc(S["wo2_ready"], 1)
            inverse_root(7, SEQ, EPS)
            for k in range(KD):
                ins = dve.scalar_tensor_tensor(out=zo[:, k, :], in0=zo[:, k, :], scalar=vcol("post_g", k),
                                               in1=rstd[:, 0:SEQ], op0=ALU.mult, op1=ALU.mult)
            step(ins)
            for k in range(KD):
                dve.tensor_tensor(x[:, k, :], x[:, k, :], zo[:, k, :], ALU.add).then_inc(S["normed"], 1)

            dve.memset(cpad, 0.0)
            norm(8, x, hn, "mix3_g", SEQ)

            def take3(p):
                dve.wait_ge(S["in3_done"], 2 * p + 2)
                b = 2 * (p % 3)
                if p >= 19:
                    ins = dve.tensor_copy(v3[:, :, (p - 19) * WIDE:(p - 18) * WIDE], ps[:, b:b + 2, 0:SEQ])
                elif 2 * p < L_G:
                    ins = dve.tensor_copy(cin[:, 2 * p:2 * p + 2, 3:3 + SEQ], ps[:, b:b + 2, 0:SEQ])
                elif 2 * p == S_Q:
                    ins = dve.tensor_scalar(proj[:, 2 * p:2 * p + 2, :], ps[:, b:b + 2, 0:SEQ], 0.125, None, ALU.mult)
                else:
                    ins = dve.tensor_copy(proj[:, 2 * p:2 * p + 2, :], ps[:, b:b + 2, 0:SEQ])
                ins.then_inc(S["in3_dve"], 1)

            def conv3(tiles, dst, done):
                for tap in range(4):
                    for n, j in enumerate(tiles):
                        u = cin[:, j, tap:tap + SEQ]
                        w = vcol("conv3", 4 * j + tap)
                        if tap == 0:
                            ins = dve.tensor_scalar(dst[:, n, :], u, w, None, ALU.mult)
                        else:
                            ins = dve.scalar_tensor_tensor(out=dst[:, n, :], in0=u, scalar=w, in1=dst[:, n, :],
                                                           op0=ALU.mult, op1=ALU.add)
                    if tap < 3:
                        step(ins)
                ins.then_inc(done, 1)

            for p in (0, 1, 2, 5, 6):
                take3(p)
            dve.wait_ge(S["in3_dve"], 3)
            conv3((0, 1), xa, S["conv3_ready"])
            conv3((2, 3, 4, 5), qk3, S["conv3_ready"])
            for p in (19, 20):
                take3(p)
            dve.wait_ge(S["lam_exp"], 1)
            e_, r_, r2, q_ = lam[:, 1, :], lam[:, 2, :], lam[:, 3, :], lam[:, 4, :]
            step(dve.tensor_scalar(r_, e_, 2.0, None, ALU.add))
            step(dve.reciprocal(r_, r_))
            step(dve.tensor_tensor(r_, r_, e_, ALU.mult))
            step(dve.tensor_tensor(r2, r_, r_, ALU.mult))
            step(dve.tensor_scalar(q_, r2, 1.0 / 17, None, ALU.mult))
            for odd in (15, 13, 11, 9, 7, 5, 3):
                step(dve.scalar_tensor_tensor(out=q_, in0=q_, scalar=1.0 / odd, in1=r2, op0=ALU.add, op1=ALU.mult))
            step(dve.scalar_tensor_tensor(out=q_, in0=q_, scalar=1.0, in1=r_, op0=ALU.add, op1=ALU.mult))
            step(dve.tensor_scalar(r_, vcol("lru_lam", 0, 2), -1.0, 0.0, ALU.mult, ALU.max))
            step(dve.scalar_tensor_tensor(out=q_, in0=q_, scalar=2.0, in1=r_, op0=ALU.mult, op1=ALU.add))
            step(dve.tensor_scalar(q_, q_, -8.0, None, ALU.mult))
            dve.wait_ge(S["lru_sig"], 2)
            for t in range(2):
                ins = dve.tensor_scalar(lru_t[:, 2, t, :], lru_t[:, 0, t, :], q_[:, t:t + 1], None, ALU.mult)
            ins.then_inc(S["lru_loga"], 1)
            dve.wait_ge(S["lru_a"], 2)
            step(dve.tensor_tensor(lru_t[:, 0, :, :], lru_t[:, 3, :, :], lru_t[:, 3, :, :], ALU.mult))
            dve.scalar_tensor_tensor(out=lru_t[:, 2, :, :], in0=lru_t[:, 0, :, :], scalar=1.0,
                                     in1=lru_t[:, 2, :, :], op0=ALU.add, op1=ALU.mult).then_inc(S["lru_f"], 1)
            dve.wait_ge(S["if_done"], 1)
            dve.wait_ge(S["in3_act"], taker3.count("act"))
            dve.tensor_scalar(irow, ps[0:4, 6, 0:SEQ], vcol("ig_b", rows=4), None, ALU.add)
            dve.tensor_scalar(frow, ps[0:4, 6, SEQ:2 * SEQ], vcol("fg_b", rows=4), None, ALU.add)\
               .then_inc(S["gate_in"], 1)
            step(dve.tensor_tensor(lru_t[:, 1, :, :], lru_t[:, 1, :, :], xa, ALU.mult))
            dve.wait_ge(S["lru_sqrt"], 1)
            step(dve.tensor_tensor(lru_t[:, 1, :, :], lru_t[:, 1, :, :], lru_t[:, 2, :, :], ALU.mult))
            for t in range(2):
                ins = dve.tensor_tensor_scan(lru_t[:, 0, t, :], lru_t[:, 3, t, :], lru_t[:, 1, t, :], 0.0,
                                             ALU.mult, ALU.add)
            step(ins)
            dve.tensor_tensor(y3[:, 0:2, :], lru_t[:, 0, :, :], proj[:, L_G:L_G + 2, :], ALU.mult)\
               .then_inc(S["lru_in"], 1)
            for hd in range(4):
                dve.wait_ge(S["sb_z_done"], hd + 1)
                dve.tensor_tensor(zs[:, hd, :], ps[:, hd, 0:3 * P], smask[:, :], ALU.add).then_inc(S["sb_zs"], 1)
            dve.wait_ge(S["gate_ln"], 1)
            step(dve.scalar_tensor_tensor(out=frow, in0=frow, scalar=0.0, in1=arow, op0=ALU.min, op1=ALU.subtract))
            step(dve.tensor_tensor_scan(brow, ones[0:4, :], frow, 0.0, ALU.mult, ALU.add))
            dve.tensor_tensor(crow, irow, brow, ALU.subtract).then_inc(S["c_ready"], 1)
            dve.wait_ge(S["c_ready"], 1)
            step(dve.tensor_tensor_scan(mrow, crow, crow, 0.0, ALU.max, ALU.max))
            step(dve.tensor_scalar(mrow, mrow, -1.0, None, ALU.mult))
            dve.tensor_tensor(floor, mrow, brow, ALU.subtract).then_inc(S["m_floor_in"], 1)
            dve.wait_ge(S["cT_done"], 1)
            dve.tensor_copy(ccol, ps[:, 7, 0:8]).then_inc(S["cT_ready"], 1)
            for hd in range(4):
                dve.wait_ge(S["sb_ln"], hd + 1)
                dve.scalar_tensor_tensor(out=sb_lk[:, hd, :], in0=zs[:, hd, :], scalar=0.0, in1=sb_lk[:, hd, :],
                                         op0=ALU.max, op1=ALU.add).then_inc(S["sb_lk"], 1)
            for hd in range(4):
                dve.wait_ge(S["sb_r_done"], hd + 1)
                dve.tensor_tensor(sb_w[:, hd, :], zs[:, hd, :], ps[:, hd, 0:3 * P], ALU.subtract)\
                   .then_inc(S["sb_arg"], 1)
            dve.wait_ge(S["mb_done"], 1)
            dve.wait_ge(S["sb_arg"], 4)
            for hd in range(4):
                nm = ps[:, hd // 2, (hd % 2) * SEQ:(hd % 2 + 1) * SEQ]
                dve.tensor_tensor(decay[:, hd, 0:SEQ], nm, tmask[:, 0:SEQ], ALU.add)
                dve.tensor_tensor(decay[:, hd, SEQ:3 * P], nm[:, P:SEQ], tmask[:, SEQ:3 * P], ALU.add)\
                   .then_inc(S["mb_ready"], 1)
            dve.wait_ge(S["sb_o_done"], 1)
            dve.tensor_copy(y3[:, 4:6, :], ps[:, 4, :].rearrange("p (k t) -> p k t", k=2)).then_inc(S["sb_y"], 1)
            for hd in range(4):
                dve.wait_ge(S["ml_exp"], hd + 1)
                dve.wait_ge(S["ml_s_done"], hd + 1)
                dve.scalar_tensor_tensor(out=sb_w[:, hd, :], in0=decay[:, hd, :], scalar=0.125,
                                         in1=ps[:, hd, 0:3 * P], op0=ALU.mult, op1=ALU.mult).then_inc(S["ml_p"], 1)
            dve.wait_ge(S["fl_ready"], 1)
            dve.wait_ge(S["fl_done"], 1)
            den = lru_t[:, 0, :, :]
            step(dve.tensor_tensor(den, ps[:, 5, :].rearrange("p (k t) -> p k t", k=2), den, ALU.max))
            step(dve.reciprocal(den, den))
            step(dve.tensor_tensor(den, ps[:, 6, :].rearrange("p (k t) -> p k t", k=2), den, ALU.mult))
            dve.tensor_tensor(y3[:, 2:4, :], den, proj[:, M_O:M_O + 2, :], ALU.mult).then_inc(S["mh_ready"], 1)
            dve.wait_ge(S["mh_ready"], 1)
            for m in range(KD):
                j, half = m // 2, m % 2
                dve.wait_ge(S["out3_done"], j + 1)
                if m >= 2:
                    dve.wait_ge(S["merged"], m - 1)
                for br in range(3):
                    ins = dve.tensor_tensor(part3[:, m % 2, br, :], ps[:, 3 * half + br, 0:SEQ],
                                            proj[:, G3 + 8 * br + m, :], ALU.mult)
                ins.then_inc(S["out3_part"], 1)
            for m in range(KD):
                dve.wait_ge(S["wo3_done"], m + 1)
                b = 2 * (m // 2 % 3) + m % 2
                dve.tensor_tensor(x[:, m, :], ps[:, b, 0:SEQ], x[:, m, :], ALU.add).then_inc(S["x3_ready"], 1)
            ffn(1, 9, x, "ffn3_g", SEQ, hid)
            norm(10, x, hn, "final3_g", SEQ)

        @block.gpsimd
        def _(pool):
            steps = [0]

            def step(ins):
                steps[0] += 1
                ins.then_inc(S["pool_step"], 1)
                pool.wait_ge(S["pool_step"], steps[0])

            step(pool.memset(ones[:, :], 1.0))
            step(pool.memset(ident[:, :], 0.0))
            step(pool.affine_select(out=ident[:, :], in_=ident[:, :], compare_op=ALU.not_equal, fill=1.0,
                                    base=0, pattern=[[-1, P]], channel_multiplier=1))
            step(pool.affine_select(out=tri[:, :], in_=ones[:, 0:P], compare_op=ALU.is_ge, fill=0.0,
                                    base=0, pattern=[[-1, P]], channel_multiplier=1))
            step(pool.memset(sel[:, :, :], 0.0))
            step(pool.affine_select(out=sel[:, :, :], in_=sel[:, :, :], compare_op=ALU.not_equal, fill=1.0,
                                    base=0, pattern=[[-1, 8], [0, P]], channel_multiplier=1))
            step(pool.iota(alibi[:, :], pattern=[[1, 2 * P]], base=-P, channel_multiplier=-1,
                           allow_small_or_imprecise_dtypes=True))
            step(pool.affine_select(out=alibi[:, :], in_=alibi[:, :], compare_op=ALU.is_ge, fill=NEG,
                                    base=P, pattern=[[-1, 2 * P]], channel_multiplier=1))
            for i in range(2):
                step(pool.iota(cbias[:, i, :], pattern=[[16, 16]], base=31 - i * P, channel_multiplier=-1,
                               allow_small_or_imprecise_dtypes=True))
                step(pool.affine_select(out=cbias[:, i, :], in_=cbias[:, i, :], compare_op=ALU.is_ge, fill=NEG,
                                        base=i * P - 31, pattern=[[-16, 16]], channel_multiplier=1))
            step(pool.memset(tmask[:, :], 0.0))
            step(pool.memset(smask[:, :], 0.0))
            for m, base in ((tmask, 0), (smask, -1)):
                for lo, hi in ((0, 2 * P), (2 * P, 3 * P)):
                    step(pool.affine_select(out=m[:, lo:hi], in_=m[:, lo:hi], compare_op=ALU.is_ge, fill=NEG,
                                            base=base, pattern=[[1, hi - lo]], channel_multiplier=-1))
            pool.iota(iota8[:, :], pattern=[[1, 8]], base=0, channel_multiplier=0,
                      allow_small_or_imprecise_dtypes=True).then_inc(S["consts_ready"], 1)
            pool.wait_ge(S["vec_landed"], 16)
            for j in range(8):
                if j >= 2:
                    pool.wait_ge(S["conv_done"], j - 1)
                for tap in range(PE_TAPS):
                    pool.tensor_scalar(diag[:, j % 2, tap, :], ident[:, :], vcol("w_dw", j * CONVW + tap), None,
                                       ALU.mult).then_inc(S["diag_ready"], 1)
            with pool.Fori(0, NE) as e:
                for p in range(KE):
                    pool.wait_ge(S["moe_up"], e * KE + (p + 1))
                    pool.wait_ge(S["moe_sig"], e * KE + (p + 1))
                    pool.tensor_tensor(hid[:, p, :], gate_sb[:, p % 2, 0:SEQ], up_sb[:, p % 2, :], ALU.mult)\
                        .then_inc(S["moe_hid"], 1)
            for m in range(KD):
                pool.wait_ge(S["br_part"], m + 1)
                pool.tensor_tensor(hn256[:, m, :], part[:, m % 2, 0, :], part[:, m % 2, 1, :], ALU.add)\
                    .then_inc(S["br_ready"], 1)
            for m in range(KD):
                pool.wait_ge(S["out3_part"], m + 1)
                step(pool.tensor_tensor(part3[:, m % 2, 0, :], part3[:, m % 2, 0, :], part3[:, m % 2, 1, :], ALU.add))
                pool.tensor_tensor(hn256[:, m, :], part3[:, m % 2, 0, :], part3[:, m % 2, 2, :], ALU.add)\
                    .then_inc(S["merged"], 1)


def _kernel_arrays(i):
    def blocks(w):
        k, n = w.shape
        return w.reshape(k // P, P, n // WIDE, WIDE).transpose(2, 0, 1, 3).reshape(-1, P, WIDE)

    def beside(a, b):
        k, n = a.shape
        return np.stack([a.reshape(k, n // P, P), b.reshape(k, n // P, P)], 2).reshape(k, 2 * n)

    def by_group(w, axis):
        s = w.shape
        if axis == 1:
            return w.reshape(s[0], 2, 4, 64).transpose(0, 2, 1, 3).reshape(s)
        return w.reshape(2, 4, 64, s[1]).transpose(1, 0, 2, 3).reshape(s)

    def interleave(ws):
        bs = [blocks(w).reshape(4, -1, P, WIDE) for w in ws]
        return np.concatenate(bs, 1).reshape(-1, P, WIDE)

    a = {n: np.asarray(v) for n, v in i.items()}
    parts = [
        blocks(beside(a["conv_w_pw1"][0][:, :D], a["conv_w_pw1"][0][:, D:])),
        blocks(a["conv_w_pw2"][0]),
        blocks(beside(a["ffn_w_gate"][0], a["ffn_w_up"][0])),
        blocks(a["ffn_w_down"][0]),
        a["pool_w_group"][0].reshape(8, P, WIDE),
        np.zeros((4, P, WIDE), np.float32),
    ]
    for e in range(NE):
        parts += [blocks(beside(a["moe_w_gate"][0, e], a["moe_w_up"][0, e])), blocks(a["moe_w_down"][0, e])]
    w = a["w_in_2"][0]
    q_a, kv, g_a, z_a, qkv_b, z_b, merge = np.split(w, np.cumsum([512, 768, 24, 512, 1536, 512]), 1)
    kv = np.split(kv, 6, 1)
    parts.append(blocks(np.concatenate(
        [by_group(q_a, 1), kv[0], kv[1], kv[2], kv[4], by_group(z_a, 1), qkv_b[:, 0:1024], z_b, merge,
         kv[3], kv[5], qkv_b[:, 1024:1536]], 1)))
    for n in ("cmp_w1_k_2", "cmp_w1_v_2"):
        w1 = a[n][0].reshape(16, 2, 64, P).transpose(0, 2, 1, 3).reshape(16, 64, WIDE)
        parts.append(np.concatenate([w1, w1], 1))
    parts.append(interleave([by_group(a["w_branch_a_2"][0], 0), a["w_branch_b_2"][0]]))
    parts.append(blocks(a["w_o_2"][0]))
    w = a["w_in_3"][0]
    l_x, l_g, m_qk, m_v, m_o, m_if, s_qk, s_v, g3 = np.split(
        w, np.cumsum([256, 256, 512, 256, 256, 8, 512, 256]), 1)
    parts.append(blocks(np.concatenate([l_x, m_qk, l_g, m_o, s_qk, g3, m_v, s_v], 1)))
    parts.append(interleave([a["w_out_lru_3"][0], a["w_out_mlstm_3"][0], a["w_out_sb_3"][0]]))
    parts.append(blocks(a["w_o_3"][0]))
    parts.append(blocks(beside(a["w_ffn_in_3"][0][:, :FF], a["w_ffn_in_3"][0][:, FF:])))
    parts.append(blocks(a["w_ffn_out_3"][0]))
    stream = np.zeros((NCH, P, CH, WIDE), np.float32)
    at = 0
    for p in parts:
        done = 0
        while done < len(p):
            c, o = (at + done) // CH, (at + done) % CH
            if o == 0 and len(p) - done >= CH:
                n = (len(p) - done) // CH
                stream[c:c + n] = p[done:done + n * CH].reshape(n, CH, P, WIDE).transpose(0, 2, 1, 3)
                done += n * CH
            else:
                n = min(CH - o, len(p) - done)
                stream[c, :, o:o + n] = p[done:done + n].transpose(1, 0, 2)
                done += n
        at += len(p)
    assert at == NBLK

    def cols(v):
        return v.reshape(-1, P).T

    def taps(w):
        return w.reshape(w.shape[0], -1, P).transpose(2, 1, 0).reshape(P, -1)

    def tall(v):
        o = np.zeros((P, v.shape[1]), np.float32)
        o[:v.shape[0]] = v
        return o

    def rows(w):
        return w.reshape(-1, P, w.shape[1]).transpose(1, 0, 2).reshape(P, -1)

    def twice(v):
        return np.concatenate([v, v], 0)

    vecs = {
        "b_pw1": cols(a["conv_b_pw1"][0]), "w_dw": taps(a["conv_w_dw"][0]), "b_dw": cols(a["conv_b_dw"][0]),
        "ln_g": cols(a["conv_ln_g"][0]), "ln_b": cols(a["conv_ln_b"][0]), "b_pw2": cols(a["conv_b_pw2"][0]),
        "pool_scale": cols(a["pool_scale"][0]), "mix_g0": cols(a["mix_norm_g"][0]), "mix_g1": cols(a["mix_norm_g"][1]),
        "ffn_g0": cols(a["ffn_norm_g"][0]), "ffn_g1": cols(a["ffn_norm_g"][1]), "final_g": cols(a["final_norm_g"]),
        "pre_g": cols(a["norm_pre_2"][0]), "post_g": cols(a["norm_post_2"][0]), "mix3_g": cols(a["norm_mix_g_3"][0]),
        "ffn3_g": cols(a["norm_ffn_g_3"][0]), "final3_g": cols(a["final_norm_g_3"]),
        "conv3": np.concatenate([taps(a["conv_lru_w_3"][0]), taps(a["conv_mlstm_w_3"][0])], 1),
        "lru_ba": cols(a["lru_ba_3"][0]), "lru_bx": cols(a["lru_bx_3"][0]), "lru_lam": cols(a["lru_lambda_3"][0]),
        "ig_b": tall(a["mlstm_ig_b_3"][0][:, None]), "fg_b": tall(a["mlstm_fg_b_3"][0][:, None]),
        "router": rows(a["moe_w_router"][0]), "w_gates": rows(g_a), "w_if": rows(m_if),
        "w2k": a["cmp_w2_k_2"][0], "w2v": a["cmp_w2_v_2"][0],
        "pek": twice(a["cmp_pe_k_2"][0].T), "pev": twice(a["cmp_pe_v_2"][0].T),
        "lru_wa": rows(a["lru_wa_3"][0].reshape(256, 64)), "lru_wx": rows(a["lru_wx_3"][0].reshape(256, 64)),
    }
    vec = np.concatenate([vecs[n] for n, _ in VECS], 1)
    assert vec.shape == (P, NV)
    h0 = np.concatenate([a["meta_tokens"], a["x"][0]], 0)
    h0 = h0.T.reshape(KD, P, T0).transpose(1, 0, 2)
    return {"w_stream": stream.reshape(NCH, P, CH * WIDE), "vec_in": np.ascontiguousarray(vec),
            "h_in": np.ascontiguousarray(h0)}


def kernel(**inputs):
    import concourse.bacc as _bacc
    from concourse.bass_utils import run_bass_kernel_spmd as _run

    arrays = _kernel_arrays(inputs)
    nc = _bacc.Bacc("TRN2", target_bir_lowering=False, num_devices=1)
    aps = [nc.dram_tensor(n, v.shape, F32, kind="ExternalInput").ap() for n, v in arrays.items()]
    out = nc.dram_tensor("out", (P, KD, SEQ), F32, kind="ExternalOutput").ap()
    program(nc, *aps, out)
    r = _run(nc, [arrays], core_ids=[0])
    got = np.asarray(r.results[0]["out"])
    return np.ascontiguousarray(got.transpose(2, 1, 0).reshape(1, SEQ, D))
```

```python
from contextlib import ExitStack

import numpy as np
import concourse.bass as bass
from concourse import mybir

F32 = mybir.dt.float32
U32 = mybir.dt.uint32
I32 = mybir.dt.int32
ALU = mybir.AluOpType
ACT = mybir.ActivationFunctionType
AX = mybir.AxisListType

P = 128
D = 1024
KD = D // P
META = 16
SEQ = 256
T0 = META + SEQ
CONVW = 31
FF = 2816
KF = FF // P
E_FF = 3584
KE = E_FF // P
NE = 8
CAP = 80
MAX_ITEMS = NE + 2 * SEQ // CAP
WIDE = 256
CH = 12
RING = 7
PE_TAPS = 16
NEG = -1.0e30
EPS = 1e-6
LN_EPS = 1e-5
CMP_N = 15

VECS = [
    ("b_pw1", 16), ("w_dw", KD * CONVW), ("b_dw", 8), ("ln_g", 8), ("ln_b", 8), ("b_pw2", 8),
    ("pool_scale", 8), ("mix_g0", 8), ("mix_g1", 8), ("ffn_g0", 8), ("ffn_g1", 8), ("final_g", 8),
    ("pre_g", 8), ("post_g", 8), ("mix3_g", 8), ("ffn3_g", 8), ("final3_g", 8),
    ("conv3", 6 * 4), ("lru_ba", 2), ("lru_bx", 2), ("lru_lam", 2), ("ig_b", 1), ("fg_b", 1),
    ("router", KD * NE), ("w_gates", KD * 24), ("w_if", KD * 8), ("w2k", 64), ("w2v", 64),
    ("pek", 32), ("pev", 32), ("lru_wa", 2 * 64), ("lru_wx", 2 * 64),
]
VOFF = {}
NV = 0
for _name, _n in VECS:
    VOFF[_name] = NV
    NV += _n

STAGES = [
    ("pw1", 8 * KD), ("pw2", 4 * KD), ("ffn0_in", KF * KD), ("ffn0_out", 4 * KF), ("pool", 8), ("pad", 4),
    ("moe", NE * (KE * KD + 4 * KE)),
    ("w_in2", 23 * KD), ("cmp", 32), ("branch", 4 * KD), ("w_o2", 4 * KD),
    ("w_in3", 21 * KD), ("outs3", 4 * 6), ("w_o3", 4 * KD), ("ffn3_in", KF * KD), ("ffn3_out", 4 * KF),
]
BOFF = {}
NBLK = 0
for _name, _n in STAGES:
    BOFF[_name] = NBLK
    NBLK += _n
assert BOFF["moe"] % CH == 0
MOE_BLK = KE * KD + 4 * KE
MOE_CH = MOE_BLK // CH
assert MOE_BLK % CH == 0 and MOE_CH % RING == 0
C_MOE = BOFF["moe"] // CH
C_POST = C_MOE + NE * MOE_CH
AHEAD = RING - 1
N_POST = -(-(-(-NBLK // CH) - C_POST - AHEAD) // RING) * RING + AHEAD
NCH = C_POST + N_POST


def nsa_slope(g, p):
    return float(np.float32(2.0 ** (-8.0 * (2 * (4 * g + p) + 1) / 16)))


def moba_slope(h):
    return float(np.float32(2.0 ** (-8.0 * (2 * h + 2) / 16)))


def program(nc, w_stream, vec_in, h_in, out):
    with ExitStack() as ctx:
        def sb(name, shape, dt=F32):
            return ctx.enter_context(nc.sbuf_tensor(name, shape, dt))

        def sem(name):
            return ctx.enter_context(nc.semaphore(name))

        ps = ctx.enter_context(nc.psum_tensor("ps", [P, 8, 512], F32))
        ring = sb("ring", [P, RING, CH * WIDE])
        vec = sb("vec", [P, NV])
        h = sb("h", [P, KD, T0])
        x = sb("x", [P, KD, SEQ])
        hn = sb("hn", [P, KD, T0])
        sq = sb("sq", [P, KD, T0])
        big = sb("big", [P, 12032])
        scr = sb("scr", [P, 5120])
        gate_sb = sb("gate_sb", [P, 2, T0])
        up_sb = sb("up_sb", [P, 2, SEQ])
        var = sb("var", [P, T0])
        rstd = sb("rstd", [P, T0])
        ident = sb("ident", [P, P])
        ones = sb("ones", [P, 2 * P])
        tri = sb("tri", [P, P])
        sel = sb("sel", [4, 4, P])
        alibi = sb("alibi", [P, 2 * P])
        cbias = sb("cbias", [P, 2, 16])
        tmask = sb("tmask", [P, 3 * P])
        smask = sb("smask", [P, 3 * P])
        small = sb("small", [P, 512])
        idx_u = sb("idx_u", [P, 2, 8], U32)
        table = sb("table", [P, 17], I32)
        upto = sb("upto", [P, P])
        iota_cap = sb("iota_cap", [P, CAP])
        iota16 = sb("iota16", [P, 16])

        def vcol(name, j=0, n=1, rows=P):
            return vec[0:rows, VOFF[name] + j:VOFF[name] + j + n]

        conv_u = big[:, 0:KD * 302].rearrange("p (k t) -> p k t", k=KD)
        conv_y = big[:, 2432:2432 + KD * T0].rearrange("p (k t) -> p k t", k=KD)
        diag = big[:, 4608:4608 + 2 * PE_TAPS * P].rearrange("p (b t c) -> p b t c", b=2, c=P)
        hid0 = big[:, 0:KF * T0].rearrange("p (k t) -> p k t", k=KF)
        pool_a = big[:, 6000:6000 + 2 * T0].rearrange("p (k t) -> p k t", k=2)
        pool_b = big[:, 6600:6600 + 2 * T0].rearrange("p (k t) -> p k t", k=2)
        hid = big[:, 0:KE * SEQ].rearrange("p (k t) -> p k t", k=KE)
        x_tok = big[:, 2560:2560 + 2 * D].rearrange("p (t d) -> p t d", t=2)
        x_item = big[:, 4608:4608 + KD * CAP].rearrange("p (k c) -> p k c", k=KD)
        y_item = big[:, 5248:5248 + KD * CAP].rearrange("p (k c) -> p k c", k=KD)
        hid_item = big[:, 0:KE * CAP].rearrange("p (k c) -> p k c", k=KE)
        y_tok = big[:, 5888:5888 + D]
        pick = big[:, 6912:6912 + 2 * CAP].rearrange("p (t c) -> p t c", t=2)
        pick2 = big[:, 7072:7072 + 2 * CAP].rearrange("p (t c) -> p t c", t=2)
        wpick = big[:, 7232:7232 + 2 * CAP].rearrange("p (t c) -> p t c", t=2)
        wpick2 = big[:, 7392:7392 + 2 * CAP].rearrange("p (t c) -> p t c", t=2)
        w_row = big[:, 7552:7552 + SEQ]
        proj = big[:, 0:40 * SEQ].rearrange("p (k t) -> p k t", k=40)
        vtok = big[:, 10240:10240 + 1536].rearrange("p (t c) -> p t c", t=2)
        mean = gate_sb[:, 0, :]
        zo = proj[:, 0:8, :]
        sq256 = sq[:, :, 0:SEQ]
        hn256 = hn[:, :, 0:SEQ]
        soft = scr[:, 0:2048].rearrange("p (b a k) -> p b a k", b=2, a=4)
        probT = scr[:, 2048:2048 + 2560].rearrange("p (u c) -> p u c", u=5)
        part = scr[:, 0:1536].rearrange("p (b n k) -> p b n k", b=2, n=3)
        logit = small[:, 0:16].rearrange("p (t e) -> p t e", t=2)
        top = small[:, 16:32].rearrange("p (t e) -> p t e", t=2)
        top_i = small[:, 32:48].rearrange("p (t e) -> p t e", t=2)
        gap = small[:, 48:64].rearrange("p (t e) -> p t e", t=2)
        hot1 = small[:, 64:80].rearrange("p (t e) -> p t e", t=2)
        hot2 = small[:, 80:96].rearrange("p (t e) -> p t e", t=2)
        hot = small[:, 96:112].rearrange("p (t e) -> p t e", t=2)
        place = small[:, 112:128].rearrange("p (t e) -> p t e", t=2)
        over = small[:, 208:216]
        ends = small[:, 216:224]
        begins = small[:, 224:232]
        owner = small[:, 232:248]
        at12 = small[:, 248:252]
        cmp_h = small[:, 128:192].rearrange("p (n c) -> p n c", n=4)
        cmp_k = small[:, 192:208]
        cmp_v = small[:, 256:384]
        gates = small[:, 384:432]
        stats = small[:, 432:464].rearrange("p (b n c) -> p b n c", b=2, n=4)
        ccol = small[:, 464:472]
        lam = small[:, 472:488].rearrange("p (n c) -> p n c", n=8)
        cmp_pe = small[:, 488:490]
        v3 = big[:, 10240:10240 + 1024].rearrange("p (t c) -> p t c", t=2)
        crow, mrow, floor = (big[0:4, 11264 + 256 * n:11520 + 256 * n] for n in range(3))
        irow, frow = (big[0:4, 9728 + 256 * n:9984 + 256 * n] for n in range(2))
        arow, brow = up_sb[0:4, 0, :], up_sb[0:4, 1, :]
        hflat = h[:, :, :].rearrange("p k t -> p (k t)")
        cin = hflat[:, 0:6 * 259].rearrange("p (k t) -> p k t", k=6)
        cpad = cin[:, :, 0:3]
        sb_lk = big[:, 0:1536].rearrange("p (h c) -> p h c", h=4)
        sb_w = sq[:, :, :].rearrange("p k t -> p (k t)")[:, 0:1536].rearrange("p (h c) -> p h c", h=4)
        zs = hn[:, :, :].rearrange("p k t -> p (k t)")[:, 0:1536].rearrange("p (h c) -> p h c", h=4)
        decay = zs
        xa = scr[:, 0:512].rearrange("p (k t) -> p k t", k=2)
        qk3 = scr[:, 512:1536].rearrange("p (k t) -> p k t", k=4)
        y3 = scr[:, 1536:3072].rearrange("p (k t) -> p k t", k=6)
        lru_t = scr[:, 3072:5120].rearrange("p (n k t) -> p n k t", n=4, k=2)
        part3 = scr[:, 3072:3072 + 1536].rearrange("p (b n k) -> p b n k", b=2, n=3)

        pre_landed = [sem(f"pre_landed{s}") for s in range(RING)]
        moe_landed = [sem(f"moe_landed{s}") for s in range(RING)]
        post_landed = [sem(f"post_landed{s}") for s in range(RING)]
        pre_begun, moe_begun, post_begun = sem("pre_begun"), sem("moe_begun"), sem("post_begun")
        S = {}
        for n in """vec_landed h_landed consts_ready pool_step dve_step act_step
                    sq_ready sum_done var_ready std_ready normed
                    pw1_done glu_sig glu_done diag_ready conv_done conv_ready mean_done xc_ready ln_ready
                    ln_silu pw2_done h1_ready ffn_gu ffn_sig ffn_hid ffn_down ffn_out
                    pooled pool_done x_ready router_done gap_ready gap_exp chosen ranks_done table_ready
                    xt_done xt_ready at_moved picks_made picks_ready pick_done pick_ready wt_done wt_ready
                    moe_gu moe_sig moe_hid moe_down moe_y moe_yt_done moe_yt moe_sum moe_out moe_all
                    in2_done in2_act in2_dve gl_done gates_ready cmp_h_done cmp_pe_ready cmp_h_ready cmp_kv_done
                    cmp_kv_ready score_done s_ready exp_ready prob_ready turn_done turned pv_done y_ready
                    br_done br_part br_ready wo2_done wo2_ready
                    in3_done in3_act in3_dve if_done conv3_ready qk_silu lru_g_done lru_sig lam_exp lam_ln
                    lru_loga lru_a lru_f lru_sqrt lru_y lru_in gelu_ready
                    gate_in gate_ln c_ready cT_done cT_ready m_floor_in m_floor mb_done mb_ready ml_s_done ml_exp
                    ml_p ml_nd_done fl_done fl_ready mh_ready
                    sb_z_done sb_zs sb_ln sb_lk sb_r_done sb_arg sb_a sb_o_done sb_y
                    out3_done out3_part merged wo3_done x3_ready out_done""".split():
            S[n] = sem(n)

        block = ctx.enter_context(nc.Block())

        jobs = [("nsa", i, g) for i in range(2) for g in range(2)] + \
               [("moba", i, hh) for i in range(2) for hh in range(2)]
        subs = []
        for j, (kind, i, g) in enumerate(jobs):
            for br in (("cmp", "slc", "win") if kind == "nsa" else ("moba",)):
                subs.append((j, kind, i, g, br))
        turns = [1 if br == "cmp" else i + 1 for (_, _, i, _, br) in subs]
        turns_before = [sum(turns[:s]) for s in range(len(subs) + 1)]
        job_last_turn = {}
        for s, (j, *_r) in enumerate(subs):
            job_last_turn[j] = turns_before[s + 1]
        prob_slot = {"cmp": 4, "slc": 0, "win": 2, "moba": 0}

        QA, KC, VC, KS, KW, ZA, QB, KB, ZB, MG = 0, 4, 5, 6, 7, 8, 12, 16, 20, 24
        L_X, M_QK, L_G, M_O, S_Q, S_K, G3 = 0, 2, 6, 8, 10, 12, 14
        taker2 = ["dve"] * 4 + ["act"] * 2 + ["dve"] * 4 + ["act"] * 10 + ["dve"] * 3
        taker3 = ["dve"] * 3 + ["act"] * 2 + ["dve"] * 2 + ["act"] * 12 + ["dve"] * 2

        def taken(taker, stage, p):
            return S[f"{stage}_{taker[p]}"], taker[:p + 1].count(taker[p])

        @block.sync
        def _(sp):
            def slot(c):
                return ring[:, c % RING, :]

            for c in range(RING):
                sp.dma_start(slot(c), w_stream[c]).then_inc(pre_landed[c], 16)
            turns_pre = C_MOE // RING
            with sp.Fori(1, turns_pre) as r:
                for n in range(RING):
                    sp.wait_ge(pre_begun, r * RING + (n - RING + 2))
                    sp.dma_start(slot(n), w_stream[r * RING + n]).then_inc(pre_landed[n], 16)
            for c in range(turns_pre * RING, C_MOE):
                sp.wait_ge(pre_begun, c - RING + 2)
                sp.dma_start(slot(c), w_stream[c]).then_inc(pre_landed[c % RING], 16)
            for c in range(C_MOE, C_MOE + AHEAD):
                sp.wait_ge(pre_begun, c - RING + 2)
                sp.dma_start(slot(c), w_stream[c]).then_inc(moe_landed[c % RING], 16)
            sp.wait_ge(S["table_ready"], 1)
            items = sp.value_load(table[0:1, 16:17], min_val=NE, max_val=MAX_ITEMS)
            with sp.Fori(0, items) as i:
                this = sp.value_load(table[0:1, bass.ds(i, 1)], min_val=0, max_val=NE)
                for c in range(AHEAD, MOE_CH):
                    sp.wait_ge(moe_begun, i * MOE_CH + (c - RING + 2))
                    sp.dma_start(slot(C_MOE + c), w_stream[this * MOE_CH + (C_MOE + c)])\
                      .then_inc(moe_landed[(C_MOE + c) % RING], 16)
                then = sp.value_load(table[0:1, bass.ds(i + 1, 1)], min_val=0, max_val=NE)
                for c in range(AHEAD):
                    sp.wait_ge(moe_begun, i * MOE_CH + (MOE_CH + c - RING + 2))
                    sp.dma_start(slot(C_MOE + c), w_stream[then * MOE_CH + (C_MOE + c)])\
                      .then_inc(moe_landed[(C_MOE + c) % RING], 16)
            with sp.Fori(0, (N_POST - AHEAD) // RING) as r:
                for n in range(RING):
                    sp.wait_ge(post_begun, r * RING + (n + 1))
                    sp.dma_start(slot(C_POST + AHEAD + n), w_stream[r * RING + (C_POST + AHEAD + n)])\
                      .then_inc(post_landed[(C_POST + AHEAD + n) % RING], 16)
            sp.wait_ge(S["normed"], 8 * 11)
            sp.dma_start(out, hn256).then_inc(S["out_done"], 16)
            sp.wait_ge(S["out_done"], 16)

        @block.tensor
        def _(pe):
            bank_owner = {}
            at_chunk = [-1]
            items = []

            def claim(b):
                if b in bank_owner:
                    pe.wait_ge(*bank_owner.pop(b))

            def block_of(b):
                c = b // CH
                first = c != at_chunk[0]
                if first:
                    assert c == at_chunk[0] + 1
                    at_chunk[0] = c
                    if c < C_MOE:
                        pe.wait_ge(pre_landed[c % RING], 16 * (c // RING + 1))
                    elif c < C_POST + AHEAD:
                        pe.wait_ge(moe_landed[c % RING], items[0] * (16 * (MOE_CH // RING)) + 16)
                    else:
                        pe.wait_ge(post_landed[c % RING], 16 * ((c - C_POST - AHEAD) // RING + 1))
                return ring[:, c % RING, (b % CH) * WIDE:(b % CH + 1) * WIDE], first

            def begun(first, mm):
                if first:
                    mm.then_inc(pre_begun if at_chunk[0] < C_MOE else post_begun, 1)

            def pair(b0, kt, src, t, bank, done, inputs=None):
                claim(bank)
                claim(bank + 1)
                for k in range(kt):
                    if inputs is not None:
                        inputs(k)
                    w, first = block_of(b0 + k)
                    for half in range(2):
                        mm = pe.matmul(ps[:, bank + half, 0:t], w[:, half * P:half * P + P], src(k),
                                       start=(k == 0), stop=(k == kt - 1))
                        if half == 0:
                            begun(first, mm)
                        if k == kt - 1:
                            mm.then_inc(done, 1)

            def token_pair(b0, src, bank, done):
                claim(bank)
                claim(bank + 1)
                for k in range(KD):
                    w, first = block_of(b0 + k)
                    for t in range(2):
                        mm = pe.matmul(ps[:, bank + t, 0:WIDE], src[:, k, t * P:(t + 1) * P], w,
                                       start=(k == 0), stop=(k == KD - 1))
                        if t == 0:
                            begun(first, mm)
                        if k == KD - 1:
                            mm.then_inc(done, 1)

            def sum_squares(i, t):
                for k in range(KD):
                    pe.wait_ge(S["sq_ready"], 8 * i + k + 1)
                    mm = pe.matmul(ps[:, 7, 0:t], ones[:, 0:P], sq[:, k, 0:t], start=(k == 0), stop=(k == KD - 1))
                mm.then_inc(S["sum_done"], 1)

            def after_norm(i):
                return lambda k: pe.wait_ge(S["normed"], 8 * i + k + 1)

            pe.wait_ge(S["consts_ready"], 1)
            pe.wait_ge(S["vec_landed"], 16)
            sum_squares(0, T0)

            def conv_tile(j):
                pe.wait_ge(S["glu_done"], j + 1)
                pe.wait_ge(S["diag_ready"], PE_TAPS * (j + 1))
                claim(6)
                for tap in range(PE_TAPS):
                    mm = pe.matmul(ps[:, 6, 0:T0], diag[:, j % 2, tap, :], conv_u[:, j, tap:tap + T0],
                                   start=(tap == 0), stop=(tap == PE_TAPS - 1))
                mm.then_inc(S["conv_done"], 1)
                bank_owner[6] = (S["conv_ready"], j + 1)

            for j in range(8):
                b = 2 * (j % 3)
                pair(BOFF["pw1"] + j * KD, KD, lambda k: hn[:, k, :], T0, b, S["pw1_done"],
                     after_norm(0) if j == 0 else None)
                bank_owner[b] = (S["glu_done"], j + 1)
                bank_owner[b + 1] = (S["glu_sig"], j + 1)
                if j >= 1:
                    conv_tile(j - 1)
            conv_tile(7)
            for k in range(KD):
                pe.wait_ge(S["conv_ready"], k + 1)
                mm = pe.matmul(ps[:, 7, 0:T0], ones[:, 0:P], conv_y[:, k, :], start=(k == 0), stop=(k == KD - 1))
            mm.then_inc(S["mean_done"], 1)
            sum_squares(1, T0)
            for j in range(4):
                b = 2 * (j % 3)
                pair(BOFF["pw2"] + j * KD, KD, lambda k: sq[:, k, :], T0, b, S["pw2_done"],
                     (lambda k: pe.wait_ge(S["ln_silu"], k + 1)) if j == 0 else None)
                bank_owner[b] = (S["h1_ready"], 2 * j + 1)
                bank_owner[b + 1] = (S["h1_ready"], 2 * j + 2)

            def ffn(n, norm_i, t, hidden, b_in, b_out):
                sum_squares(norm_i, t)
                for p in range(KF):
                    b = 2 * (p % 3)
                    pair(b_in + p * KD, KD, lambda k: hn[:, k, 0:t], t, b, S["ffn_gu"],
                         after_norm(norm_i) if p == 0 else None)
                    bank_owner[b] = (S["ffn_sig"], n * KF + p + 1)
                    bank_owner[b + 1] = (S["ffn_hid"], n * KF + p + 1)
                for j in range(4):
                    b = 2 * (j % 3)
                    pair(b_out + j * KF, KF, lambda k: hidden[:, k, 0:t], t, b, S["ffn_down"],
                         (lambda k: pe.wait_ge(S["ffn_hid"], n * KF + k + 1)) if j == 0 else None)
                    bank_owner[b] = (S["ffn_out"], 8 * n + 2 * j + 1)
                    bank_owner[b + 1] = (S["ffn_out"], 8 * n + 2 * j + 2)

            ffn(0, 2, T0, hid0, BOFF["ffn0_in"], BOFF["ffn0_out"])
            sum_squares(3, T0)
            for g in range(4):
                b = 2 * (g % 3)
                pe.wait_ge(S["pooled"], g + 1)
                pair(BOFF["pool"] + 2 * g, 2, lambda k: sq256[:, 2 * g + k, :], SEQ, b, S["pool_done"])
                bank_owner[b] = (S["x_ready"], 2 * g + 1)
                bank_owner[b + 1] = (S["x_ready"], 2 * g + 2)
            sum_squares(4, SEQ)
            pe.wait_ge(S["normed"], 8 * 5)
            for t in range(2):
                for k in range(KD):
                    mm = pe.matmul(ps[:, 6, t * NE:(t + 1) * NE], hn[:, k, t * P:(t + 1) * P],
                                   vcol("router", k * NE, NE), start=(k == 0), stop=(k == KD - 1))
            mm.then_inc(S["router_done"], 1)
            pe.wait_ge(S["chosen"], 1)
            pe.matmul(ps[:, 6, 16:24], upto[:, :], hot[:, 0, :], start=True, stop=True)
            pe.matmul(ps[:, 6, 24:32], ones[:, 0:P], hot[:, 0, :], start=True, stop=False)
            pe.matmul(ps[:, 6, 24:32], upto[:, :], hot[:, 1, :], start=False, stop=True)
            pe.matmul(ps[:, 6, 32:40], ones[:, 0:P], hot[:, 0, :], start=True, stop=False)
            pe.matmul(ps[:, 6, 32:40], ones[:, 0:P], hot[:, 1, :], start=False, stop=True)\
              .then_inc(S["ranks_done"], 1)
            pe.wait_ge(S["x_ready"], 8)
            for t in range(2):
                for k in range(KD):
                    mm = pe.transpose(ps[:, 2 * t + k // 4, (k % 4) * P:(k % 4 + 1) * P],
                                      hn[:, k, t * P:(t + 1) * P], ident[:, :])
                mm.then_inc(S["xt_done"], 1)
            bank_owner.clear()
            pe.wait_ge(S["xt_ready"], 2)
            assert at_chunk[0] == C_MOE - 1
            pe.wait_ge(S["table_ready"], 1)
            items.append(pe.value_load(table[0:1, 16:17], min_val=NE, max_val=MAX_ITEMS))
            with pe.Fori(0, items[0]) as i:
                blk = [0, -1]

                def moe_block():
                    b, blk[0] = blk[0], blk[0] + 1
                    c = b // CH
                    first = c != blk[1]
                    blk[1] = c
                    s = (C_MOE + c) % RING
                    if first:
                        pe.wait_ge(moe_landed[s], i * (16 * (MOE_CH // RING)) + 16 * (c // RING + 1))
                    return ring[:, s, (b % CH) * WIDE:(b % CH + 1) * WIDE], first

                def moe_pair(kt, src, bank, done):
                    for k in range(kt):
                        w, first = moe_block()
                        for half in range(2):
                            mm = pe.matmul(ps[:, bank + half, 0:CAP], w[:, half * P:half * P + P], src[:, k, :],
                                           start=(k == 0), stop=(k == kt - 1))
                            if half == 0 and first:
                                mm.then_inc(moe_begun, 1)
                            if k == kt - 1:
                                mm.then_inc(done, 1)

                pe.wait_ge(S["picks_ready"], i + 1)
                pe.wait_ge(S["moe_out"], i * 4 + 1)
                for k in range(KD):
                    for t in range(2):
                        mm = pe.matmul(ps[:, k // 4, (k % 4) * CAP:(k % 4 + 1) * CAP],
                                       x_tok[:, t, k * P:(k + 1) * P], pick[:, t, :], start=(t == 0), stop=(t == 1))
                mm.then_inc(S["pick_done"], 1)
                for t in range(2):
                    mm = pe.transpose(ps[0:CAP, 2, t * P:(t + 1) * P], wpick[:, t, :], ident[:, :])
                mm.then_inc(S["wt_done"], 1)
                pe.wait_ge(S["pick_ready"], i + 1)
                for p in range(KE):
                    if p == 1:
                        pe.wait_ge(S["wt_ready"], i + 1)
                    if p >= 3:
                        pe.wait_ge(S["moe_sig"], i * KE + (p - 2))
                        pe.wait_ge(S["moe_hid"], i * KE + (p - 2))
                    moe_pair(KD, x_item, 2 * (p % 3), S["moe_gu"])
                pe.wait_ge(S["moe_hid"], i * KE + KE)
                for j in range(4):
                    if j == 3:
                        pe.wait_ge(S["moe_y"], i * 4 + 1)
                    moe_pair(KE, hid_item, 2 * (j % 3), S["moe_down"])
                for j in range(4):
                    pe.wait_ge(S["moe_y"], i * 4 + (j + 1))
                    for k in (2 * j, 2 * j + 1):
                        mm = pe.transpose(ps[0:CAP, 6 + k // 4, (k % 4) * P:(k % 4 + 1) * P], y_item[:, k, :],
                                          ident[:, :])
                    if j % 2:
                        mm.then_inc(S["moe_yt_done"], 1)
                for k in range(KD):
                    if k % 4 == 0:
                        pe.wait_ge(S["moe_yt"], i * 2 + (k // 4 + 1))
                    mm = pe.matmul(ps[:, k // 2, (k % 2) * SEQ:(k % 2 + 1) * SEQ], y_tok[0:CAP, k * P:(k + 1) * P],
                                   w_row[0:CAP, :], start=True, stop=True)
                    if k % 2:
                        mm.then_inc(S["moe_sum"], 1)
            at_chunk[0] = C_POST - 1
            pe.wait_ge(S["moe_all"], 1)

            sum_squares(5, SEQ)
            sum_squares(6, SEQ)
            for p in range(23):
                b = 2 * (p % 3)
                if p < 20:
                    pair(BOFF["w_in2"] + p * KD, KD, lambda k: hn256[:, k, :], SEQ, b, S["in2_done"],
                         after_norm(6) if p == 0 else None)
                else:
                    token_pair(BOFF["w_in2"] + p * KD, hn256, b, S["in2_done"])
                bank_owner[b] = bank_owner[b + 1] = taken(taker2, "in2", p)
            for t in range(2):
                for k in range(KD):
                    mm = pe.matmul(ps[:, 6, t * 24:(t + 1) * 24], hn256[:, k, t * P:(t + 1) * P],
                                   vcol("w_gates", k * 24, 24), start=(k == 0), stop=(k == KD - 1))
            mm.then_inc(S["gl_done"], 1)
            pe.wait_ge(S["in2_act"], taker2.count("act"))
            pe.wait_ge(S["in2_dve"], taker2.count("dve"))
            bank_owner.clear()
            for kv in range(2):
                src = proj[:, KC + kv, :]
                pe_off = VOFF["pev" if kv else "pek"]
                for l in range(32):
                    w, first = block_of(BOFF["cmp"] + 16 * kv + l // 2)
                    for g in range(2):
                        lo = 64 * g
                        lw = w[lo:lo + 64, (l % 2) * P:(l % 2) * P + P]
                        mm = pe.matmul(ps[:, 2 * kv + g, 0:CMP_N], lw,
                                       src[lo:lo + 64, l:l + 16 * (CMP_N - 1) + 1:16],
                                       start=(l == 0), stop=(l == 31))
                        begun(g == 0 and l % 2 == 0 and first, mm)
                    mm = pe.matmul(ps[:, 4 + kv, 0:1], w[0:64, (l % 2) * P:(l % 2) * P + P],
                                   vec[0:64, pe_off + l:pe_off + l + 1], start=(l == 0), stop=(l == 31))
                mm.then_inc(S["cmp_h_done"], 1)
            for kv in range(2):
                pe.wait_ge(S["cmp_h_ready"], 2 * kv + 2)
                for g in range(2):
                    hidc = cmp_h[:, 2 * kv + g, 0:CMP_N]
                    if kv == 0:
                        mm = pe.matmul(ps[64 * g:64 * g + 64, 6, 64:64 + CMP_N], vcol("w2k", 0, 64), hidc,
                                       start=True, stop=True)
                    else:
                        mm = pe.matmul(ps[0:CMP_N, 7, 64 * g:64 * g + 64], hidc, vcol("w2v", 0, 64),
                                       start=True, stop=True)
            mm.then_inc(S["cmp_kv_done"], 1)
            pe.wait_ge(S["cmp_kv_ready"], 2)
            pe.wait_ge(S["gates_ready"], 1)

            def scores(s):
                j, kind, i, g, br = subs[s]
                if s >= 2:
                    pe.wait_ge(S["s_ready"], s - 1)
                n = CMP_N if br == "cmp" else (i + 1) * P
                for p in range(4):
                    bank = 2 * (s % 2) + p % 2
                    if kind == "nsa":
                        lo = 64 * g
                        q = proj[lo:lo + 64, QA + p, i * P:(i + 1) * P]
                        key = cmp_k[lo:lo + 64, 0:CMP_N] if br == "cmp" else \
                            proj[lo:lo + 64, KS if br == "slc" else KW, 0:n]
                    else:
                        hd = 4 * g + p
                        lo = 64 * (hd % 2)
                        q = proj[lo:lo + 64, QB + hd // 2, i * P:(i + 1) * P]
                        key = proj[lo:lo + 64, KB + hd // 2, 0:n]
                    mm = pe.matmul(ps[:, bank, (p // 2) * 256:(p // 2) * 256 + n], q, key, start=True, stop=True)
                mm.then_inc(S["score_done"], 1)

            def turn(s):
                j, kind, i, g, br = subs[s]
                pe.wait_ge(S["prob_ready"], s + 1)
                for kt in range(turns[s]):
                    u = turns_before[s] + kt
                    if u >= 2:
                        pe.wait_ge(S["turned"], u - 1)
                    for p in range(4):
                        if br == "cmp":
                            mm = pe.transpose(ps[0:CMP_N, 4 + u % 2, p * P:(p + 1) * P],
                                              soft[:, s % 2, p, 0:CMP_N], ident[:, :])
                        else:
                            mm = pe.transpose(ps[:, 4 + u % 2, p * P:(p + 1) * P],
                                              soft[:, s % 2, p, kt * P:(kt + 1) * P], ident[:, :])
                    mm.then_inc(S["turn_done"], 1)

            def values(j):
                kind, i, g = jobs[j]
                pe.wait_ge(S["turned"], job_last_turn[j])
                if j >= 2:
                    pe.wait_ge(S["y_ready"], j - 1)
                for p in range(4):
                    if kind == "nsa":
                        o = ps[64 * g:64 * g + 64, 6 + j % 2, p * P:(p + 1) * P]
                        terms = [(cmp_v[0:CMP_N, 64 * g:64 * g + 64], probT[0:CMP_N, 4, p * P:(p + 1) * P])]
                        for br in (0, 1):
                            terms += [(vtok[:, kt, br * P + 64 * g:br * P + 64 * g + 64],
                                       probT[:, 2 * br + kt, p * P:(p + 1) * P]) for kt in range(i + 1)]
                    else:
                        hd = 4 * g + p
                        lo = 64 * (hd % 2)
                        o = ps[lo:lo + 64, 6 + j % 2, (p // 2) * P:(p // 2 + 1) * P]
                        terms = [(vtok[:, kt, 256 + 64 * hd:256 + 64 * hd + 64],
                                  probT[:, kt, p * P:(p + 1) * P]) for kt in range(i + 1)]
                    for n, (lw, r) in enumerate(terms):
                        mm = pe.matmul(o, lw, r, start=(n == 0), stop=(n == len(terms) - 1))
                mm.then_inc(S["pv_done"], 1)

            scores(0)
            for s in range(len(subs)):
                if s + 1 < len(subs):
                    scores(s + 1)
                turn(s)
                if s + 1 == len(subs) or subs[s + 1][0] != subs[s][0]:
                    values(subs[s][0])
            pe.wait_ge(S["y_ready"], 8)
            for j in range(4):
                if j >= 2:
                    pe.wait_ge(S["br_ready"], 2 * j - 2)
                for br in range(2):
                    for k in range(4):
                        w, first = block_of(BOFF["branch"] + j * KD + 4 * br + k)
                        for half in range(2):
                            mm = pe.matmul(ps[:, 4 * (j % 2) + 2 * br + half, 0:SEQ], w[:, half * P:half * P + P],
                                           sq256[:, 4 * br + k, :], start=(k == 0), stop=(k == 3))
                            begun(half == 0 and first, mm)
                mm.then_inc(S["br_done"], 1)
            pe.wait_ge(S["br_ready"], 8)
            for j in range(4):
                b = 2 * (j % 3)
                pair(BOFF["w_o2"] + j * KD, KD, lambda k: hn256[:, k, :], SEQ, b, S["wo2_done"])
                bank_owner[b] = (S["wo2_ready"], 2 * j + 1)
                bank_owner[b + 1] = (S["wo2_ready"], 2 * j + 2)
            sum_squares(7, SEQ)

            sum_squares(8, SEQ)
            for p in range(21):
                b = 2 * (p % 3)
                if p < 19:
                    pair(BOFF["w_in3"] + p * KD, KD, lambda k: hn256[:, k, :], SEQ, b, S["in3_done"],
                         after_norm(8) if p == 0 else None)
                else:
                    token_pair(BOFF["w_in3"] + p * KD, hn256, b, S["in3_done"])
                bank_owner[b] = bank_owner[b + 1] = taken(taker3, "in3", p)
            for n in range(2):
                for k in range(KD):
                    mm = pe.matmul(ps[0:4, 6, n * SEQ:(n + 1) * SEQ], vcol("w_if", k * 8 + 4 * n, 4),
                                   hn256[:, k, :], start=(k == 0), stop=(k == KD - 1))
            mm.then_inc(S["if_done"], 1)
            bank_owner.clear()
            pe.wait_ge(S["in3_act"], taker3.count("act"))
            pe.wait_ge(S["in3_dve"], taker3.count("dve"))
            for hd in range(4):
                lo = 64 * (hd % 2)
                for kt in range(2):
                    mm = pe.matmul(ps[:, hd, 256 * kt:256 * kt + SEQ - P * kt],
                                   proj[lo:lo + 64, S_K + hd // 2, kt * P:(kt + 1) * P],
                                   proj[lo:lo + 64, S_Q + hd // 2, kt * P:SEQ], start=True, stop=True)
                mm.then_inc(S["sb_z_done"], 1)
            pe.wait_ge(S["conv3_ready"], 1)
            for n, name in enumerate(("lru_wa", "lru_wx")):
                for t in range(2):
                    for lo in (0, 64):
                        mm = pe.matmul(ps[lo:lo + 64, 4 + n, t * SEQ:(t + 1) * SEQ],
                                       vec[lo:lo + 64, VOFF[name] + 64 * t:VOFF[name] + 64 * t + 64],
                                       xa[lo:lo + 64, t, :], start=True, stop=True)
            mm.then_inc(S["lru_g_done"], 1)
            pe.wait_ge(S["c_ready"], 1)
            for t in range(2):
                mm = pe.transpose(ps[:, 7, 4 * t:4 * t + 4], crow[:, t * P:(t + 1) * P], ident[0:4, 0:4])
            mm.then_inc(S["cT_done"], 1)
            for hd in range(4):
                pe.wait_ge(S["sb_lk"], hd + 1)
                pe.matmul(ps[:, hd, 0:SEQ], tri[:, :], sb_lk[:, hd, 0:SEQ], start=True, stop=False)
                pe.matmul(ps[:, hd, P:SEQ], ones[:, 0:P], sb_lk[:, hd, SEQ:3 * P], start=False, stop=True)
                mm = pe.matmul(ps[:, hd, SEQ:3 * P], tri[:, :], sb_lk[:, hd, SEQ:3 * P], start=True, stop=True)
                mm.then_inc(S["sb_r_done"], 1)
            pe.wait_ge(S["lru_sig"], 2)
            for hd in range(4):
                lo = 64 * (hd % 2)
                c0v = 256 + 64 * hd
                pe.wait_ge(S["sb_a"], hd + 1)
                o = ps[lo:lo + 64, 4, (hd // 2) * SEQ:(hd // 2 + 1) * SEQ]
                pe.matmul(o, v3[:, 0, c0v:c0v + 64], sb_w[:, hd, 0:SEQ], start=True, stop=False)
                mm = pe.matmul(o[:, P:SEQ], v3[:, 1, c0v:c0v + 64], sb_w[:, hd, SEQ:3 * P], start=False, stop=True)
            mm.then_inc(S["sb_o_done"], 1)
            pe.wait_ge(S["m_floor"], 1)
            pe.wait_ge(S["cT_ready"], 1)
            for hd in range(4):
                mm = pe.matmul(ps[:, hd // 2, (hd % 2) * SEQ:(hd % 2 + 1) * SEQ], sel[0:4, hd, :], mrow,
                               start=True, stop=True)
            mm.then_inc(S["mb_done"], 1)
            for hd in range(4):
                lo = 64 * (hd % 2)
                mm = pe.matmul(ps[lo:lo + 64, 5, (hd // 2) * SEQ:(hd // 2 + 1) * SEQ], sel[0:4, hd, 0:64],
                               floor, start=True, stop=True)
            mm.then_inc(S["fl_done"], 1)
            pe.wait_ge(S["mb_ready"], 4)
            pe.wait_ge(S["qk_silu"], 1)
            for hd in range(4):
                lo = 64 * (hd % 2)
                for kt in range(2):
                    mm = pe.matmul(ps[:, hd, 256 * kt:256 * kt + SEQ - P * kt],
                                   qk3[lo:lo + 64, 2 + hd // 2, kt * P:(kt + 1) * P],
                                   qk3[lo:lo + 64, hd // 2, kt * P:SEQ], start=True, stop=True)
                mm.then_inc(S["ml_s_done"], 1)
            for hd in range(4):
                lo = 64 * (hd % 2)
                pe.wait_ge(S["ml_p"], hd + 1)
                for bank, lws in ((6, (v3[:, 0, 64 * hd:64 * hd + 64], v3[:, 1, 64 * hd:64 * hd + 64])),
                                  (7, (ones[:, 0:64], ones[:, 0:64]))):
                    o = ps[lo:lo + 64, bank, (hd // 2) * SEQ:(hd // 2 + 1) * SEQ]
                    pe.matmul(o, lws[0], sb_w[:, hd, 0:SEQ], start=True, stop=False)
                    mm = pe.matmul(o[:, P:SEQ], lws[1], sb_w[:, hd, SEQ:3 * P], start=False, stop=True)
            mm.then_inc(S["ml_nd_done"], 1)
            pe.wait_ge(S["lru_in"], 1)
            pe.wait_ge(S["sb_y"], 1)
            pe.wait_ge(S["mh_ready"], 1)
            for j in range(4):
                pe.wait_ge(S["merged"], 2 * j)
                for br in range(3):
                    for k in range(2):
                        w, first = block_of(BOFF["outs3"] + j * 6 + 2 * br + k)
                        for half in range(2):
                            mm = pe.matmul(ps[:, 3 * half + br, 0:SEQ], w[:, half * P:half * P + P],
                                           y3[:, 2 * br + k, :], start=(k == 0), stop=(k == 1))
                            begun(half == 0 and first, mm)
                mm.then_inc(S["out3_done"], 1)
            pe.wait_ge(S["merged"], 8)
            for j in range(4):
                b = 2 * (j % 3)
                pair(BOFF["w_o3"] + j * KD, KD, lambda k: hn256[:, k, :], SEQ, b, S["wo3_done"])
                bank_owner[b] = (S["x3_ready"], 2 * j + 1)
                bank_owner[b + 1] = (S["x3_ready"], 2 * j + 2)
            ffn(1, 9, SEQ, hid, BOFF["ffn3_in"], BOFF["ffn3_out"])
            sum_squares(10, SEQ)
            for c in range(at_chunk[0] + 1, NCH):
                pe.wait_ge(post_landed[c % RING], 16 * ((c - C_POST - AHEAD) // RING + 1))

        @block.scalar
        def _(act):
            steps = [0]

            def step(ins):
                steps[0] += 1
                ins.then_inc(S["act_step"], 1)
                act.wait_ge(S["act_step"], steps[0])

            def norm(i, src, t, ready):
                for k in range(KD):
                    ready(k)
                    act.activation(sq[:, k, 0:t], src[:, k, 0:t], ACT.Square).then_inc(S["sq_ready"], 1)
                act.wait_ge(S["var_ready"], i + 1)
                act.activation(var[:, 0:t], var[:, 0:t], ACT.Sqrt).then_inc(S["std_ready"], 1)

            act.dma_start(h[:, :, :], h_in).then_inc(S["h_landed"], 16)
            act.dma_start(vec[:, :], vec_in).then_inc(S["vec_landed"], 16)
            act.wait_ge(S["h_landed"], 16)
            norm(0, h, T0, lambda k: None)
            act.wait_ge(S["vec_landed"], 16)
            for j in range(8):
                act.wait_ge(S["pw1_done"], 2 * j + 2)
                if j >= 2:
                    act.wait_ge(S["glu_done"], j - 1)
                act.activation(gate_sb[:, j % 2, :], ps[:, 2 * (j % 3) + 1, 0:T0], ACT.Sigmoid,
                               bias=vcol("b_pw1", 8 + j)).then_inc(S["glu_sig"], 1)
            norm(1, conv_y, T0, lambda k: act.wait_ge(S["xc_ready"], k + 1))
            for k in range(KD):
                act.wait_ge(S["normed"], 8 * 1 + k + 1)
                act.activation(sq[:, k, :], conv_y[:, k, :], ACT.Silu, bias=vcol("ln_b", k)).then_inc(S["ln_silu"], 1)
            norm(2, h, T0, lambda k: act.wait_ge(S["h1_ready"], max(k + 1, 8)))

            def ffn(n, t):
                for p in range(KF):
                    act.wait_ge(S["ffn_gu"], n * 2 * KF + 2 * p + 2)
                    if p >= 2:
                        act.wait_ge(S["ffn_hid"], n * KF + p - 1)
                    act.activation(gate_sb[:, p % 2, 0:t], ps[:, 2 * (p % 3), 0:t], ACT.Silu).then_inc(S["ffn_sig"], 1)

            ffn(0, T0)
            norm(3, h, T0, lambda k: act.wait_ge(S["ffn_out"], k + 1))
            norm(4, x, SEQ, lambda k: act.wait_ge(S["x_ready"], 8))
            act.wait_ge(S["gap_ready"], 1)
            act.activation(gap[:, :, 1:2], gap[:, :, 0:1], ACT.Exp).then_inc(S["gap_exp"], 1)
            for t in range(2):
                act.wait_ge(S["xt_done"], t + 1)
                act.activation(x_tok[:, t, :].rearrange("p (b c) -> p b c", b=2), ps[:, 2 * t:2 * t + 2, :], ACT.Copy)\
                   .then_inc(S["xt_ready"], 1)
            act.wait_ge(S["table_ready"], 1)
            items = act.value_load(table[0:1, 16:17], min_val=NE, max_val=MAX_ITEMS)
            with act.Fori(0, items) as i:
                act.wait_ge(S["wt_done"], i + 1)
                act.activation(w_row[0:CAP, :], ps[0:CAP, 2, 0:SEQ], ACT.Copy).then_inc(S["wt_ready"], 1)
                for p in range(KE):
                    act.wait_ge(S["moe_gu"], i * (2 * KE) + (2 * p + 2))
                    if p >= 2:
                        act.wait_ge(S["moe_hid"], i * KE + (p - 1))
                    act.activation(gate_sb[:, p % 2, 0:CAP], ps[:, 2 * (p % 3), 0:CAP], ACT.Silu)\
                       .then_inc(S["moe_sig"], 1)
                for j in range(4):
                    act.wait_ge(S["moe_down"], i * 8 + (2 * j + 2))
                    b = 2 * (j % 3)
                    act.activation(y_item[:, 2 * j:2 * j + 2, :], ps[:, b:b + 2, 0:CAP], ACT.Copy)\
                       .then_inc(S["moe_y"], 1)
            norm(5, x, SEQ, lambda k: act.wait_ge(S["moe_all"], 1))
            norm(6, x, SEQ, lambda k: act.wait_ge(S["normed"], 8 * 5 + k + 1))
            for p in range(20):
                if taker2[p] != "act":
                    continue
                act.wait_ge(S["in2_done"], 2 * p + 2)
                b = 2 * (p % 3)
                act.activation(proj[:, 2 * p:2 * p + 2, :], ps[:, b:b + 2, 0:SEQ],
                               ACT.Silu if 2 * p < MG else ACT.Sigmoid).then_inc(S["in2_act"], 1)
            act.wait_ge(S["gl_done"], 1)
            act.activation(gates, ps[:, 6, 0:48], ACT.Sigmoid).then_inc(S["gates_ready"], 1)
            act.wait_ge(S["cmp_pe_ready"], 1)
            for kv in range(2):
                act.wait_ge(S["cmp_pe_ready"], kv + 1)
                for g in range(2):
                    act.activation(cmp_h[:, 2 * kv + g, 0:CMP_N], ps[:, 2 * kv + g, 0:CMP_N], ACT.Silu,
                                   bias=cmp_pe[:, kv:kv + 1]).then_inc(S["cmp_h_ready"], 1)

            def exps(s):
                j, kind, i, g, br = subs[s]
                act.wait_ge(S["s_ready"], s + 1)
                n = CMP_N if br == "cmp" else (i + 1) * P
                for p in range(4):
                    ins = act.activation(soft[:, s % 2, p, 0:n], soft[:, s % 2, p, 0:n], ACT.Exp,
                                         bias=stats[:, s % 2, 1, p:p + 1], accum_out=stats[:, s % 2, 2, p:p + 1])
                ins.then_inc(S["exp_ready"], 1)

            def copies(s):
                j, kind, i, g, br = subs[s]
                for kt in range(turns[s]):
                    u = turns_before[s] + kt
                    act.wait_ge(S["turn_done"], u + 1)
                    if j >= 1:
                        act.wait_ge(S["pv_done"], j)
                    rows_n = CMP_N if br == "cmp" else P
                    act.activation(probT[0:rows_n, prob_slot[br] + kt, :], ps[0:rows_n, 4 + u % 2, :], ACT.Copy)\
                       .then_inc(S["turned"], 1)

            exps(0)
            for s in range(len(subs)):
                if s + 1 < len(subs):
                    exps(s + 1)
                copies(s)
            norm(7, zo, SEQ, lambda k: act.wait_ge(S["wo2_ready"], k + 1))
            norm(8, x, SEQ, lambda k: act.wait_ge(S["normed"], 8 * 7 + k + 1))
            for p in range(19):
                if taker3[p] != "act":
                    continue
                act.wait_ge(S["in3_done"], 2 * p + 2)
                b = 2 * (p % 3)
                act.activation(proj[:, 2 * p:2 * p + 2, :], ps[:, b:b + 2, 0:SEQ],
                               ACT.Gelu_apprx_tanh if 2 * p == L_G else ACT.Sigmoid).then_inc(S["in3_act"], 1)
            act.wait_ge(S["conv3_ready"], 2)
            act.activation(qk3, qk3, ACT.Silu).then_inc(S["qk_silu"], 1)
            act.wait_ge(S["lru_g_done"], 1)
            for n, name in enumerate(("lru_ba", "lru_bx")):
                for t in range(2):
                    ins = act.activation(lru_t[:, n, t, :], ps[:, 4 + n, t * SEQ:(t + 1) * SEQ], ACT.Sigmoid,
                                         bias=vcol(name, t))
                ins.then_inc(S["lru_sig"], 1)
            step(act.activation(lam[:, 0, :], vcol("lru_lam", 0, 2), ACT.Abs))
            act.activation(lam[:, 1, :], lam[:, 0, :], ACT.Exp, scale=-1.0).then_inc(S["lam_exp"], 1)
            act.wait_ge(S["lru_loga"], 1)
            act.activation(lru_t[:, 3, :, :], lru_t[:, 2, :, :], ACT.Exp).then_inc(S["lru_a"], 1)
            act.wait_ge(S["lru_a"], 1)
            act.activation(lru_t[:, 2, :, :], lru_t[:, 2, :, :], ACT.Tanh).then_inc(S["lru_a"], 1)
            act.wait_ge(S["lru_f"], 1)
            act.activation(lru_t[:, 2, :, :], lru_t[:, 2, :, :], ACT.Sqrt, scale=-1.0).then_inc(S["lru_sqrt"], 1)
            act.wait_ge(S["gate_in"], 1)
            step(act.activation(arow, frow, ACT.Abs))
            step(act.activation(arow, arow, ACT.Exp, scale=-1.0))
            act.activation(arow, arow, ACT.Ln, bias=1.0).then_inc(S["gate_ln"], 1)
            for hd in range(4):
                act.wait_ge(S["sb_zs"], hd + 1)
                step(act.activation(sb_lk[:, hd, :], zs[:, hd, :], ACT.Abs))
                step(act.activation(sb_lk[:, hd, :], sb_lk[:, hd, :], ACT.Exp, scale=-1.0))
                act.activation(sb_lk[:, hd, :], sb_lk[:, hd, :], ACT.Ln, bias=1.0).then_inc(S["sb_ln"], 1)
            for hd in range(4):
                act.wait_ge(S["sb_arg"], hd + 1)
                act.activation(sb_w[:, hd, :], sb_w[:, hd, :], ACT.Exp).then_inc(S["sb_a"], 1)
            act.wait_ge(S["m_floor_in"], 1)
            act.activation(floor, floor, ACT.Exp).then_inc(S["m_floor"], 1)
            act.wait_ge(S["cT_ready"], 1)
            for hd in range(4):
                act.wait_ge(S["mb_ready"], hd + 1)
                act.activation(decay[:, hd, 0:SEQ], decay[:, hd, 0:SEQ], ACT.Exp, bias=ccol[:, hd:hd + 1])
                act.activation(decay[:, hd, SEQ:3 * P], decay[:, hd, SEQ:3 * P], ACT.Exp,
                               bias=ccol[:, 4 + hd:5 + hd]).then_inc(S["ml_exp"], 1)
            act.wait_ge(S["ml_nd_done"], 1)
            act.activation(lru_t[:, 0, :, :], ps[:, 7, :].rearrange("p (k t) -> p k t", k=2), ACT.Abs)\
               .then_inc(S["fl_ready"], 1)
            norm(9, x, SEQ, lambda k: act.wait_ge(S["x3_ready"], k + 1))
            ffn(1, SEQ)
            norm(10, x, SEQ, lambda k: act.wait_ge(S["ffn_out"], 8 + k + 1))

        @block.vector
        def _(dve):
            steps = [0]

            def step(ins):
                steps[0] += 1
                ins.then_inc(S["dve_step"], 1)
                dve.wait_ge(S["dve_step"], steps[0])

            def inverse_root(i, t, eps):
                dve.wait_ge(S["sum_done"], i + 1)
                dve.tensor_scalar(var[:, 0:t], ps[:, 7, 0:t], 1.0 / D, eps, ALU.mult, ALU.add)\
                   .then_inc(S["var_ready"], 1)
                dve.wait_ge(S["std_ready"], i + 1)
                step(dve.reciprocal(rstd[:, 0:t], var[:, 0:t]))

            def norm(i, src, dst, gain, t, eps=EPS):
                inverse_root(i, t, eps)
                for k in range(KD):
                    dve.scalar_tensor_tensor(out=dst[:, k, 0:t], in0=src[:, k, 0:t], scalar=vcol(gain, k),
                                             in1=rstd[:, 0:t], op0=ALU.mult, op1=ALU.mult).then_inc(S["normed"], 1)

            dve.wait_ge(S["consts_ready"], 1)
            dve.wait_ge(S["vec_landed"], 16)
            dve.wait_ge(S["h_landed"], 16)
            step(dve.memset(conv_u[:, :, 0:CONVW - 1], 0.0))
            norm(0, h, hn, "mix_g0", T0)

            def conv_dve(j):
                dve.wait_ge(S["glu_done"], j + 1)
                for tap in range(PE_TAPS, CONVW):
                    u = conv_u[:, j, tap:tap + T0]
                    w = vcol("w_dw", j * CONVW + tap)
                    if tap == PE_TAPS:
                        step(dve.tensor_scalar(conv_y[:, j, :], u, w, None, ALU.mult))
                    else:
                        step(dve.scalar_tensor_tensor(out=conv_y[:, j, :], in0=u, scalar=w, in1=conv_y[:, j, :],
                                                      op0=ALU.mult, op1=ALU.add))
                dve.wait_ge(S["conv_done"], j + 1)
                dve.scalar_tensor_tensor(out=conv_y[:, j, :], in0=ps[:, 6, 0:T0], scalar=vcol("b_dw", j),
                                         in1=conv_y[:, j, :], op0=ALU.add, op1=ALU.add).then_inc(S["conv_ready"], 1)

            for j in range(8):
                dve.wait_ge(S["glu_sig"], j + 1)
                dve.scalar_tensor_tensor(out=conv_u[:, j, CONVW - 1:CONVW - 1 + T0], in0=ps[:, 2 * (j % 3), 0:T0],
                                         scalar=vcol("b_pw1", j), in1=gate_sb[:, j % 2, :],
                                         op0=ALU.add, op1=ALU.mult).then_inc(S["glu_done"], 1)
                if j >= 1:
                    conv_dve(j - 1)
            conv_dve(7)
            dve.wait_ge(S["mean_done"], 1)
            step(dve.tensor_scalar(mean, ps[:, 7, 0:T0], 1.0 / D, None, ALU.mult))
            for k in range(KD):
                dve.tensor_tensor(conv_y[:, k, :], conv_y[:, k, :], mean, ALU.subtract).then_inc(S["xc_ready"], 1)
            norm(1, conv_y, conv_y, "ln_g", T0, LN_EPS)
            for m in range(KD):
                dve.wait_ge(S["pw2_done"], m + 1)
                b = 2 * (m // 2 % 3) + m % 2
                dve.scalar_tensor_tensor(out=h[:, m, :], in0=ps[:, b, 0:T0], scalar=vcol("b_pw2", m),
                                         in1=h[:, m, :], op0=ALU.add, op1=ALU.add).then_inc(S["h1_ready"], 1)

            def ffn(n, norm_i, res, gain, t, hidden):
                norm(norm_i, res, hn, gain, t)
                for p in range(KF):
                    dve.wait_ge(S["ffn_sig"], n * KF + p + 1)
                    dve.tensor_tensor(hidden[:, p, 0:t], ps[:, 2 * (p % 3) + 1, 0:t], gate_sb[:, p % 2, 0:t],
                                      ALU.mult).then_inc(S["ffn_hid"], 1)
                for m in range(KD):
                    dve.wait_ge(S["ffn_down"], 8 * n + m + 1)
                    b = 2 * (m // 2 % 3) + m % 2
                    dve.tensor_tensor(res[:, m, 0:t], ps[:, b, 0:t], res[:, m, 0:t], ALU.add)\
                       .then_inc(S["ffn_out"], 1)

            ffn(0, 2, h, "ffn_g0", T0, hid0)
            norm(3, h, hn, "mix_g1", T0)
            dve.wait_ge(S["normed"], 8 * 4)
            for g in range(4):
                src, width, at = hn[:, 2 * g:2 * g + 2, :], 1, 0
                if g:
                    dve.wait_ge(S["pooled"], g)
                for dst in (pool_a, pool_b, pool_a, pool_b)[:g + 1]:
                    at += width
                    step(dve.tensor_tensor(dst[:, :, at:T0], src[:, :, at:T0], src[:, :, at - width:T0 - width],
                                           ALU.add))
                    src, width = dst, 2 * width
                dve.scalar_tensor_tensor(out=sq256[:, 2 * g:2 * g + 2, :], in0=src[:, :, META:T0],
                                         scalar=1.0 / width, in1=hn[:, 2 * g:2 * g + 2, META:T0],
                                         op0=ALU.mult, op1=ALU.subtract).then_inc(S["pooled"], 1)
            for m in range(KD):
                dve.wait_ge(S["pool_done"], m + 1)
                b = 2 * (m // 2 % 3) + m % 2
                dve.scalar_tensor_tensor(out=x[:, m, :], in0=ps[:, b, 0:SEQ], scalar=vcol("pool_scale", m),
                                         in1=h[:, m, META:T0], op0=ALU.mult, op1=ALU.add).then_inc(S["x_ready"], 1)
            norm(4, x, hn, "ffn_g1", SEQ)
            dve.wait_ge(S["router_done"], 1)
            step(dve.tensor_copy(logit, ps[:, 6, 0:2 * NE].rearrange("p (t e) -> p t e", t=2)))
            for t in range(2):
                step(dve.max(top[:, t, :], logit[:, t, :]))
                step(dve.max_index(idx_u[:, t, :], top[:, t, :], logit[:, t, :]))
            step(dve.tensor_copy(top_i, idx_u[:, :, :]))
            dve.tensor_tensor(gap[:, :, 0:1], top[:, :, 1:2], top[:, :, 0:1], ALU.subtract)\
               .then_inc(S["gap_ready"], 1)
            dve.wait_ge(S["gap_exp"], 1)
            step(dve.tensor_scalar(gap[:, :, 2:3], gap[:, :, 1:2], 1.0, None, ALU.add))
            step(dve.reciprocal(gap[:, :, 3:4], gap[:, :, 2:3]))
            step(dve.tensor_tensor(gap[:, :, 4:5], gap[:, :, 3:4], gap[:, :, 1:2], ALU.mult))
            for t in range(2):
                dve.tensor_scalar(hot1[:, t, :], iota16[:, 0:NE], top_i[:, t, 0:1], None, ALU.is_equal)
                step(dve.tensor_scalar(hot2[:, t, :], iota16[:, 0:NE], top_i[:, t, 1:2], None, ALU.is_equal))
            dve.tensor_tensor(hot, hot1, hot2, ALU.add).then_inc(S["chosen"], 1)
            dve.wait_ge(S["ranks_done"], 1)
            count = small[:, 252:260]
            step(dve.tensor_copy(count, ps[:, 6, 32:40]))
            step(dve.tensor_scalar(over, count, float(CAP), 1.0, ALU.is_gt, ALU.add))
            for n in range(2, -(-SEQ // CAP)):
                step(dve.scalar_tensor_tensor(out=over, in0=count, scalar=float(n * CAP), in1=over,
                                              op0=ALU.is_gt, op1=ALU.add))
            step(dve.tensor_tensor_scan(ends, ones[:, 0:NE], over, 0.0, ALU.mult, ALU.add))
            step(dve.tensor_scalar(owner, iota16[:, :], ends[:, 0:1], None, ALU.is_ge))
            for e in range(1, NE):
                step(dve.scalar_tensor_tensor(out=owner, in0=iota16[:, :], scalar=ends[:, e:e + 1], in1=owner,
                                              op0=ALU.is_ge, op1=ALU.add))
            step(dve.tensor_copy(table[:, 0:16], owner))
            dve.tensor_copy(table[:, 16:17], ends[:, NE - 1:NE]).then_inc(S["table_ready"], 1)
            step(dve.tensor_tensor(begins, ends, over, ALU.subtract))
            step(dve.tensor_scalar(begins, begins, float(CAP), -1.0, ALU.mult, ALU.add))
            for t in range(2):
                ins = dve.tensor_tensor(place[:, t, :], ps[:, 6, 16 + 8 * t:24 + 8 * t], begins, ALU.add)
            step(ins)
            step(dve.tensor_tensor(hot1, hot1, place, ALU.mult))
            step(dve.tensor_tensor(hot2, hot2, place, ALU.mult))
            dve.tensor_reduce(at12[:, 0:2], hot1, AX.X, ALU.add)
            step(dve.tensor_reduce(at12[:, 2:4], hot2, AX.X, ALU.add))

            def picks():
                for t in range(2):
                    dve.tensor_scalar(pick2[:, t, :], iota_cap[:, :], at12[:, 2 + t:3 + t], None, ALU.is_equal)
                    dve.tensor_scalar(pick[:, t, :], iota_cap[:, :], at12[:, t:t + 1], None, ALU.is_equal)
                    dve.tensor_scalar(wpick2[:, t, :], iota_cap[:, :], at12[:, 2 + t:3 + t], gap[:, t, 4:5],
                                      ALU.is_equal, ALU.mult)
                    ins = dve.tensor_scalar(wpick[:, t, :], iota_cap[:, :], at12[:, t:t + 1], gap[:, t, 3:4],
                                            ALU.is_equal, ALU.mult)
                return ins

            def pick_sums():
                dve.tensor_tensor(pick, pick, pick2, ALU.add)
                return dve.tensor_tensor(wpick, wpick, wpick2, ALU.add)

            step(picks())
            pick_sums().then_inc(S["picks_ready"], 1)
            dve.memset(gap[:, :, 5:6], 0.0).then_inc(S["moe_out"], 1)
            items = dve.value_load(table[0:1, 16:17], min_val=NE, max_val=MAX_ITEMS)
            with dve.Fori(0, items) as i:
                dve.wait_ge(S["pick_done"], i + 1)
                dve.tensor_copy(x_item.rearrange("p (b k) c -> p b (k c)", b=2), ps[:, 0:2, 0:4 * CAP])\
                   .then_inc(S["pick_ready"], 1)
                dve.wait_ge(S["wt_done"], i + 1)
                dve.tensor_scalar(at12, at12, -float(CAP), None, ALU.add).then_inc(S["at_moved"], 1)
                dve.wait_ge(S["at_moved"], i + 1)
                picks().then_inc(S["picks_made"], 1)
                dve.wait_ge(S["picks_made"], i + 1)
                pick_sums().then_inc(S["picks_ready"], 1)
                for p in range(KE):
                    dve.wait_ge(S["moe_sig"], i * KE + (p + 1))
                    dve.tensor_tensor(hid_item[:, p, :], ps[:, 2 * (p % 3) + 1, 0:CAP], gate_sb[:, p % 2, 0:CAP],
                                      ALU.mult).then_inc(S["moe_hid"], 1)
                for n in range(2):
                    dve.wait_ge(S["moe_yt_done"], i * 2 + (n + 1))
                    dve.tensor_copy(y_tok[0:CAP, n * 512:(n + 1) * 512], ps[0:CAP, 6 + n, :]).then_inc(S["moe_yt"], 1)
                for n in range(4):
                    dve.wait_ge(S["moe_sum"], i * 4 + (n + 1))
                    dve.tensor_tensor(x[:, 2 * n:2 * n + 2, :], ps[:, n, :].rearrange("p (k t) -> p k t", k=2),
                                      x[:, 2 * n:2 * n + 2, :], ALU.add).then_inc(S["moe_out"], 1)
            dve.wait_ge(S["moe_out"], items * 4 + 1)
            dve.memset(gap[:, :, 5:6], 0.0).then_inc(S["moe_all"], 1)
            norm(5, x, x, "final_g", SEQ)
            norm(6, x, hn, "pre_g", SEQ)
            for p in range(23):
                if taker2[p] != "dve":
                    continue
                dve.wait_ge(S["in2_done"], 2 * p + 2)
                b = 2 * (p % 3)
                if p >= 20:
                    c = p - 20
                    ins = dve.tensor_copy(vtok[:, :, c * WIDE:(c + 1) * WIDE], ps[:, b:b + 2, 0:SEQ])
                elif QA <= 2 * p < KC or QB <= 2 * p < KB:
                    ins = dve.tensor_scalar(proj[:, 2 * p:2 * p + 2, :], ps[:, b:b + 2, 0:SEQ], 0.125, None, ALU.mult)
                else:
                    ins = dve.tensor_copy(proj[:, 2 * p:2 * p + 2, :], ps[:, b:b + 2, 0:SEQ])
                ins.then_inc(S["in2_dve"], 1)
            for kv in range(2):
                dve.wait_ge(S["cmp_h_done"], kv + 1)
                dve.tensor_copy(cmp_pe[:, kv:kv + 1], ps[:, 4 + kv, 0:1]).then_inc(S["cmp_pe_ready"], 1)
            dve.wait_ge(S["cmp_kv_done"], 1)
            dve.tensor_copy(cmp_k[:, 0:CMP_N], ps[:, 6, 64:64 + CMP_N]).then_inc(S["cmp_kv_ready"], 1)
            dve.tensor_copy(cmp_v[0:CMP_N, :], ps[0:CMP_N, 7, 0:P]).then_inc(S["cmp_kv_ready"], 1)
            dve.wait_ge(S["gates_ready"], 1)

            def biased(s):
                j, kind, i, g, br = subs[s]
                dve.wait_ge(S["score_done"], s + 1)
                if s >= 2:
                    dve.wait_ge(S["turn_done"], turns_before[s - 1])
                n = CMP_N if br == "cmp" else (i + 1) * P
                for p in range(4):
                    slope = moba_slope(4 * g + p) if kind == "moba" else nsa_slope(g, p)
                    bias = cbias[:, i, 0:CMP_N] if br == "cmp" else alibi[:, 2 * P - n:2 * P]
                    ins = dve.scalar_tensor_tensor(out=soft[:, s % 2, p, 0:n], in0=bias, scalar=slope,
                                                   in1=ps[:, 2 * (s % 2) + p % 2, (p // 2) * 256:(p // 2) * 256 + n],
                                                   op0=ALU.mult, op1=ALU.add)
                step(ins)
                step(dve.tensor_reduce(stats[:, s % 2, 0, :], soft[:, s % 2, :, 0:n], AX.X, ALU.max))
                dve.tensor_scalar(stats[:, s % 2, 1, :], stats[:, s % 2, 0, :], -1.0, 1.0e20, ALU.mult, ALU.min)\
                   .then_inc(S["s_ready"], 1)

            def scaled(s):
                j, kind, i, g, br = subs[s]
                dve.wait_ge(S["exp_ready"], s + 1)
                n = CMP_N if br == "cmp" else (i + 1) * P
                step(dve.tensor_scalar(stats[:, s % 2, 3, :], stats[:, s % 2, 2, :], 1.0e-30, None, ALU.max))
                step(dve.reciprocal(stats[:, s % 2, 3, :], stats[:, s % 2, 3, :]))
                if kind == "nsa":
                    col = i * 24 + ("cmp", "slc", "win").index(br) * 8 + g * 4
                    step(dve.tensor_tensor(stats[:, s % 2, 3, :], stats[:, s % 2, 3, :], gates[:, col:col + 4],
                                           ALU.mult))
                for p in range(4):
                    ins = dve.tensor_scalar(soft[:, s % 2, p, 0:n], soft[:, s % 2, p, 0:n],
                                            stats[:, s % 2, 3, p:p + 1], None, ALU.mult)
                ins.then_inc(S["prob_ready"], 1)

            def gated(j):
                kind, i, g = jobs[j]
                dve.wait_ge(S["pv_done"], j + 1)
                q = slice(i * P, (i + 1) * P)
                if kind == "nsa":
                    lo = 64 * g
                    ins = dve.tensor_tensor(sq256[lo:lo + 64, 0:4, q],
                                            ps[lo:lo + 64, 6 + j % 2, :].rearrange("p (a t) -> p a t", a=4),
                                            proj[lo:lo + 64, ZA:ZA + 4, q], ALU.mult)
                else:
                    ins = dve.tensor_tensor(sq256[:, 4 + 2 * g:6 + 2 * g, q],
                                            ps[:, 6 + j % 2, 0:2 * P].rearrange("p (a t) -> p a t", a=2),
                                            proj[:, ZB + 2 * g:ZB + 2 * g + 2, q], ALU.mult)
                ins.then_inc(S["y_ready"], 1)

            biased(0)
            for s in range(len(subs)):
                if s + 1 < len(subs):
                    biased(s + 1)
                scaled(s)
                if s >= 1 and subs[s][0] != subs[s - 1][0]:
                    gated(subs[s - 1][0])
            gated(len(jobs) - 1)
            for m in range(KD):
                j, half = m // 2, m % 2
                dve.wait_ge(S["br_done"], j + 1)
                if m >= 2:
                    dve.wait_ge(S["br_ready"], m - 1)
                for br in range(2):
                    ins = dve.tensor_tensor(part[:, m % 2, br, :], ps[:, 4 * (j % 2) + 2 * br + half, 0:SEQ],
                                            proj[:, MG + 8 * br + m, :], ALU.mult)
                ins.then_inc(S["br_part"], 1)
            for m in range(KD):
                dve.wait_ge(S["wo2_done"], m + 1)
                b = 2 * (m // 2 % 3) + m % 2
                dve.tensor_copy(zo[:, m, :], ps[:, b, 0:SEQ]).then_inc(S["wo2_ready"], 1)
            inverse_root(7, SEQ, EPS)
            for k in range(KD):
                ins = dve.scalar_tensor_tensor(out=zo[:, k, :], in0=zo[:, k, :], scalar=vcol("post_g", k),
                                               in1=rstd[:, 0:SEQ], op0=ALU.mult, op1=ALU.mult)
            step(ins)
            for k in range(KD):
                dve.tensor_tensor(x[:, k, :], x[:, k, :], zo[:, k, :], ALU.add).then_inc(S["normed"], 1)

            dve.memset(cpad, 0.0)
            norm(8, x, hn, "mix3_g", SEQ)

            def take3(p):
                dve.wait_ge(S["in3_done"], 2 * p + 2)
                b = 2 * (p % 3)
                if p >= 19:
                    ins = dve.tensor_copy(v3[:, :, (p - 19) * WIDE:(p - 18) * WIDE], ps[:, b:b + 2, 0:SEQ])
                elif 2 * p < L_G:
                    ins = dve.tensor_copy(cin[:, 2 * p:2 * p + 2, 3:3 + SEQ], ps[:, b:b + 2, 0:SEQ])
                elif 2 * p == S_Q:
                    ins = dve.tensor_scalar(proj[:, 2 * p:2 * p + 2, :], ps[:, b:b + 2, 0:SEQ], 0.125, None, ALU.mult)
                else:
                    ins = dve.tensor_copy(proj[:, 2 * p:2 * p + 2, :], ps[:, b:b + 2, 0:SEQ])
                ins.then_inc(S["in3_dve"], 1)

            def conv3(tiles, dst, done):
                for tap in range(4):
                    for n, j in enumerate(tiles):
                        u = cin[:, j, tap:tap + SEQ]
                        w = vcol("conv3", 4 * j + tap)
                        if tap == 0:
                            ins = dve.tensor_scalar(dst[:, n, :], u, w, None, ALU.mult)
                        else:
                            ins = dve.scalar_tensor_tensor(out=dst[:, n, :], in0=u, scalar=w, in1=dst[:, n, :],
                                                           op0=ALU.mult, op1=ALU.add)
                    if tap < 3:
                        step(ins)
                ins.then_inc(done, 1)

            for p in (0, 1, 2, 5, 6):
                take3(p)
            dve.wait_ge(S["in3_dve"], 3)
            conv3((0, 1), xa, S["conv3_ready"])
            conv3((2, 3, 4, 5), qk3, S["conv3_ready"])
            for p in (19, 20):
                take3(p)
            dve.wait_ge(S["lam_exp"], 1)
            e_, r_, r2, q_ = lam[:, 1, :], lam[:, 2, :], lam[:, 3, :], lam[:, 4, :]
            step(dve.tensor_scalar(r_, e_, 2.0, None, ALU.add))
            step(dve.reciprocal(r_, r_))
            step(dve.tensor_tensor(r_, r_, e_, ALU.mult))
            step(dve.tensor_tensor(r2, r_, r_, ALU.mult))
            step(dve.tensor_scalar(q_, r2, 1.0 / 17, None, ALU.mult))
            for odd in (15, 13, 11, 9, 7, 5, 3):
                step(dve.scalar_tensor_tensor(out=q_, in0=q_, scalar=1.0 / odd, in1=r2, op0=ALU.add, op1=ALU.mult))
            step(dve.scalar_tensor_tensor(out=q_, in0=q_, scalar=1.0, in1=r_, op0=ALU.add, op1=ALU.mult))
            step(dve.tensor_scalar(r_, vcol("lru_lam", 0, 2), -1.0, 0.0, ALU.mult, ALU.max))
            step(dve.scalar_tensor_tensor(out=q_, in0=q_, scalar=2.0, in1=r_, op0=ALU.mult, op1=ALU.add))
            step(dve.tensor_scalar(q_, q_, -8.0, None, ALU.mult))
            dve.wait_ge(S["lru_sig"], 2)
            for t in range(2):
                ins = dve.tensor_scalar(lru_t[:, 2, t, :], lru_t[:, 0, t, :], q_[:, t:t + 1], None, ALU.mult)
            ins.then_inc(S["lru_loga"], 1)
            dve.wait_ge(S["lru_a"], 2)
            step(dve.tensor_tensor(lru_t[:, 0, :, :], lru_t[:, 3, :, :], lru_t[:, 3, :, :], ALU.mult))
            dve.scalar_tensor_tensor(out=lru_t[:, 2, :, :], in0=lru_t[:, 0, :, :], scalar=1.0,
                                     in1=lru_t[:, 2, :, :], op0=ALU.add, op1=ALU.mult).then_inc(S["lru_f"], 1)
            dve.wait_ge(S["if_done"], 1)
            dve.wait_ge(S["in3_act"], taker3.count("act"))
            dve.tensor_scalar(irow, ps[0:4, 6, 0:SEQ], vcol("ig_b", rows=4), None, ALU.add)
            dve.tensor_scalar(frow, ps[0:4, 6, SEQ:2 * SEQ], vcol("fg_b", rows=4), None, ALU.add)\
               .then_inc(S["gate_in"], 1)
            step(dve.tensor_tensor(lru_t[:, 1, :, :], lru_t[:, 1, :, :], xa, ALU.mult))
            dve.wait_ge(S["lru_sqrt"], 1)
            step(dve.tensor_tensor(lru_t[:, 1, :, :], lru_t[:, 1, :, :], lru_t[:, 2, :, :], ALU.mult))
            for t in range(2):
                ins = dve.tensor_tensor_scan(lru_t[:, 0, t, :], lru_t[:, 3, t, :], lru_t[:, 1, t, :], 0.0,
                                             ALU.mult, ALU.add)
            step(ins)
            dve.tensor_tensor(y3[:, 0:2, :], lru_t[:, 0, :, :], proj[:, L_G:L_G + 2, :], ALU.mult)\
               .then_inc(S["lru_in"], 1)
            for hd in range(4):
                dve.wait_ge(S["sb_z_done"], hd + 1)
                dve.tensor_tensor(zs[:, hd, :], ps[:, hd, 0:3 * P], smask[:, :], ALU.add).then_inc(S["sb_zs"], 1)
            dve.wait_ge(S["gate_ln"], 1)
            step(dve.scalar_tensor_tensor(out=frow, in0=frow, scalar=0.0, in1=arow, op0=ALU.min, op1=ALU.subtract))
            step(dve.tensor_tensor_scan(brow, ones[0:4, :], frow, 0.0, ALU.mult, ALU.add))
            dve.tensor_tensor(crow, irow, brow, ALU.subtract).then_inc(S["c_ready"], 1)
            dve.wait_ge(S["c_ready"], 1)
            step(dve.tensor_tensor_scan(mrow, crow, crow, 0.0, ALU.max, ALU.max))
            step(dve.tensor_scalar(mrow, mrow, -1.0, None, ALU.mult))
            dve.tensor_tensor(floor, mrow, brow, ALU.subtract).then_inc(S["m_floor_in"], 1)
            dve.wait_ge(S["cT_done"], 1)
            dve.tensor_copy(ccol, ps[:, 7, 0:8]).then_inc(S["cT_ready"], 1)
            for hd in range(4):
                dve.wait_ge(S["sb_ln"], hd + 1)
                dve.scalar_tensor_tensor(out=sb_lk[:, hd, :], in0=zs[:, hd, :], scalar=0.0, in1=sb_lk[:, hd, :],
                                         op0=ALU.max, op1=ALU.add).then_inc(S["sb_lk"], 1)
            for hd in range(4):
                dve.wait_ge(S["sb_r_done"], hd + 1)
                dve.tensor_tensor(sb_w[:, hd, :], zs[:, hd, :], ps[:, hd, 0:3 * P], ALU.subtract)\
                   .then_inc(S["sb_arg"], 1)
            dve.wait_ge(S["mb_done"], 1)
            dve.wait_ge(S["sb_arg"], 4)
            for hd in range(4):
                nm = ps[:, hd // 2, (hd % 2) * SEQ:(hd % 2 + 1) * SEQ]
                dve.tensor_tensor(decay[:, hd, 0:SEQ], nm, tmask[:, 0:SEQ], ALU.add)
                dve.tensor_tensor(decay[:, hd, SEQ:3 * P], nm[:, P:SEQ], tmask[:, SEQ:3 * P], ALU.add)\
                   .then_inc(S["mb_ready"], 1)
            dve.wait_ge(S["sb_o_done"], 1)
            dve.tensor_copy(y3[:, 4:6, :], ps[:, 4, :].rearrange("p (k t) -> p k t", k=2)).then_inc(S["sb_y"], 1)
            for hd in range(4):
                dve.wait_ge(S["ml_exp"], hd + 1)
                dve.wait_ge(S["ml_s_done"], hd + 1)
                dve.scalar_tensor_tensor(out=sb_w[:, hd, :], in0=decay[:, hd, :], scalar=0.125,
                                         in1=ps[:, hd, 0:3 * P], op0=ALU.mult, op1=ALU.mult).then_inc(S["ml_p"], 1)
            dve.wait_ge(S["fl_ready"], 1)
            dve.wait_ge(S["fl_done"], 1)
            den = lru_t[:, 0, :, :]
            step(dve.tensor_tensor(den, ps[:, 5, :].rearrange("p (k t) -> p k t", k=2), den, ALU.max))
            step(dve.reciprocal(den, den))
            step(dve.tensor_tensor(den, ps[:, 6, :].rearrange("p (k t) -> p k t", k=2), den, ALU.mult))
            dve.tensor_tensor(y3[:, 2:4, :], den, proj[:, M_O:M_O + 2, :], ALU.mult).then_inc(S["mh_ready"], 1)
            dve.wait_ge(S["mh_ready"], 1)
            for m in range(KD):
                j, half = m // 2, m % 2
                dve.wait_ge(S["out3_done"], j + 1)
                if m >= 2:
                    dve.wait_ge(S["merged"], m - 1)
                for br in range(3):
                    ins = dve.tensor_tensor(part3[:, m % 2, br, :], ps[:, 3 * half + br, 0:SEQ],
                                            proj[:, G3 + 8 * br + m, :], ALU.mult)
                ins.then_inc(S["out3_part"], 1)
            for m in range(KD):
                dve.wait_ge(S["wo3_done"], m + 1)
                b = 2 * (m // 2 % 3) + m % 2
                dve.tensor_tensor(x[:, m, :], ps[:, b, 0:SEQ], x[:, m, :], ALU.add).then_inc(S["x3_ready"], 1)
            ffn(1, 9, x, "ffn3_g", SEQ, hid)
            norm(10, x, hn, "final3_g", SEQ)

        @block.gpsimd
        def _(pool):
            steps = [0]

            def step(ins):
                steps[0] += 1
                ins.then_inc(S["pool_step"], 1)
                pool.wait_ge(S["pool_step"], steps[0])

            step(pool.memset(ones[:, :], 1.0))
            step(pool.memset(ident[:, :], 0.0))
            step(pool.affine_select(out=ident[:, :], in_=ident[:, :], compare_op=ALU.not_equal, fill=1.0,
                                    base=0, pattern=[[-1, P]], channel_multiplier=1))
            step(pool.affine_select(out=tri[:, :], in_=ones[:, 0:P], compare_op=ALU.is_ge, fill=0.0,
                                    base=0, pattern=[[-1, P]], channel_multiplier=1))
            step(pool.memset(sel[:, :, :], 0.0))
            step(pool.affine_select(out=sel[:, :, :], in_=sel[:, :, :], compare_op=ALU.not_equal, fill=1.0,
                                    base=0, pattern=[[-1, 4], [0, P]], channel_multiplier=1))
            step(pool.iota(alibi[:, :], pattern=[[1, 2 * P]], base=-P, channel_multiplier=-1,
                           allow_small_or_imprecise_dtypes=True))
            step(pool.affine_select(out=alibi[:, :], in_=alibi[:, :], compare_op=ALU.is_ge, fill=NEG,
                                    base=P, pattern=[[-1, 2 * P]], channel_multiplier=1))
            for i in range(2):
                step(pool.iota(cbias[:, i, :], pattern=[[16, 16]], base=31 - i * P, channel_multiplier=-1,
                               allow_small_or_imprecise_dtypes=True))
                step(pool.affine_select(out=cbias[:, i, :], in_=cbias[:, i, :], compare_op=ALU.is_ge, fill=NEG,
                                        base=i * P - 31, pattern=[[-16, 16]], channel_multiplier=1))
            step(pool.memset(tmask[:, :], 0.0))
            step(pool.memset(smask[:, :], 0.0))
            for m, base in ((tmask, 0), (smask, -1)):
                for lo, hi in ((0, 2 * P), (2 * P, 3 * P)):
                    step(pool.affine_select(out=m[:, lo:hi], in_=m[:, lo:hi], compare_op=ALU.is_ge, fill=NEG,
                                            base=base, pattern=[[1, hi - lo]], channel_multiplier=-1))
            step(pool.affine_select(out=upto[:, :], in_=ones[:, 0:P], compare_op=ALU.is_ge, fill=0.0,
                                    base=0, pattern=[[1, P]], channel_multiplier=-1))
            step(pool.iota(iota_cap[:, :], pattern=[[1, CAP]], base=0, channel_multiplier=0,
                           allow_small_or_imprecise_dtypes=True))
            pool.iota(iota16[:, :], pattern=[[1, 16]], base=0, channel_multiplier=0,
                      allow_small_or_imprecise_dtypes=True).then_inc(S["consts_ready"], 1)
            pool.wait_ge(S["vec_landed"], 16)
            for j in range(8):
                if j >= 2:
                    pool.wait_ge(S["conv_done"], j - 1)
                for tap in range(PE_TAPS):
                    pool.tensor_scalar(diag[:, j % 2, tap, :], ident[:, :], vcol("w_dw", j * CONVW + tap), None,
                                       ALU.mult).then_inc(S["diag_ready"], 1)
            for m in range(KD):
                pool.wait_ge(S["br_part"], m + 1)
                pool.tensor_tensor(hn256[:, m, :], part[:, m % 2, 0, :], part[:, m % 2, 1, :], ALU.add)\
                    .then_inc(S["br_ready"], 1)
            for m in range(KD):
                pool.wait_ge(S["out3_part"], m + 1)
                step(pool.tensor_tensor(part3[:, m % 2, 0, :], part3[:, m % 2, 0, :], part3[:, m % 2, 1, :], ALU.add))
                pool.tensor_tensor(hn256[:, m, :], part3[:, m % 2, 0, :], part3[:, m % 2, 2, :], ALU.add)\
                    .then_inc(S["merged"], 1)


def _kernel_arrays(i):
    def blocks(w):
        k, n = w.shape
        return w.reshape(k // P, P, n // WIDE, WIDE).transpose(2, 0, 1, 3).reshape(-1, P, WIDE)

    def beside(a, b):
        k, n = a.shape
        return np.stack([a.reshape(k, n // P, P), b.reshape(k, n // P, P)], 2).reshape(k, 2 * n)

    def by_group(w, axis):
        s = w.shape
        if axis == 1:
            return w.reshape(s[0], 2, 4, 64).transpose(0, 2, 1, 3).reshape(s)
        return w.reshape(2, 4, 64, s[1]).transpose(1, 0, 2, 3).reshape(s)

    def interleave(ws):
        bs = [blocks(w).reshape(4, -1, P, WIDE) for w in ws]
        return np.concatenate(bs, 1).reshape(-1, P, WIDE)

    a = {n: np.asarray(v) for n, v in i.items()}
    parts = [
        blocks(beside(a["conv_w_pw1"][0][:, :D], a["conv_w_pw1"][0][:, D:])),
        blocks(a["conv_w_pw2"][0]),
        blocks(beside(a["ffn_w_gate"][0], a["ffn_w_up"][0])),
        blocks(a["ffn_w_down"][0]),
        a["pool_w_group"][0].reshape(8, P, WIDE),
        np.zeros((4, P, WIDE), np.float32),
    ]
    for e in range(NE):
        parts += [blocks(beside(a["moe_w_gate"][0, e], a["moe_w_up"][0, e])), blocks(a["moe_w_down"][0, e])]
    w = a["w_in_2"][0]
    q_a, kv, g_a, z_a, qkv_b, z_b, merge = np.split(w, np.cumsum([512, 768, 24, 512, 1536, 512]), 1)
    kv = np.split(kv, 6, 1)
    parts.append(blocks(np.concatenate(
        [by_group(q_a, 1), kv[0], kv[1], kv[2], kv[4], by_group(z_a, 1), qkv_b[:, 0:1024], z_b, merge,
         kv[3], kv[5], qkv_b[:, 1024:1536]], 1)))
    for n in ("cmp_w1_k_2", "cmp_w1_v_2"):
        w1 = a[n][0].reshape(16, 2, 64, P).transpose(0, 2, 1, 3).reshape(16, 64, WIDE)
        parts.append(np.concatenate([w1, w1], 1))
    parts.append(interleave([by_group(a["w_branch_a_2"][0], 0), a["w_branch_b_2"][0]]))
    parts.append(blocks(a["w_o_2"][0]))
    w = a["w_in_3"][0]
    l_x, l_g, m_qk, m_v, m_o, m_if, s_qk, s_v, g3 = np.split(
        w, np.cumsum([256, 256, 512, 256, 256, 8, 512, 256]), 1)
    parts.append(blocks(np.concatenate([l_x, m_qk, l_g, m_o, s_qk, g3, m_v, s_v], 1)))
    parts.append(interleave([a["w_out_lru_3"][0], a["w_out_mlstm_3"][0], a["w_out_sb_3"][0]]))
    parts.append(blocks(a["w_o_3"][0]))
    parts.append(blocks(beside(a["w_ffn_in_3"][0][:, :FF], a["w_ffn_in_3"][0][:, FF:])))
    parts.append(blocks(a["w_ffn_out_3"][0]))
    stream = np.zeros((NCH, P, CH, WIDE), np.float32)
    at = 0
    for p in parts:
        done = 0
        while done < len(p):
            c, o = (at + done) // CH, (at + done) % CH
            if o == 0 and len(p) - done >= CH:
                n = (len(p) - done) // CH
                stream[c:c + n] = p[done:done + n * CH].reshape(n, CH, P, WIDE).transpose(0, 2, 1, 3)
                done += n * CH
            else:
                n = min(CH - o, len(p) - done)
                stream[c, :, o:o + n] = p[done:done + n].transpose(1, 0, 2)
                done += n
        at += len(p)
    assert at == NBLK

    def cols(v):
        return v.reshape(-1, P).T

    def taps(w):
        return w.reshape(w.shape[0], -1, P).transpose(2, 1, 0).reshape(P, -1)

    def tall(v):
        o = np.zeros((P, v.shape[1]), np.float32)
        o[:v.shape[0]] = v
        return o

    def rows(w):
        return w.reshape(-1, P, w.shape[1]).transpose(1, 0, 2).reshape(P, -1)

    def twice(v):
        return np.concatenate([v, v], 0)

    vecs = {
        "b_pw1": cols(a["conv_b_pw1"][0]), "w_dw": taps(a["conv_w_dw"][0]), "b_dw": cols(a["conv_b_dw"][0]),
        "ln_g": cols(a["conv_ln_g"][0]), "ln_b": cols(a["conv_ln_b"][0]), "b_pw2": cols(a["conv_b_pw2"][0]),
        "pool_scale": cols(a["pool_scale"][0]), "mix_g0": cols(a["mix_norm_g"][0]), "mix_g1": cols(a["mix_norm_g"][1]),
        "ffn_g0": cols(a["ffn_norm_g"][0]), "ffn_g1": cols(a["ffn_norm_g"][1]), "final_g": cols(a["final_norm_g"]),
        "pre_g": cols(a["norm_pre_2"][0]), "post_g": cols(a["norm_post_2"][0]), "mix3_g": cols(a["norm_mix_g_3"][0]),
        "ffn3_g": cols(a["norm_ffn_g_3"][0]), "final3_g": cols(a["final_norm_g_3"]),
        "conv3": np.concatenate([taps(a["conv_lru_w_3"][0]), taps(a["conv_mlstm_w_3"][0])], 1),
        "lru_ba": cols(a["lru_ba_3"][0]), "lru_bx": cols(a["lru_bx_3"][0]), "lru_lam": cols(a["lru_lambda_3"][0]),
        "ig_b": tall(a["mlstm_ig_b_3"][0][:, None]), "fg_b": tall(a["mlstm_fg_b_3"][0][:, None]),
        "router": rows(a["moe_w_router"][0]), "w_gates": rows(g_a), "w_if": rows(m_if),
        "w2k": a["cmp_w2_k_2"][0], "w2v": a["cmp_w2_v_2"][0],
        "pek": twice(a["cmp_pe_k_2"][0].T), "pev": twice(a["cmp_pe_v_2"][0].T),
        "lru_wa": rows(a["lru_wa_3"][0].reshape(256, 64)), "lru_wx": rows(a["lru_wx_3"][0].reshape(256, 64)),
    }
    vec = np.concatenate([vecs[n] for n, _ in VECS], 1)
    assert vec.shape == (P, NV)
    h0 = np.concatenate([a["meta_tokens"], a["x"][0]], 0)
    h0 = h0.T.reshape(KD, P, T0).transpose(1, 0, 2)
    return {"w_stream": stream.reshape(NCH, P, CH * WIDE), "vec_in": np.ascontiguousarray(vec),
            "h_in": np.ascontiguousarray(h0)}


def kernel(**inputs):
    import concourse.bacc as _bacc
    from concourse.bass_utils import run_bass_kernel_spmd as _run

    arrays = _kernel_arrays(inputs)
    nc = _bacc.Bacc("TRN2", target_bir_lowering=False, num_devices=1)
    aps = [nc.dram_tensor(n, v.shape, F32, kind="ExternalInput").ap() for n, v in arrays.items()]
    out = nc.dram_tensor("out", (P, KD, SEQ), F32, kind="ExternalOutput").ap()
    program(nc, *aps, out)
    r = _run(nc, [arrays], core_ids=[0])
    got = np.asarray(r.results[0]["out"])
    return np.ascontiguousarray(got.transpose(2, 1, 0).reshape(1, SEQ, D))
```

```python
from contextlib import ExitStack

import numpy as np
import concourse.bass as bass
from concourse import mybir

F32 = mybir.dt.float32
F32R = mybir.dt.float32r
U32 = mybir.dt.uint32
I32 = mybir.dt.int32
ALU = mybir.AluOpType
ACT = mybir.ActivationFunctionType
AX = mybir.AxisListType

P = 128
D = 1024
KD = D // P
META = 16
SEQ = 256
T0 = META + SEQ
CONVW = 31
FF = 2816
KF = FF // P
E_FF = 3584
KE = E_FF // P
NE = 8
CAP = 80
MAX_ITEMS = NE + 2 * SEQ // CAP
WIDE = 256
CH = 6
RING = 8
HIGH = 6
LOOK = 3
PE_TAPS = 15
NEG = -1.0e30
EPS = 1e-6
LN_EPS = 1e-5
CMP_N = 15

VECS = [
    ("b_pw1", 16), ("w_dw", KD * CONVW), ("b_dw", 8), ("ln_g", 8), ("ln_b", 8), ("b_pw2", 8),
    ("pool_scale", 8), ("mix_g0", 8), ("mix_g1", 8), ("ffn_g0", 8), ("ffn_g1", 8), ("final_g", 8),
    ("pre_g", 8), ("post_g", 8), ("mix3_g", 8), ("ffn3_g", 8), ("final3_g", 8),
    ("conv3", 6 * 4), ("lru_ba", 2), ("lru_bx", 2), ("lru_lam", 2), ("ig_b", 1), ("fg_b", 1),
    ("router", KD * NE), ("w_gates", KD * 24), ("w_if", KD * 8), ("w2k", 64), ("w2v", 64),
    ("pek", 16), ("pev", 16), ("lru_wa", 2 * 64), ("lru_wx", 2 * 64),
]
VOFF = {}
NV = 0
for _name, _n in VECS:
    VOFF[_name] = NV
    NV += _n

STAGES = [
    ("pw1", 8 * KD), ("pw2", 4 * KD), ("ffn0_in", KF * KD), ("ffn0_out", 4 * KF), ("pool", 8), ("pad", 4),
    ("moe", NE * (KE * KD + 4 * KE)),
    ("w_in2", 24 * KD), ("cmp", 16), ("branch", 4 * KD), ("w_o2", 4 * KD),
    ("w_in3", 21 * KD), ("outs3", 4 * 6), ("w_o3", 4 * KD), ("ffn3_in", KF * KD), ("ffn3_out", 4 * KF),
]
BOFF = {}
NBLK = 0
for _name, _n in STAGES:
    BOFF[_name] = NBLK
    NBLK += _n
assert BOFF["moe"] % CH == 0
MOE_BLK = KE * KD + 4 * KE
MOE_CH = MOE_BLK // CH
assert MOE_BLK % CH == 0 and MOE_CH % RING == 0
C_MOE = BOFF["moe"] // CH
C_POST = C_MOE + NE * MOE_CH
MOE_DOWN = KE * KD
MOE_SPLIT = list(range(MOE_DOWN // CH, MOE_CH))
AHEAD = RING - 1
N_POST = -(-(-(-NBLK // CH) - C_POST - AHEAD) // RING) * RING + AHEAD
NCH = C_POST + N_POST
SPLIT = {}
for _name, _n in STAGES:
    if _name in ("pw1", "pw2", "ffn0_in", "ffn0_out", "w_in2", "w_in3", "ffn3_in", "ffn3_out"):
        for _b in range(BOFF[_name], BOFF[_name] + _n):
            _lo = SPLIT.get(_b // CH, (_b % CH,))[0]
            SPLIT[_b // CH] = (_lo, _b % CH + 1)
SPLIT_CHUNKS = sorted(SPLIT)


def nsa_slope(g, p):
    return float(np.float32(2.0 ** (-8.0 * (2 * (4 * g + p) + 1) / 16)))


def moba_slope(h):
    return float(np.float32(2.0 ** (-8.0 * (2 * h + 2) / 16)))


def program(nc, w_stream, vec_in, h_in, out):
    with ExitStack() as ctx:
        def sb(name, shape, dt=F32):
            return ctx.enter_context(nc.sbuf_tensor(name, shape, dt))

        def sb_two(name, shape):
            with nc.sbuf_tensor(name + "_r", shape, F32R) as rounded:
                pass
            return sb(name, shape), rounded

        def sem(name):
            return ctx.enter_context(nc.semaphore(name))

        ps = ctx.enter_context(nc.psum_tensor("ps", [P, 8, 512], F32))
        ring, ring_r = sb_two("ring", [P, RING, CH * WIDE])
        high = sb("high", [P, HIGH, CH * WIDE], F32R)
        vec = sb("vec", [P, NV])
        h = sb("h", [P, KD, T0])
        x = sb("x", [P, KD, SEQ])
        hn, hn_r = sb_two("hn", [P, KD, T0])
        sq, sq_r = sb_two("sq", [P, KD, T0])
        big, big_r = sb_two("big", [P, 12032])
        scr, scr_r = sb_two("scr", [P, 5120])
        gate_sb = sb("gate_sb", [P, 2, T0])
        up_sb = sb("up_sb", [P, 2, SEQ])
        var = sb("var", [P, T0])
        rstd = sb("rstd", [P, T0])
        ident = sb("ident", [P, P])
        ones = sb("ones", [P, 2 * P])
        tri = sb("tri", [P, P])
        sel = sb("sel", [4, 4, P])
        alibi = sb("alibi", [P, 2 * P])
        cbias = sb("cbias", [P, 2, 16])
        tmask = sb("tmask", [P, 3 * P])
        smask = sb("smask", [P, 3 * P])
        small = sb("small", [P, 512])
        idx_u = sb("idx_u", [P, 2, 8], U32)
        table = sb("table", [P, 17], I32)
        upto = sb("upto", [P, P])
        iota_cap = sb("iota_cap", [P, CAP])
        iota16 = sb("iota16", [P, 16])

        def vcol(name, j=0, n=1, rows=P):
            return vec[0:rows, VOFF[name] + j:VOFF[name] + j + n]

        conv_u = big[:, 0:KD * 302].rearrange("p (k t) -> p k t", k=KD)
        conv_y = big[:, 2432:2432 + KD * T0].rearrange("p (k t) -> p k t", k=KD)
        diag = big[:, 4608:4608 + 2 * PE_TAPS * P].rearrange("p (b t c) -> p b t c", b=2, c=P)
        pool_a = big[:, 6000:6000 + 2 * T0].rearrange("p (k t) -> p k t", k=2)
        pool_b = big[:, 6600:6600 + 2 * T0].rearrange("p (k t) -> p k t", k=2)
        x_tok = big[:, 2560:2560 + 2 * D].rearrange("p (t d) -> p t d", t=2)
        x_item = big[:, 4608:4608 + KD * CAP].rearrange("p (k c) -> p k c", k=KD)
        y_tok = big[:, 5888:5888 + D]
        hid_item_high = big_r[:, 0:KE * CAP].rearrange("p (k c) -> p k c", k=KE)
        hid_item_low = big_r[:, 7808:7808 + KE * CAP].rearrange("p (k c) -> p k c", k=KE)
        pick = big[:, 6912:6912 + 2 * CAP].rearrange("p (t c) -> p t c", t=2)
        pick2 = big[:, 7072:7072 + 2 * CAP].rearrange("p (t c) -> p t c", t=2)
        wpick = big[:, 7232:7232 + 2 * CAP].rearrange("p (t c) -> p t c", t=2)
        wpick2 = big[:, 7392:7392 + 2 * CAP].rearrange("p (t c) -> p t c", t=2)
        w_row = big[:, 7552:7552 + SEQ]
        proj = big[:, 0:40 * SEQ].rearrange("p (k t) -> p k t", k=40)
        vtok = big[:, 10240:10240 + 1536].rearrange("p (t c) -> p t c", t=2)
        in_high = sq_r
        in_low0 = scr_r[:, 0:KD * T0].rearrange("p (k t) -> p k t", k=KD)
        in_low = scr_r[:, 3072:3072 + KD * SEQ].rearrange("p (k t) -> p k t", k=KD)
        hid_high0, hid_low0 = (big_r[:, n * KF * T0:(n + 1) * KF * T0].rearrange("p (k t) -> p k t", k=KF)
                               for n in range(2))
        hid_high, hid_low = (big_r[:, n * KF * SEQ:(n + 1) * KF * SEQ].rearrange("p (k t) -> p k t", k=KF)
                             for n in range(2))
        mean = gate_sb[:, 0, :]
        zo = proj[:, 0:8, :]
        sq256 = sq[:, :, 0:SEQ]
        hn256 = hn[:, :, 0:SEQ]
        soft = scr[:, 0:3072].rearrange("p (b a k) -> p b a k", b=3, a=4)

        def probs_turned(slot):
            if slot == 4:
                return up_sb[:, :, :].rearrange("p a c -> p (a c)")
            return scr[:, 3072 + slot * 512:3072 + (slot + 1) * 512]

        windows = h[:, :, :].rearrange("p k t -> p (k t)")[:, 0:6 * SEQ].rearrange("p (v g t) -> p v g t", v=2, g=3)
        part = scr[:, 0:1536].rearrange("p (b n k) -> p b n k", b=2, n=3)
        logit = small[:, 0:16].rearrange("p (t e) -> p t e", t=2)
        top = small[:, 16:32].rearrange("p (t e) -> p t e", t=2)
        top_i = small[:, 32:48].rearrange("p (t e) -> p t e", t=2)
        gap = small[:, 48:64].rearrange("p (t e) -> p t e", t=2)
        hot1 = small[:, 64:80].rearrange("p (t e) -> p t e", t=2)
        hot2 = small[:, 80:96].rearrange("p (t e) -> p t e", t=2)
        hot = small[:, 96:112].rearrange("p (t e) -> p t e", t=2)
        place = small[:, 112:128].rearrange("p (t e) -> p t e", t=2)
        over = small[:, 208:216]
        ends = small[:, 216:224]
        begins = small[:, 224:232]
        owner = small[:, 232:248]
        at12 = small[:, 248:252]
        cmp_h = small[:, 128:192].rearrange("p (n c) -> p n c", n=4)
        cmp_k = small[:, 192:208]
        cmp_v = small[:, 256:384]
        gates = small[:, 384:432]
        stats = small[:, 432:480].rearrange("p (b n c) -> p b n c", b=3, n=4)
        ccol = small[:, 464:472]
        lam = small[:, 472:488].rearrange("p (n c) -> p n c", n=8)
        cmp_pe = small[:, 488:490]
        v3 = big[:, 10240:10240 + 1024].rearrange("p (t c) -> p t c", t=2)
        crow, mrow, floor = (big[0:4, 11264 + 256 * n:11520 + 256 * n] for n in range(3))
        irow, frow = (big[0:4, 9728 + 256 * n:9984 + 256 * n] for n in range(2))
        arow, brow = up_sb[0:4, 0, :], up_sb[0:4, 1, :]
        hflat = h[:, :, :].rearrange("p k t -> p (k t)")
        cin = hflat[:, 0:6 * 259].rearrange("p (k t) -> p k t", k=6)
        cpad = cin[:, :, 0:3]
        sb_lk = big[:, 0:1536].rearrange("p (h c) -> p h c", h=4)
        sb_w = sq[:, :, :].rearrange("p k t -> p (k t)")[:, 0:1536].rearrange("p (h c) -> p h c", h=4)
        zs = hn[:, :, :].rearrange("p k t -> p (k t)")[:, 0:1536].rearrange("p (h c) -> p h c", h=4)
        decay = zs
        xa = scr[:, 0:512].rearrange("p (k t) -> p k t", k=2)
        qk3 = scr[:, 512:1536].rearrange("p (k t) -> p k t", k=4)
        y3 = scr[:, 1536:3072].rearrange("p (k t) -> p k t", k=6)
        lru_t = scr[:, 3072:5120].rearrange("p (n k t) -> p n k t", n=4, k=2)
        part3 = scr[:, 3072:3072 + 1536].rearrange("p (b n k) -> p b n k", b=2, n=3)

        dense_landed = [sem(f"dense_landed{s}") for s in range(RING)]
        moe_landed = [sem(f"moe_landed{s}") for s in range(RING)]
        pre_begun, moe_begun, post_begun = sem("pre_begun"), sem("moe_begun"), sem("post_begun")
        S = {}
        for n in """ones_ready weights_high weights_low input_high input_low ffn_mul vec_landed h_landed consts_ready pool_step dve_step act_step
                    sq_ready sum_done var_ready std_ready normed
                    pw1_done glu_sig glu_done diag_ready conv_done conv_ready mean_done xc_ready 
                    ln_silu pw2_done h1_ready ffn_gu ffn_sig ffn_hid ffn_down ffn_out
                    pooled pool_done x_ready router_done gap_ready gap_exp chosen ranks_done table_ready
                    xt_done xt_ready at_moved picks_made picks_ready pick_done pick_ready wt_done wt_ready
                    moe_gu moe_sig moe_mul moe_hid_high moe_hid moe_high moe_low moe_down moe_y moe_sum moe_out moe_all
                    in2_done in2_act in2_dve gl_done gates_ready cmp_h_done cmp_pe_ready cmp_h_ready cmp_kv_done
                    cmp_kv_ready score_done s_ready exp_ready prob_ready turn_done turned pv_done y_ready
                    br_done br_part br_ready wo2_done wo2_ready
                    in3_done in3_act in3_dve if_done conv3_ready qk_silu lru_g_done lru_sig lam_exp 
                    lru_loga lru_a lru_f lru_sqrt  lru_in 
                    gate_in gate_ln c_ready cT_done cT_ready m_floor_in m_floor mb_done mb_ready ml_s_done ml_exp
                    ml_p ml_nd_done fl_done fl_ready mh_ready
                    sb_z_done sb_zs sb_ln sb_lk sb_r_done sb_arg sb_a sb_o_done sb_y
                    out3_done out3_part merged wo3_done x3_ready out_done""".split():
            S[n] = sem(n)

        block = ctx.enter_context(nc.Block())

        jobs = [("nsa", i, g) for i in range(2) for g in range(2)] + \
               [("moba", i, hh) for i in range(2) for hh in range(2)]
        subs = []
        for j, (kind, i, g) in enumerate(jobs):
            for br in (("cmp", "slc", "win") if kind == "nsa" else ("moba",)):
                subs.append((j, kind, i, g, br))
        turns = [1 if br == "cmp" else i + 1 for (_, _, i, _, br) in subs]
        turns_before = [sum(turns[:s]) for s in range(len(subs) + 1)]
        job_last_turn = {}
        for s, (j, *_r) in enumerate(subs):
            job_last_turn[j] = turns_before[s + 1]
        prob_slot = {"cmp": 4, "slc": 0, "win": 2, "moba": 0}

        QA, KS, KW, ZA, QB, KB, ZB, MG = 0, 4, 5, 6, 10, 14, 18, 22
        L_X, M_QK, L_G, M_O, S_Q, S_K, G3 = 0, 2, 6, 8, 10, 12, 14
        taker2 = ["dve"] * 5 + ["act"] * 2 + ["dve"] * 4 + ["act"] * 10 + ["dve"] * 3
        taker3 = ["dve"] * 3 + ["act"] * 2 + ["dve"] * 2 + ["act"] * 12 + ["dve"] * 2

        def blocks_at(c, lo, hi):
            return ring[:, c % RING, lo * WIDE:hi * WIDE]

        def parts_at(c, lo, hi):
            cols = slice(lo * WIDE, hi * WIDE)
            return high[:, SPLIT_CHUNKS.index(c) % HIGH, cols], ring_r[:, c % RING, cols]

        def moe_parts(n, b):
            c = MOE_SPLIT[n]
            s = (C_MOE + c) % RING
            cols = slice((b % CH) * WIDE, (b % CH + 1) * WIDE)
            return high[:, n % HIGH, cols], ring_r[:, s, cols]

        def moe_split(n):
            c = MOE_SPLIT[n]
            s = (C_MOE + c) % RING
            cols = slice(max(MOE_DOWN - c * CH, 0) * WIDE, CH * WIDE)
            return high[:, n % HIGH, cols], ring_r[:, s, cols], ring[:, s, cols]

        def moe_splits(j):
            def last(j):
                return min((MOE_DOWN + KE * (j + 1) - 1) // CH + LOOK - MOE_SPLIT[0], len(MOE_SPLIT) - 1)
            return range(5 if j == 0 else last(j - 1) + 1, last(j) + 1)

        def wait_landed(eng, c, items):
            if c < C_MOE:
                eng.wait_ge(dense_landed[c % RING], 16 * (c // RING + 1))
            elif c < C_POST + AHEAD:
                eng.wait_ge(moe_landed[c % RING], items * (16 * (MOE_CH // RING)) + 16)
            else:
                before = -(-(C_MOE - c % RING) // RING)
                eng.wait_ge(dense_landed[c % RING], 16 * (before + (c - C_POST - AHEAD) // RING + 1))

        def tiles2(p):
            n = 2 * p if p < 2 else 2 * p - 4
            return proj[:, n:n + 2, :], n

        def taken(taker, stage, p):
            return S[f"{stage}_{taker[p]}"], taker[:p + 1].count(taker[p])

        @block.sync
        def _(sp):
            def slot(c):
                return ring[:, c % RING, :]

            sp.dma_start(h[:, :, :], h_in).then_inc(S["h_landed"], 16)
            for c in range(RING):
                sp.dma_start(slot(c), w_stream[c]).then_inc(dense_landed[c], 16)
                if c == 0:
                    sp.dma_start(vec[:, :], vec_in).then_inc(S["vec_landed"], 16)
            turns_pre = C_MOE // RING
            with sp.Fori(1, turns_pre) as r:
                for n in range(RING):
                    sp.wait_ge(pre_begun, r * RING + (n - RING + 2))
                    sp.dma_start(slot(n), w_stream[r * RING + n]).then_inc(dense_landed[n], 16)
            for c in range(turns_pre * RING, C_MOE):
                sp.wait_ge(pre_begun, c - RING + 2)
                sp.dma_start(slot(c), w_stream[c]).then_inc(dense_landed[c % RING], 16)
            for c in range(C_MOE, C_MOE + AHEAD):
                sp.wait_ge(pre_begun, c - RING + 2)
                sp.dma_start(slot(c), w_stream[c]).then_inc(moe_landed[c % RING], 16)
            sp.wait_ge(S["table_ready"], 1)
            items = sp.value_load(table[0:1, 16:17], min_val=NE, max_val=MAX_ITEMS)
            with sp.Fori(0, items) as i:
                this = sp.value_load(table[0:1, bass.ds(i, 1)], min_val=0, max_val=NE)
                for c in range(AHEAD, MOE_CH):
                    sp.wait_ge(moe_begun, i * MOE_CH + (c - RING + 2))
                    sp.dma_start(slot(C_MOE + c), w_stream[this * MOE_CH + (C_MOE + c)])\
                      .then_inc(moe_landed[(C_MOE + c) % RING], 16)
                then = sp.value_load(table[0:1, bass.ds(i + 1, 1)], min_val=0, max_val=NE)
                for c in range(AHEAD):
                    sp.wait_ge(moe_begun, i * MOE_CH + (MOE_CH + c - RING + 2))
                    sp.dma_start(slot(C_MOE + c), w_stream[then * MOE_CH + (C_MOE + c)])\
                      .then_inc(moe_landed[(C_MOE + c) % RING], 16)
            with sp.Fori(0, (N_POST - AHEAD) // RING) as r:
                for n in range(RING):
                    sp.wait_ge(post_begun, r * RING + (n + 1))
                    sp.dma_start(slot(C_POST + AHEAD + n), w_stream[r * RING + (C_POST + AHEAD + n)])\
                      .then_inc(dense_landed[(C_POST + AHEAD + n) % RING], 16)
            sp.wait_ge(S["normed"], 8 * 11)
            sp.dma_start(out, hn256).then_inc(S["out_done"], 16)
            sp.wait_ge(S["out_done"], 16)

        @block.tensor
        def _(pe):
            bank_owner = {}
            at_chunk = [-1]
            items = []

            def claim(b):
                if b in bank_owner:
                    pe.wait_ge(*bank_owner.pop(b))

            def block_of(b):
                c = b // CH
                first = c != at_chunk[0]
                if first:
                    assert c == at_chunk[0] + 1
                    at_chunk[0] = c
                    wait_landed(pe, c, items[0] if items else None)
                return blocks_at(c, b % CH, b % CH + 1), first

            def parts_of(b):
                c = b // CH
                first = c != at_chunk[0]
                at_chunk[0] = c
                if b % CH == SPLIT[c][0]:
                    pe.wait_ge(S["weights_low"], SPLIT_CHUNKS.index(c) + 1)
                return *parts_at(c, b % CH, b % CH + 1), first

            def begun(first, mm):
                if first:
                    mm.then_inc(pre_begun if at_chunk[0] < C_MOE else post_begun, 1)

            def pair(b0, kt, src, t, bank, done, inputs=None):
                claim(bank)
                claim(bank + 1)
                for k in range(kt):
                    if inputs is not None:
                        inputs(k)
                    w, first = block_of(b0 + k)
                    for half in range(2):
                        mm = pe.matmul(ps[:, bank + half, 0:t], w[:, half * P:half * P + P], src(k),
                                       start=(k == 0), stop=(k == kt - 1))
                        if half == 0:
                            begun(first, mm)
                        if k == kt - 1:
                            mm.then_inc(done, 1)

            def split_pair(b0, kt, x_high, x_low, t, bank, done, inputs=None):
                claim(bank)
                claim(bank + 1)
                for k in range(kt):
                    if inputs is not None:
                        inputs(k)
                    w_high, w_low, first = parts_of(b0 + k)
                    for half in range(2):
                        cols = slice(half * P, half * P + P)
                        o = ps[:, bank + half, 0:t]
                        mm = pe.matmul(o, w_high[:, cols], x_high[:, k, 0:t], start=(k == 0), stop=False)
                        if half == 0:
                            begun(first, mm)
                        pe.matmul(o, w_high[:, cols], x_low[:, k, 0:t], start=False, stop=False)
                        mm = pe.matmul(o, w_low[:, cols], x_high[:, k, 0:t], start=False, stop=(k == kt - 1))
                        if k == kt - 1:
                            mm.then_inc(done, 1)

            def token_pair(b0, x_high, x_low, bank, done):
                claim(bank)
                claim(bank + 1)
                for k in range(KD):
                    w_high, w_low, first = parts_of(b0 + k)
                    for t in range(2):
                        rows = slice(t * P, (t + 1) * P)
                        o = ps[:, bank + t, 0:WIDE]
                        mm = pe.matmul(o, x_high[:, k, rows], w_high, start=(k == 0), stop=False)
                        if t == 0:
                            begun(first, mm)
                        pe.matmul(o, x_high[:, k, rows], w_low, start=False, stop=False)
                        mm = pe.matmul(o, x_low[:, k, rows], w_high, start=False, stop=(k == KD - 1))
                        if k == KD - 1:
                            mm.then_inc(done, 1)

            def sum_squares(i, t):
                for k in range(KD):
                    pe.wait_ge(S["sq_ready"], 8 * i + k + 1)
                    mm = pe.matmul(ps[:, 7, 0:t], ones[:, 0:P], sq[:, k, 0:t], start=(k == 0), stop=(k == KD - 1))
                mm.then_inc(S["sum_done"], 1)

            def after_split(n):
                return lambda k: pe.wait_ge(S["input_low"], 8 * n + k + 1)

            pe.wait_ge(S["ones_ready"], 1)
            sum_squares(0, T0)
            pe.wait_ge(S["consts_ready"], 1)
            pe.wait_ge(S["vec_landed"], 16)

            def conv_tile(j):
                pe.wait_ge(S["glu_done"], j + 1)
                pe.wait_ge(S["diag_ready"], PE_TAPS * (j + 1))
                claim(6)
                for tap in range(PE_TAPS):
                    mm = pe.matmul(ps[:, 6, 0:T0], diag[:, j % 2, tap, :], conv_u[:, j, tap:tap + T0],
                                   start=(tap == 0), stop=(tap == PE_TAPS - 1))
                mm.then_inc(S["conv_done"], 1)
                bank_owner[6] = (S["conv_ready"], j + 1)

            for j in range(8):
                b = 2 * (j % 3)
                split_pair(BOFF["pw1"] + j * KD, KD, in_high, in_low0, T0, b, S["pw1_done"],
                           after_split(0) if j == 0 else None)
                bank_owner[b] = (S["glu_done"], j + 1)
                bank_owner[b + 1] = (S["glu_sig"], j + 1)
                if j >= 1:
                    conv_tile(j - 1)
            conv_tile(7)
            for k in range(KD):
                pe.wait_ge(S["conv_ready"], k + 1)
                mm = pe.matmul(ps[:, 7, 0:T0], ones[:, 0:P], conv_y[:, k, :], start=(k == 0), stop=(k == KD - 1))
            mm.then_inc(S["mean_done"], 1)
            sum_squares(1, T0)
            for j in range(4):
                b = 2 * (j % 3)
                split_pair(BOFF["pw2"] + j * KD, KD, hn_r, in_low0, T0, b, S["pw2_done"],
                           after_split(1) if j == 0 else None)
                bank_owner[b] = (S["h1_ready"], 2 * j + 1)
                bank_owner[b + 1] = (S["h1_ready"], 2 * j + 2)

            def ffn(n, norm_i, split_n, t, x_low, hidden_high, hidden_low, b_in, b_out):
                sum_squares(norm_i, t)
                for p in range(KF):
                    b = 2 * (p % 3)
                    split_pair(b_in + p * KD, KD, in_high, x_low, t, b, S["ffn_gu"],
                               after_split(split_n) if p == 0 else None)
                    bank_owner[b] = (S["ffn_sig"], n * KF + p + 1)
                    bank_owner[b + 1] = (S["ffn_mul"], n * KF + p + 1)
                for j in range(4):
                    b = 2 * (j % 3)
                    split_pair(b_out + j * KF, KF, hidden_high, hidden_low, t, b, S["ffn_down"],
                               (lambda k: pe.wait_ge(S["ffn_hid"], n * KF + k + 1)) if j == 0 else None)
                    bank_owner[b] = (S["ffn_out"], 8 * n + 2 * j + 1)
                    bank_owner[b + 1] = (S["ffn_out"], 8 * n + 2 * j + 2)

            ffn(0, 2, 2, T0, in_low0, hid_high0, hid_low0, BOFF["ffn0_in"], BOFF["ffn0_out"])
            sum_squares(3, T0)
            for g in range(4):
                b = 2 * (g % 3)
                pe.wait_ge(S["pooled"], g + 1)
                pair(BOFF["pool"] + 2 * g, 2, lambda k: sq256[:, 2 * g + k, :], SEQ, b, S["pool_done"])
                bank_owner[b] = (S["x_ready"], 2 * g + 1)
                bank_owner[b + 1] = (S["x_ready"], 2 * g + 2)
            sum_squares(4, SEQ)
            pe.wait_ge(S["normed"], 8 * 5)
            for t in range(2):
                for k in range(KD):
                    mm = pe.matmul(ps[:, 6, t * NE:(t + 1) * NE], hn[:, k, t * P:(t + 1) * P],
                                   vcol("router", k * NE, NE), start=(k == 0), stop=(k == KD - 1))
            mm.then_inc(S["router_done"], 1)
            pe.wait_ge(S["chosen"], 1)
            pe.matmul(ps[:, 6, 16:24], upto[:, :], hot[:, 0, :], start=True, stop=True)
            pe.matmul(ps[:, 6, 24:32], ones[:, 0:P], hot[:, 0, :], start=True, stop=False)
            pe.matmul(ps[:, 6, 24:32], upto[:, :], hot[:, 1, :], start=False, stop=True)
            pe.matmul(ps[:, 6, 32:40], ones[:, 0:P], hot[:, 0, :], start=True, stop=False)
            pe.matmul(ps[:, 6, 32:40], ones[:, 0:P], hot[:, 1, :], start=False, stop=True)\
              .then_inc(S["ranks_done"], 1)
            pe.wait_ge(S["x_ready"], 8)
            for t in range(2):
                for k in range(KD):
                    mm = pe.transpose(ps[:, 2 * t + k // 4, (k % 4) * P:(k % 4 + 1) * P],
                                      hn[:, k, t * P:(t + 1) * P], ident[:, :])
                mm.then_inc(S["xt_done"], 1)
            bank_owner.clear()
            pe.wait_ge(S["xt_ready"], 2)
            assert at_chunk[0] == C_MOE - 1
            pe.wait_ge(S["table_ready"], 1)
            items.append(pe.value_load(table[0:1, 16:17], min_val=NE, max_val=MAX_ITEMS))

            def pick_tokens():
                for k in range(KD):
                    for t in range(2):
                        mm = pe.matmul(ps[:, 6 + k // 4, (k % 4) * CAP:(k % 4 + 1) * CAP],
                                       x_tok[:, t, k * P:(k + 1) * P], pick[:, t, :], start=(t == 0), stop=(t == 1))
                mm.then_inc(S["pick_done"], 1)

            def sum_outputs(n):
                for k in range(4 * n, 4 * n + 4):
                    mm = pe.matmul(ps[:, 6 + k % 4 // 2, (k % 2) * SEQ:(k % 2 + 1) * SEQ],
                                   y_tok[0:CAP, k * P:(k + 1) * P], w_row[0:CAP, :], start=True, stop=True)
                    if k % 2:
                        mm.then_inc(S["moe_sum"], 1)

            for _ in range(10):
                pe.matmul(ps[:, 5, 0:SEQ], ones[:, 0:P], hn[:, 0, 0:SEQ], start=True, stop=True)
            pe.wait_ge(S["picks_ready"], 1)
            pick_tokens()
            with pe.Fori(0, items[0]) as i:
                blk = [0, -1]

                def moe_block():
                    b, blk[0] = blk[0], blk[0] + 1
                    c = b // CH
                    first = c != blk[1]
                    blk[1] = c
                    s = (C_MOE + c) % RING
                    if first:
                        pe.wait_ge(moe_landed[s], i * (16 * (MOE_CH // RING)) + 16 * (c // RING + 1))
                    return ring[:, s, (b % CH) * WIDE:(b % CH + 1) * WIDE], first

                def moe_pair(kt, src, bank, done, inputs=None):
                    for k in range(kt):
                        if inputs is not None:
                            inputs(k)
                        w, first = moe_block()
                        for half in range(2):
                            mm = pe.matmul(ps[:, bank + half, 0:CAP], w[:, half * P:half * P + P], src[:, k, :],
                                           start=(k == 0), stop=(k == kt - 1))
                            if half == 0 and first:
                                mm.then_inc(moe_begun, 1)
                            if k == kt - 1:
                                mm.then_inc(done, 1)

                for p in range(KE):
                    if p < 2:
                        pe.wait_ge(S["moe_y"], i * 4 + (3 + p))
                    elif p >= 3:
                        pe.wait_ge(S["moe_sig"], i * KE + (p - 2))
                        pe.wait_ge(S["moe_mul"], i * KE + (p - 2))
                    if p == 0:
                        pe.wait_ge(S["pick_ready"], i + 1)
                    moe_pair(KD, x_item, 2 * (p % 3), S["moe_gu"])
                    if p == 4:
                        pe.wait_ge(S["wt_ready"], i + 1)
                        pe.wait_ge(S["moe_y"], i * 4 + 4)
                        sum_outputs(0)
                    if p == 9:
                        pe.wait_ge(S["moe_out"], i * 4 + 2)
                        sum_outputs(1)
                pe.wait_ge(S["picks_ready"], i + 2)
                pe.wait_ge(S["moe_out"], i * 4 + 4)
                pick_tokens()
                for t in range(2):
                    mm = pe.transpose(ps[0:CAP, 6 + t, 384:512], wpick[:, t, :], ident[:, :])
                mm.then_inc(S["wt_done"], 1)
                for j in range(4):
                    if j == 0:
                        pe.wait_ge(S["moe_mul"], i * KE + KE)
                    if j == 3:
                        pe.wait_ge(S["moe_y"], i * 4 + 5)
                    for k in range(KE):
                        if j == 0:
                            pe.wait_ge(S["moe_hid"], i * KE + max(k + 1, KE - 2))
                        b = MOE_DOWN + j * KE + k
                        c = b // CH
                        n = c - MOE_SPLIT[0]
                        if c != blk[1] or b == MOE_DOWN:
                            pe.wait_ge(S["moe_low"], i * len(MOE_SPLIT) + (n + 1))
                        w_high, w_low = moe_parts(n, b)
                        o = ps[0:CAP, 2 * ((j + 1) % 3), 0:WIDE]
                        mm = pe.matmul(o, hid_item_high[:, k, :], w_high, start=(k == 0), stop=False)
                        if c != blk[1]:
                            mm.then_inc(moe_begun, 1)
                            blk[1] = c
                        pe.matmul(o, hid_item_high[:, k, :], w_low, start=False, stop=False)
                        mm = pe.matmul(o, hid_item_low[:, k, :], w_high, start=False, stop=(k == KE - 1))
                    mm.then_inc(S["moe_down"], 1)
            at_chunk[0] = C_POST - 1
            pe.wait_ge(S["moe_y"], items[0] * 4 + 4)
            pe.wait_ge(S["wt_ready"], items[0] + 1)
            sum_outputs(0)
            pe.wait_ge(S["moe_out"], items[0] * 4 + 2)
            sum_outputs(1)
            pe.wait_ge(S["moe_all"], 1)

            sum_squares(5, SEQ)
            sum_squares(6, SEQ)
            for p in range(24):
                b = 2 * (p % 3)
                if p < 21:
                    split_pair(BOFF["w_in2"] + p * KD, KD, in_high, in_low, SEQ, b, S["in2_done"],
                               after_split(3) if p == 0 else None)
                else:
                    token_pair(BOFF["w_in2"] + p * KD, in_high, in_low, b, S["in2_done"])
                bank_owner[b] = bank_owner[b + 1] = taken(taker2, "in2", p)
            for t in range(2):
                for k in range(KD):
                    mm = pe.matmul(ps[:, 6, t * 24:(t + 1) * 24], hn256[:, k, t * P:(t + 1) * P],
                                   vcol("w_gates", k * 24, 24), start=(k == 0), stop=(k == KD - 1))
            mm.then_inc(S["gl_done"], 1)
            pe.wait_ge(S["in2_act"], taker2.count("act"))
            pe.wait_ge(S["in2_dve"], taker2.count("dve"))
            bank_owner.clear()
            for kv in range(2):
                for a in range(16):
                    w, first = block_of(BOFF["cmp"] + 8 * kv + a // 2)
                    mm = pe.matmul(ps[:, 2 * kv, 0:3 * CMP_N].rearrange("p (g n) -> p g n", g=3),
                                   w[:, (a % 2) * P:(a % 2) * P + P],
                                   windows[:, kv, :, 2 * a:2 * a + 16 * (CMP_N - 1) + 1:16],
                                   start=(a == 0), stop=(a == 15))
                    if a == 15:
                        mm.then_inc(S["cmp_h_done"], 1)
                    else:
                        begun(first, mm)
            for kv in range(2):
                pe.wait_ge(S["cmp_h_ready"], 2 * kv + 2)
                for g in range(2):
                    hidc = cmp_h[:, 2 * kv + g, 0:CMP_N]
                    if kv == 0:
                        mm = pe.matmul(ps[64 * g:64 * g + 64, 6, 64:64 + CMP_N], vcol("w2k", 0, 64), hidc,
                                       start=True, stop=True)
                    else:
                        mm = pe.matmul(ps[0:CMP_N, 7, 64 * g:64 * g + 64], hidc, vcol("w2v", 0, 64),
                                       start=True, stop=True)
            mm.then_inc(S["cmp_kv_done"], 1)
            pe.wait_ge(S["cmp_kv_ready"], 2)
            pe.wait_ge(S["gates_ready"], 1)

            def scores(s):
                j, kind, i, g, br = subs[s]
                if s >= 2:
                    pe.wait_ge(S["s_ready"], s - 1)
                n = CMP_N if br == "cmp" else (i + 1) * P
                for p in range(4):
                    bank = 2 * (s % 2) + p % 2
                    if kind == "nsa":
                        lo = 64 * g
                        q = proj[lo:lo + 64, QA + p, i * P:(i + 1) * P]
                        key = cmp_k[lo:lo + 64, 0:CMP_N] if br == "cmp" else \
                            proj[lo:lo + 64, KS if br == "slc" else KW, 0:n]
                    else:
                        hd = 4 * g + p
                        lo = 64 * (hd % 2)
                        q = proj[lo:lo + 64, QB + hd // 2, i * P:(i + 1) * P]
                        key = proj[lo:lo + 64, KB + hd // 2, 0:n]
                    mm = pe.matmul(ps[:, bank, (p // 2) * 256:(p // 2) * 256 + n], q, key, start=True, stop=True)
                mm.then_inc(S["score_done"], 1)

            def turn(s):
                j, kind, i, g, br = subs[s]
                pe.wait_ge(S["prob_ready"], s + 1)
                for kt in range(turns[s]):
                    u = turns_before[s] + kt
                    if u >= 2:
                        pe.wait_ge(S["turned"], u - 1)
                    for p in range(4):
                        if br == "cmp":
                            mm = pe.transpose(ps[0:CMP_N, 4 + u % 2, p * P:(p + 1) * P],
                                              soft[:, s % 3, p, 0:CMP_N], ident[:, :])
                        else:
                            mm = pe.transpose(ps[:, 4 + u % 2, p * P:(p + 1) * P],
                                              soft[:, s % 3, p, kt * P:(kt + 1) * P], ident[:, :])
                    mm.then_inc(S["turn_done"], 1)

            def values(j):
                kind, i, g = jobs[j]
                pe.wait_ge(S["turned"], job_last_turn[j])
                if j >= 2:
                    pe.wait_ge(S["y_ready"], j - 1)
                for p in range(4):
                    if kind == "nsa":
                        o = ps[64 * g:64 * g + 64, 6 + j % 2, p * P:(p + 1) * P]
                        terms = [(cmp_v[0:CMP_N, 64 * g:64 * g + 64], probs_turned(4)[0:CMP_N, p * P:(p + 1) * P])]
                        for br in (0, 1):
                            terms += [(vtok[:, kt, br * P + 64 * g:br * P + 64 * g + 64],
                                       probs_turned(2 * br + kt)[:, p * P:(p + 1) * P]) for kt in range(i + 1)]
                    else:
                        hd = 4 * g + p
                        lo = 64 * (hd % 2)
                        o = ps[lo:lo + 64, 6 + j % 2, (p // 2) * P:(p // 2 + 1) * P]
                        terms = [(vtok[:, kt, 256 + 64 * hd:256 + 64 * hd + 64],
                                  probs_turned(kt)[:, p * P:(p + 1) * P]) for kt in range(i + 1)]
                    for n, (lw, r) in enumerate(terms):
                        mm = pe.matmul(o, lw, r, start=(n == 0), stop=(n == len(terms) - 1))
                mm.then_inc(S["pv_done"], 1)

            scores(0)
            scores(1)
            for s in range(len(subs)):
                if s + 2 < len(subs):
                    scores(s + 2)
                if s and subs[s - 1][0] != subs[s][0]:
                    values(subs[s - 1][0])
                turn(s)
            values(len(jobs) - 1)
            pe.wait_ge(S["y_ready"], 8)
            for j in range(4):
                if j >= 2:
                    pe.wait_ge(S["br_ready"], 2 * j - 2)
                for br in range(2):
                    for k in range(4):
                        w, first = block_of(BOFF["branch"] + j * KD + 4 * br + k)
                        for half in range(2):
                            mm = pe.matmul(ps[:, 4 * (j % 2) + 2 * br + half, 0:SEQ], w[:, half * P:half * P + P],
                                           sq256[:, 4 * br + k, :], start=(k == 0), stop=(k == 3))
                            begun(half == 0 and first, mm)
                mm.then_inc(S["br_done"], 1)
            pe.wait_ge(S["br_ready"], 8)
            for j in range(4):
                b = 2 * (j % 3)
                pair(BOFF["w_o2"] + j * KD, KD, lambda k: hn256[:, k, :], SEQ, b, S["wo2_done"])
                bank_owner[b] = (S["wo2_ready"], 2 * j + 1)
                bank_owner[b + 1] = (S["wo2_ready"], 2 * j + 2)
            sum_squares(7, SEQ)

            sum_squares(8, SEQ)
            for p in range(21):
                b = 2 * (p % 3)
                if p < 19:
                    split_pair(BOFF["w_in3"] + p * KD, KD, in_high, in_low, SEQ, b, S["in3_done"],
                               after_split(4) if p == 0 else None)
                else:
                    token_pair(BOFF["w_in3"] + p * KD, in_high, in_low, b, S["in3_done"])
                bank_owner[b] = bank_owner[b + 1] = taken(taker3, "in3", p)
            for n in range(2):
                for k in range(KD):
                    mm = pe.matmul(ps[0:4, 6, n * SEQ:(n + 1) * SEQ], vcol("w_if", k * 8 + 4 * n, 4),
                                   hn256[:, k, :], start=(k == 0), stop=(k == KD - 1))
            mm.then_inc(S["if_done"], 1)
            bank_owner.clear()
            pe.wait_ge(S["in3_act"], taker3.count("act"))
            pe.wait_ge(S["in3_dve"], taker3.count("dve"))
            for hd in range(4):
                lo = 64 * (hd % 2)
                for kt in range(2):
                    mm = pe.matmul(ps[:, hd, 256 * kt:256 * kt + SEQ - P * kt],
                                   proj[lo:lo + 64, S_K + hd // 2, kt * P:(kt + 1) * P],
                                   proj[lo:lo + 64, S_Q + hd // 2, kt * P:SEQ], start=True, stop=True)
                mm.then_inc(S["sb_z_done"], 1)
            pe.wait_ge(S["conv3_ready"], 1)
            for n, name in enumerate(("lru_wa", "lru_wx")):
                for t in range(2):
                    for lo in (0, 64):
                        mm = pe.matmul(ps[lo:lo + 64, 4 + n, t * SEQ:(t + 1) * SEQ],
                                       vec[lo:lo + 64, VOFF[name] + 64 * t:VOFF[name] + 64 * t + 64],
                                       xa[lo:lo + 64, t, :], start=True, stop=True)
            mm.then_inc(S["lru_g_done"], 1)
            for hd in range(4):
                pe.wait_ge(S["sb_lk"], hd + 1)
                pe.matmul(ps[:, hd, 0:SEQ], tri[:, :], sb_lk[:, hd, 0:SEQ], start=True, stop=False)
                pe.matmul(ps[:, hd, P:SEQ], ones[:, 0:P], sb_lk[:, hd, SEQ:3 * P], start=False, stop=True)
                mm = pe.matmul(ps[:, hd, SEQ:3 * P], tri[:, :], sb_lk[:, hd, SEQ:3 * P], start=True, stop=True)
                mm.then_inc(S["sb_r_done"], 1)
            pe.wait_ge(S["c_ready"], 1)
            for t in range(2):
                mm = pe.transpose(ps[:, 7, 4 * t:4 * t + 4], crow[:, t * P:(t + 1) * P], ident[0:4, 0:4])
            mm.then_inc(S["cT_done"], 1)
            pe.wait_ge(S["lru_sig"], 2)
            for hd in range(4):
                lo = 64 * (hd % 2)
                c0v = 256 + 64 * hd
                pe.wait_ge(S["sb_a"], hd + 1)
                o = ps[lo:lo + 64, 4, (hd // 2) * SEQ:(hd // 2 + 1) * SEQ]
                pe.matmul(o, v3[:, 0, c0v:c0v + 64], sb_w[:, hd, 0:SEQ], start=True, stop=False)
                mm = pe.matmul(o[:, P:SEQ], v3[:, 1, c0v:c0v + 64], sb_w[:, hd, SEQ:3 * P], start=False, stop=True)
            mm.then_inc(S["sb_o_done"], 1)
            pe.wait_ge(S["m_floor"], 1)
            pe.wait_ge(S["cT_ready"], 1)
            for hd in range(4):
                mm = pe.matmul(ps[:, hd // 2, (hd % 2) * SEQ:(hd % 2 + 1) * SEQ], sel[0:4, hd, :], mrow,
                               start=True, stop=True)
            mm.then_inc(S["mb_done"], 1)
            for hd in range(4):
                lo = 64 * (hd % 2)
                mm = pe.matmul(ps[lo:lo + 64, 5, (hd // 2) * SEQ:(hd // 2 + 1) * SEQ], sel[0:4, hd, 0:64],
                               floor, start=True, stop=True)
            mm.then_inc(S["fl_done"], 1)
            pe.wait_ge(S["mb_ready"], 4)
            pe.wait_ge(S["qk_silu"], 1)
            for hd in range(4):
                lo = 64 * (hd % 2)
                for kt in range(2):
                    mm = pe.matmul(ps[:, hd, 256 * kt:256 * kt + SEQ - P * kt],
                                   qk3[lo:lo + 64, 2 + hd // 2, kt * P:(kt + 1) * P],
                                   qk3[lo:lo + 64, hd // 2, kt * P:SEQ], start=True, stop=True)
                mm.then_inc(S["ml_s_done"], 1)
            for hd in range(4):
                lo = 64 * (hd % 2)
                pe.wait_ge(S["ml_p"], hd + 1)
                for bank, lws in ((6, (v3[:, 0, 64 * hd:64 * hd + 64], v3[:, 1, 64 * hd:64 * hd + 64])),
                                  (7, (ones[:, 0:64], ones[:, 0:64]))):
                    o = ps[lo:lo + 64, bank, (hd // 2) * SEQ:(hd // 2 + 1) * SEQ]
                    pe.matmul(o, lws[0], sb_w[:, hd, 0:SEQ], start=True, stop=False)
                    mm = pe.matmul(o[:, P:SEQ], lws[1], sb_w[:, hd, SEQ:3 * P], start=False, stop=True)
            mm.then_inc(S["ml_nd_done"], 1)
            pe.wait_ge(S["lru_in"], 1)
            pe.wait_ge(S["sb_y"], 1)
            pe.wait_ge(S["mh_ready"], 1)
            for j in range(4):
                for br in range(3):
                    for k in range(2):
                        w, first = block_of(BOFF["outs3"] + j * 6 + 2 * br + k)
                        for half in range(2):
                            if j and br == 0 and k == 0:
                                pe.wait_ge(S["out3_part"], 2 * j - 1 + half)
                            mm = pe.matmul(ps[:, 3 * half + br, 0:SEQ], w[:, half * P:half * P + P],
                                           y3[:, 2 * br + k, :], start=(k == 0), stop=(k == 1))
                            begun(half == 0 and first, mm)
                mm.then_inc(S["out3_done"], 1)
            pe.wait_ge(S["merged"], 8)
            for j in range(4):
                b = 2 * (j % 3)
                pair(BOFF["w_o3"] + j * KD, KD, lambda k: hn256[:, k, :], SEQ, b, S["wo3_done"])
                bank_owner[b] = (S["x3_ready"], 2 * j + 1)
                bank_owner[b + 1] = (S["x3_ready"], 2 * j + 2)
            ffn(1, 9, 5, SEQ, in_low, hid_high, hid_low, BOFF["ffn3_in"], BOFF["ffn3_out"])
            sum_squares(10, SEQ)
            for c in range(at_chunk[0] + 1, NCH):
                wait_landed(pe, c, items[0])

        @block.scalar
        def _(act):
            steps = [0]

            def step(ins):
                steps[0] += 1
                ins.then_inc(S["act_step"], 1)
                act.wait_ge(S["act_step"], steps[0])

            split = [0]
            items_of = []

            def split_weights(last):
                while split[0] < len(SPLIT_CHUNKS) and SPLIT_CHUNKS[split[0]] <= last:
                    n, c = split[0], SPLIT_CHUNKS[split[0]]
                    wait_landed(act, c, items_of[0] if items_of else None)
                    if n >= HIGH:
                        before = SPLIT_CHUNKS[n - HIGH]
                        if c < C_MOE:
                            act.wait_ge(pre_begun, before + 2)
                        elif before >= C_POST:
                            act.wait_ge(post_begun, before - C_POST + 2)
                    act.activation(parts_at(c, *SPLIT[c])[0], blocks_at(c, *SPLIT[c]), ACT.Copy).then_inc(S["weights_high"], 1)
                    split[0] += 1

            def norm(i, src, t, ready, first_block=None, split_n=None):
                for k in range(KD):
                    if first_block and k in (4, 6):
                        split_weights((first_block - 1) // CH + k - 2)
                    ready(k)
                    act.activation(sq[:, k, 0:t], src[:, k, 0:t], ACT.Square).then_inc(S["sq_ready"], 1)
                act.wait_ge(S["var_ready"], i + 1)
                act.activation(var[:, 0:t], var[:, 0:t], ACT.Sqrt).then_inc(S["std_ready"], 1)
                if first_block == 0:
                    split_weights(0)
                if split_n is not None:
                    for k in range(KD):
                        if first_block == 0 and k == 3:
                            split_weights(1)
                        act.wait_ge(S["normed"], 8 * i + k + 1)
                        act.activation(in_high[:, k, 0:t], hn[:, k, 0:t], ACT.Copy).then_inc(S["input_high"], 1)

            act.wait_ge(S["h_landed"], 16)
            norm(0, h, T0, lambda k: None, 0, 0)
            act.wait_ge(S["vec_landed"], 16)
            for j in range(8):
                split_weights((BOFF["pw1"] + j * KD + KD - 1) // CH + LOOK)
                act.wait_ge(S["pw1_done"], 2 * j + 2)
                if j >= 2:
                    act.wait_ge(S["glu_done"], j - 1)
                act.activation(gate_sb[:, j % 2, :], ps[:, 2 * (j % 3) + 1, 0:T0], ACT.Sigmoid,
                               bias=vcol("b_pw1", 8 + j)).then_inc(S["glu_sig"], 1)
            norm(1, conv_y, T0, lambda k: act.wait_ge(S["xc_ready"], k + 1))
            for k in range(KD + 1):
                if k < KD:
                    act.wait_ge(S["normed"], 8 * 1 + k + 1)
                    act.activation(sq[:, k, :], conv_y[:, k, :], ACT.Silu, bias=vcol("ln_b", k))\
                       .then_inc(S["ln_silu"], 1)
                if k:
                    act.wait_ge(S["ln_silu"], k)
                    act.activation(hn_r[:, k - 1, :], sq[:, k - 1, :], ACT.Copy)\
                       .then_inc(S["input_high"], 1)
            for j in range(4):
                split_weights((BOFF["pw2"] + j * KD + KD - 1) // CH + LOOK)
            norm(2, h, T0, lambda k: act.wait_ge(S["h1_ready"], k + 1), BOFF["ffn0_in"], 2)

            def ffn(n, t, hidden_high, b_in, b_out):
                for p in range(KF + 1):
                    if p < KF:
                        split_weights((b_in + p * KD + KD - 1) // CH + LOOK)
                        act.wait_ge(S["ffn_gu"], n * 2 * KF + 2 * p + 2)
                        if p >= 2:
                            act.wait_ge(S["ffn_hid"], n * KF + p - 1)
                        act.activation(gate_sb[:, p % 2, 0:t], ps[:, 2 * (p % 3), 0:t], ACT.Silu)\
                           .then_inc(S["ffn_sig"], 1)
                    if p:
                        act.wait_ge(S["ffn_mul"], n * KF + p)
                        act.activation(hidden_high[:, p - 1, 0:t], gate_sb[:, (p - 1) % 2, 0:t], ACT.Copy)\
                           .then_inc(S["input_high"], 1)
                split_weights((b_out + KD // 2 * KF - 1) // CH)

            ffn(0, T0, hid_high0, BOFF["ffn0_in"], BOFF["ffn0_out"])
            norm(3, h, T0, lambda k: act.wait_ge(S["ffn_out"], k + 1))
            norm(4, x, SEQ, lambda k: act.wait_ge(S["x_ready"], 8))
            act.wait_ge(S["gap_ready"], 1)
            act.activation(gap[:, :, 1:2], gap[:, :, 0:1], ACT.Exp).then_inc(S["gap_exp"], 1)
            for t in range(2):
                act.wait_ge(S["xt_done"], t + 1)
                act.activation(x_tok[:, t, :].rearrange("p (b c) -> p b c", b=2), ps[:, 2 * t:2 * t + 2, :], ACT.Copy)\
                   .then_inc(S["xt_ready"], 1)
            act.wait_ge(S["table_ready"], 1)
            items = act.value_load(table[0:1, 16:17], min_val=NE, max_val=MAX_ITEMS)
            items_of.append(items)
            with act.Fori(0, items) as i:
                def split_down(n):
                    c = MOE_SPLIT[n]
                    act.wait_ge(moe_landed[(C_MOE + c) % RING],
                                i * (16 * (MOE_CH // RING)) + 16 * (c // RING + 1))
                    act.wait_ge(moe_begun, i * MOE_CH + (c - HIGH + 2 if n >= HIGH else 1))
                    w_high, _, w = moe_split(n)
                    act.activation(w_high, w, ACT.Copy).then_inc(S["moe_high"], 1)

                for p in range(KE + 1):
                    if p < KE:
                        act.wait_ge(S["moe_gu"], i * (2 * KE) + (2 * p + 2))
                        if p >= 2:
                            act.wait_ge(S["moe_hid"], i * KE + (p - 1))
                        act.activation(gate_sb[:, p % 2, 0:CAP], ps[:, 2 * (p % 3), 0:CAP], ACT.Silu)\
                           .then_inc(S["moe_sig"], 1)
                    if p:
                        act.wait_ge(S["moe_mul"], i * KE + p)
                        act.activation(hid_item_high[:, p - 1, :], gate_sb[:, (p - 1) % 2, 0:CAP], ACT.Copy)\
                           .then_inc(S["moe_hid_high"], 1)
                    for n in {KE - 3: (0,), KE - 2: (1, 2), KE: (3, 4)}.get(p, ()):
                        split_down(n)
                act.wait_ge(S["pick_ready"], i + 2)
                act.activation(w_row[0:CAP, :].rearrange("p (t c) -> p t c", t=2), ps[0:CAP, 6:8, 384:512], ACT.Copy)\
                   .then_inc(S["wt_ready"], 1)
                for j in range(4):
                    for n in moe_splits(j):
                        split_down(n)
                    act.wait_ge(S["moe_down"], i * 4 + (j + 1))
                    act.activation(y_tok[0:CAP, j * WIDE:(j + 1) * WIDE], ps[0:CAP, 2 * ((j + 1) % 3), 0:WIDE],
                                   ACT.Copy).then_inc(S["moe_y"], 1)
            split_weights(C_POST + LOOK)
            norm(5, x, SEQ, lambda k: act.wait_ge(S["moe_all"], 1))
            norm(6, x, SEQ, lambda k: act.wait_ge(S["normed"], 8 * 5 + k + 1), split_n=3)
            for p in range(24):
                split_weights((BOFF["w_in2"] + p * KD + KD - 1) // CH + LOOK)
                if taker2[p] != "act":
                    continue
                act.wait_ge(S["in2_done"], 2 * p + 2)
                b = 2 * (p % 3)
                dst, n = tiles2(p)
                act.activation(dst, ps[:, b:b + 2, 0:SEQ], ACT.Silu if n < MG else ACT.Sigmoid)\
                   .then_inc(S["in2_act"], 1)
            act.wait_ge(S["gl_done"], 1)
            act.activation(gates, ps[:, 6, 0:48], ACT.Sigmoid).then_inc(S["gates_ready"], 1)
            act.wait_ge(S["cmp_pe_ready"], 1)
            for kv in range(2):
                act.wait_ge(S["cmp_pe_ready"], kv + 1)
                for g in range(2):
                    act.activation(cmp_h[:, 2 * kv + g, 0:CMP_N], ps[:, 2 * kv, g * CMP_N:(g + 1) * CMP_N], ACT.Silu,
                                   bias=cmp_pe[:, kv:kv + 1]).then_inc(S["cmp_h_ready"], 1)

            def exps(s):
                j, kind, i, g, br = subs[s]
                act.wait_ge(S["s_ready"], s + 1)
                n = CMP_N if br == "cmp" else (i + 1) * P
                for p in range(4):
                    ins = act.activation(soft[:, s % 3, p, 0:n], soft[:, s % 3, p, 0:n], ACT.Exp,
                                         bias=stats[:, s % 3, 1, p:p + 1], accum_out=stats[:, s % 3, 2, p:p + 1])
                ins.then_inc(S["exp_ready"], 1)

            def copies(s):
                j, kind, i, g, br = subs[s]
                for kt in range(turns[s]):
                    u = turns_before[s] + kt
                    act.wait_ge(S["turn_done"], u + 1)
                    if j >= 1:
                        act.wait_ge(S["pv_done"], j)
                    rows_n = CMP_N if br == "cmp" else P
                    act.activation(probs_turned(prob_slot[br] + kt)[0:rows_n, :], ps[0:rows_n, 4 + u % 2, :], ACT.Copy)\
                       .then_inc(S["turned"], 1)

            exps(0)
            exps(1)
            for s in range(len(subs)):
                copies(s)
                if s + 2 < len(subs):
                    exps(s + 2)
            norm(7, zo, SEQ, lambda k: act.wait_ge(S["wo2_ready"], k + 1), BOFF["w_in3"])
            norm(8, x, SEQ, lambda k: act.wait_ge(S["normed"], 8 * 7 + k + 1), split_n=4)
            step(act.activation(lam[:, 0, :], vcol("lru_lam", 0, 2), ACT.Abs))
            act.activation(lam[:, 1, :], lam[:, 0, :], ACT.Exp, scale=-1.0).then_inc(S["lam_exp"], 1)
            for p in range(21):
                split_weights((BOFF["w_in3"] + p * KD + KD - 1) // CH + LOOK)
                if taker3[p] != "act":
                    continue
                act.wait_ge(S["in3_done"], 2 * p + 2)
                b = 2 * (p % 3)
                act.activation(proj[:, 2 * p:2 * p + 2, :], ps[:, b:b + 2, 0:SEQ],
                               ACT.Gelu_apprx_tanh if 2 * p == L_G else ACT.Sigmoid).then_inc(S["in3_act"], 1)
            act.wait_ge(S["conv3_ready"], 3)
            act.activation(qk3, qk3, ACT.Silu).then_inc(S["qk_silu"], 1)
            act.wait_ge(S["lru_g_done"], 1)
            for n, name in enumerate(("lru_ba", "lru_bx")):
                for t in range(2):
                    ins = act.activation(lru_t[:, n, t, :], ps[:, 4 + n, t * SEQ:(t + 1) * SEQ], ACT.Sigmoid,
                                         bias=vcol(name, t))
                ins.then_inc(S["lru_sig"], 1)
            for hd in range(4):
                act.wait_ge(S["sb_zs"], hd + 1)
                ins = act.activation(sb_lk[:, hd, :], zs[:, hd, :], ACT.Abs)
            step(ins)
            act.wait_ge(S["gate_in"], 1)
            step(act.activation(arow, frow, ACT.Abs))
            act.activation(sb_lk, sb_lk, ACT.Exp, scale=-1.0)
            act.wait_ge(S["lru_loga"], 1)
            act.activation(lru_t[:, 3, :, :], lru_t[:, 2, :, :], ACT.Exp).then_inc(S["lru_a"], 1)
            step(act.activation(arow, arow, ACT.Exp, scale=-1.0))
            for hd in range(4):
                act.activation(sb_lk[:, hd, :], sb_lk[:, hd, :], ACT.Ln, bias=1.0).then_inc(S["sb_ln"], 1)
            act.activation(arow, arow, ACT.Ln, bias=1.0).then_inc(S["gate_ln"], 1)
            act.wait_ge(S["lru_a"], 1)
            act.activation(lru_t[:, 2, :, :], lru_t[:, 2, :, :], ACT.Tanh).then_inc(S["lru_a"], 1)
            act.wait_ge(S["lru_f"], 1)
            act.activation(lru_t[:, 2, :, :], lru_t[:, 2, :, :], ACT.Sqrt, scale=-1.0).then_inc(S["lru_sqrt"], 1)
            for hd in range(4):
                act.wait_ge(S["sb_arg"], hd + 1)
                act.activation(sb_w[:, hd, :], sb_w[:, hd, :], ACT.Exp).then_inc(S["sb_a"], 1)
            act.wait_ge(S["m_floor_in"], 1)
            act.activation(floor, floor, ACT.Exp).then_inc(S["m_floor"], 1)
            act.wait_ge(S["cT_ready"], 1)
            for hd in range(4):
                act.wait_ge(S["mb_ready"], hd + 1)
                act.activation(decay[:, hd, 0:SEQ], decay[:, hd, 0:SEQ], ACT.Exp, bias=ccol[:, hd:hd + 1])
                act.activation(decay[:, hd, SEQ:3 * P], decay[:, hd, SEQ:3 * P], ACT.Exp,
                               bias=ccol[:, 4 + hd:5 + hd]).then_inc(S["ml_exp"], 1)
            act.wait_ge(S["ml_nd_done"], 1)
            act.activation(lru_t[:, 0, :, :], ps[:, 7, :].rearrange("p (k t) -> p k t", k=2), ACT.Abs)\
               .then_inc(S["fl_ready"], 1)
            norm(9, x, SEQ, lambda k: act.wait_ge(S["x3_ready"], k + 1), BOFF["ffn3_in"], 5)
            ffn(1, SEQ, hid_high, BOFF["ffn3_in"], BOFF["ffn3_out"])
            norm(10, x, SEQ, lambda k: act.wait_ge(S["ffn_out"], 8 + k + 1))

        @block.vector
        def _(dve):
            steps = [0]

            def step(ins):
                steps[0] += 1
                ins.then_inc(S["dve_step"], 1)
                dve.wait_ge(S["dve_step"], steps[0])

            def inverse_root(i, t, eps):
                dve.wait_ge(S["sum_done"], i + 1)
                dve.tensor_scalar(var[:, 0:t], ps[:, 7, 0:t], 1.0 / D, eps, ALU.mult, ALU.add)\
                   .then_inc(S["var_ready"], 1)
                dve.wait_ge(S["std_ready"], i + 1)
                step(dve.reciprocal(rstd[:, 0:t], var[:, 0:t]))

            split = [0]
            inputs_split = [0]

            def split_weights(last):
                while split[0] < len(SPLIT_CHUNKS) and SPLIT_CHUNKS[split[0]] <= last:
                    n, c = split[0], SPLIT_CHUNKS[split[0]]
                    dve.wait_ge(S["weights_high"], n + 1)
                    w_high, w_low = parts_at(c, *SPLIT[c])
                    dve.tensor_tensor(w_low, blocks_at(c, *SPLIT[c]), w_high.bitcast(F32), ALU.subtract).then_inc(S["weights_low"], 1)
                    split[0] += 1

            def low_part(low, whole, high_part, done):
                inputs_split[0] += 1
                dve.wait_ge(S["input_high"], inputs_split[0])
                dve.tensor_tensor(low, whole, high_part.bitcast(F32), ALU.subtract).then_inc(S[done], 1)

            def norm(i, src, dst, gain, t, eps=EPS, first_block=None, low=None):
                if first_block:
                    split_weights(first_block // CH + 1)
                inverse_root(i, t, eps)
                if first_block == 0:
                    split_weights(0)
                    dve.wait_ge(S["vec_landed"], 16)
                for k in range(KD + 1):
                    if first_block == 0 and k == 4:
                        split_weights(1)
                    if k < KD:
                        dve.scalar_tensor_tensor(out=dst[:, k, 0:t], in0=src[:, k, 0:t], scalar=vcol(gain, k),
                                                 in1=rstd[:, 0:t], op0=ALU.mult, op1=ALU.mult)\
                           .then_inc(S["normed"], 1)
                    if k and low is not None:
                        low_part(low[:, k - 1, 0:t], dst[:, k - 1, 0:t], in_high[:, k - 1, 0:t], "input_low")

            step(dve.memset(conv_u[:, :, 0:CONVW - 1], 0.0))
            dve.wait_ge(S["h_landed"], 16)
            norm(0, h, hn, "mix_g0", T0, first_block=0, low=in_low0)

            dve.wait_ge(S["consts_ready"], 1)

            def conv_dve(j):
                dve.wait_ge(S["glu_done"], j + 1)
                for tap in range(PE_TAPS, CONVW):
                    u = conv_u[:, j, tap:tap + T0]
                    w = vcol("w_dw", j * CONVW + tap)
                    if tap == PE_TAPS:
                        step(dve.tensor_scalar(conv_y[:, j, :], u, w, None, ALU.mult))
                    else:
                        step(dve.scalar_tensor_tensor(out=conv_y[:, j, :], in0=u, scalar=w, in1=conv_y[:, j, :],
                                                      op0=ALU.mult, op1=ALU.add))
                dve.wait_ge(S["conv_done"], j + 1)
                dve.scalar_tensor_tensor(out=conv_y[:, j, :], in0=ps[:, 6, 0:T0], scalar=vcol("b_dw", j),
                                         in1=conv_y[:, j, :], op0=ALU.add, op1=ALU.add).then_inc(S["conv_ready"], 1)

            for j in range(8):
                split_weights((BOFF["pw1"] + j * KD + KD - 1) // CH + LOOK)
                dve.wait_ge(S["glu_sig"], j + 1)
                dve.scalar_tensor_tensor(out=conv_u[:, j, CONVW - 1:CONVW - 1 + T0], in0=ps[:, 2 * (j % 3), 0:T0],
                                         scalar=vcol("b_pw1", j), in1=gate_sb[:, j % 2, :],
                                         op0=ALU.add, op1=ALU.mult).then_inc(S["glu_done"], 1)
                if j >= 1:
                    conv_dve(j - 1)
            conv_dve(7)
            dve.wait_ge(S["mean_done"], 1)
            step(dve.tensor_scalar(mean, ps[:, 7, 0:T0], 1.0 / D, None, ALU.mult))
            for k in range(KD):
                dve.tensor_tensor(conv_y[:, k, :], conv_y[:, k, :], mean, ALU.subtract).then_inc(S["xc_ready"], 1)
            inverse_root(1, T0, LN_EPS)
            for k in range(KD + 2):
                if k < KD:
                    dve.scalar_tensor_tensor(out=conv_y[:, k, :], in0=conv_y[:, k, :], scalar=vcol("ln_g", k),
                                             in1=rstd[:, 0:T0], op0=ALU.mult, op1=ALU.mult).then_inc(S["normed"], 1)
                if k >= 2:
                    low_part(in_low0[:, k - 2, :], sq[:, k - 2, :], hn_r[:, k - 2, :], "input_low")
            for m in range(KD):
                split_weights((BOFF["pw2"] + m // 2 * KD + KD - 1) // CH + LOOK + m // 6)
                dve.wait_ge(S["pw2_done"], m + 1)
                b = 2 * (m // 2 % 3) + m % 2
                dve.scalar_tensor_tensor(out=h[:, m, :], in0=ps[:, b, 0:T0], scalar=vcol("b_pw2", m),
                                         in1=h[:, m, :], op0=ALU.add, op1=ALU.add).then_inc(S["h1_ready"], 1)

            def ffn(n, norm_i, res, gain, t, x_low, hidden_high, hidden_low, b_in, b_out):
                norm(norm_i, res, hn, gain, t, first_block=b_in, low=x_low)
                for p in range(KF + 1):
                    if p < KF:
                        split_weights((b_in + p * KD + KD - 1) // CH + LOOK)
                        dve.wait_ge(S["ffn_sig"], n * KF + p + 1)
                        dve.tensor_tensor(gate_sb[:, p % 2, 0:t], ps[:, 2 * (p % 3) + 1, 0:t],
                                          gate_sb[:, p % 2, 0:t], ALU.mult).then_inc(S["ffn_mul"], 1)
                    if p:
                        low_part(hidden_low[:, p - 1, 0:t], gate_sb[:, (p - 1) % 2, 0:t],
                                 hidden_high[:, p - 1, 0:t], "ffn_hid")
                for m in range(KD):
                    split_weights((b_out + (m // 2 + 1) * KF - 1) // CH + LOOK)
                    dve.wait_ge(S["ffn_down"], 8 * n + m + 1)
                    b = 2 * (m // 2 % 3) + m % 2
                    dve.tensor_tensor(res[:, m, 0:t], ps[:, b, 0:t], res[:, m, 0:t], ALU.add)\
                       .then_inc(S["ffn_out"], 1)

            ffn(0, 2, h, "ffn_g0", T0, in_low0, hid_high0, hid_low0, BOFF["ffn0_in"], BOFF["ffn0_out"])
            inverse_root(3, T0, EPS)
            for g in range(4):
                for k in (2 * g, 2 * g + 1):
                    dve.scalar_tensor_tensor(out=hn[:, k, :], in0=h[:, k, :], scalar=vcol("mix_g1", k),
                                             in1=rstd[:, 0:T0], op0=ALU.mult, op1=ALU.mult).then_inc(S["normed"], 1)
                dve.wait_ge(S["normed"], 8 * 3 + 2 * g + 2)
                src, width, at = hn[:, 2 * g:2 * g + 2, :], 1, 0
                if g:
                    dve.wait_ge(S["pooled"], g)
                for dst in (pool_a, pool_b, pool_a, pool_b)[:g + 1]:
                    at += width
                    step(dve.tensor_tensor(dst[:, :, at:T0], src[:, :, at:T0], src[:, :, at - width:T0 - width],
                                           ALU.add))
                    src, width = dst, 2 * width
                dve.scalar_tensor_tensor(out=sq256[:, 2 * g:2 * g + 2, :], in0=src[:, :, META:T0],
                                         scalar=1.0 / width, in1=hn[:, 2 * g:2 * g + 2, META:T0],
                                         op0=ALU.mult, op1=ALU.subtract).then_inc(S["pooled"], 1)
            for m in range(KD):
                dve.wait_ge(S["pool_done"], m + 1)
                b = 2 * (m // 2 % 3) + m % 2
                dve.scalar_tensor_tensor(out=x[:, m, :], in0=ps[:, b, 0:SEQ], scalar=vcol("pool_scale", m),
                                         in1=h[:, m, META:T0], op0=ALU.mult, op1=ALU.add).then_inc(S["x_ready"], 1)
            norm(4, x, hn, "ffn_g1", SEQ)
            dve.wait_ge(S["router_done"], 1)
            step(dve.tensor_copy(logit, ps[:, 6, 0:2 * NE].rearrange("p (t e) -> p t e", t=2)))
            for t in range(2):
                step(dve.max(top[:, t, :], logit[:, t, :]))
                step(dve.max_index(idx_u[:, t, :], top[:, t, :], logit[:, t, :]))
            step(dve.tensor_copy(top_i, idx_u[:, :, :]))
            dve.tensor_tensor(gap[:, :, 0:1], top[:, :, 1:2], top[:, :, 0:1], ALU.subtract)\
               .then_inc(S["gap_ready"], 1)
            dve.wait_ge(S["gap_exp"], 1)
            step(dve.tensor_scalar(gap[:, :, 2:3], gap[:, :, 1:2], 1.0, None, ALU.add))
            step(dve.reciprocal(gap[:, :, 3:4], gap[:, :, 2:3]))
            step(dve.tensor_tensor(gap[:, :, 4:5], gap[:, :, 3:4], gap[:, :, 1:2], ALU.mult))
            for t in range(2):
                dve.tensor_scalar(hot1[:, t, :], iota16[:, 0:NE], top_i[:, t, 0:1], None, ALU.is_equal)
                step(dve.tensor_scalar(hot2[:, t, :], iota16[:, 0:NE], top_i[:, t, 1:2], None, ALU.is_equal))
            dve.tensor_tensor(hot, hot1, hot2, ALU.add).then_inc(S["chosen"], 1)
            dve.wait_ge(S["ranks_done"], 1)
            count = small[:, 252:260]
            step(dve.tensor_copy(count, ps[:, 6, 32:40]))
            step(dve.tensor_scalar(over, count, float(CAP), 1.0, ALU.is_gt, ALU.add))
            for n in range(2, -(-SEQ // CAP)):
                step(dve.scalar_tensor_tensor(out=over, in0=count, scalar=float(n * CAP), in1=over,
                                              op0=ALU.is_gt, op1=ALU.add))
            step(dve.tensor_tensor_scan(ends, ones[:, 0:NE], over, 0.0, ALU.mult, ALU.add))
            step(dve.tensor_scalar(owner, iota16[:, :], ends[:, 0:1], None, ALU.is_ge))
            for e in range(1, NE):
                step(dve.scalar_tensor_tensor(out=owner, in0=iota16[:, :], scalar=ends[:, e:e + 1], in1=owner,
                                              op0=ALU.is_ge, op1=ALU.add))
            step(dve.tensor_copy(table[:, 0:16], owner))
            dve.tensor_copy(table[:, 16:17], ends[:, NE - 1:NE]).then_inc(S["table_ready"], 1)
            step(dve.tensor_tensor(begins, ends, over, ALU.subtract))
            step(dve.tensor_scalar(begins, begins, float(CAP), -1.0, ALU.mult, ALU.add))
            for t in range(2):
                ins = dve.tensor_tensor(place[:, t, :], ps[:, 6, 16 + 8 * t:24 + 8 * t], begins, ALU.add)
            step(ins)
            step(dve.tensor_tensor(hot1, hot1, place, ALU.mult))
            step(dve.tensor_tensor(hot2, hot2, place, ALU.mult))
            dve.tensor_reduce(at12[:, 0:2], hot1, AX.X, ALU.add)
            step(dve.tensor_reduce(at12[:, 2:4], hot2, AX.X, ALU.add))

            def picks(to, to2, weigh):
                for t in range(2):
                    if weigh:
                        dve.tensor_scalar(to2[:, t, :], iota_cap[:, :], at12[:, 2 + t:3 + t], gap[:, t, 4:5],
                                          ALU.is_equal, ALU.mult)
                        ins = dve.tensor_scalar(to[:, t, :], iota_cap[:, :], at12[:, t:t + 1], gap[:, t, 3:4],
                                                ALU.is_equal, ALU.mult)
                    else:
                        dve.tensor_scalar(to2[:, t, :], iota_cap[:, :], at12[:, 2 + t:3 + t], None, ALU.is_equal)
                        ins = dve.tensor_scalar(to[:, t, :], iota_cap[:, :], at12[:, t:t + 1], None, ALU.is_equal)
                return ins

            def take_item():
                dve.tensor_copy(x_item.rearrange("p (b k) c -> p b (k c)", b=2), ps[:, 6:8, 0:4 * CAP])\
                   .then_inc(S["pick_ready"], 1)

            step(picks(pick, pick2, False))
            dve.tensor_tensor(pick, pick, pick2, ALU.add).then_inc(S["picks_ready"], 1)
            for n in range(4):
                dve.memset(y_tok[0:CAP, n * WIDE:(n + 1) * WIDE], 0.0).then_inc(S["moe_y"], 1)
            dve.memset(w_row[0:CAP, :], 0.0).then_inc(S["wt_ready"], 1)
            dve.wait_ge(S["pick_done"], 1)
            take_item()
            items = dve.value_load(table[0:1, 16:17], min_val=NE, max_val=MAX_ITEMS)

            def take_sum(n, value):
                dve.wait_ge(S["moe_sum"], value)
                dve.tensor_tensor(x[:, 2 * n:2 * n + 2, :], ps[:, 6 + n % 2, :].rearrange("p (k t) -> p k t", k=2),
                                  x[:, 2 * n:2 * n + 2, :], ALU.add).then_inc(S["moe_out"], 1)

            with dve.Fori(0, items) as i:
                dve.wait_ge(S["wt_ready"], i + 1)
                picks(wpick, wpick2, True).then_inc(S["picks_made"], 1)
                dve.wait_ge(S["picks_made"], i * 2 + 1)
                dve.tensor_tensor(wpick, wpick, wpick2, ALU.add)
                dve.tensor_scalar(at12, at12, -float(CAP), None, ALU.add).then_inc(S["at_moved"], 1)
                dve.wait_ge(S["at_moved"], i + 1)
                picks(pick, pick2, False).then_inc(S["picks_made"], 1)
                dve.wait_ge(S["picks_made"], i * 2 + 2)
                dve.tensor_tensor(pick, pick, pick2, ALU.add).then_inc(S["picks_ready"], 1)
                def split_down(n):
                    dve.wait_ge(S["moe_high"], i * len(MOE_SPLIT) + (n + 1))
                    w_high, w_low, w = moe_split(n)
                    dve.tensor_tensor(w_low, w, w_high.bitcast(F32), ALU.subtract).then_inc(S["moe_low"], 1)

                for p in range(KE + 1):
                    if p < KE:
                        dve.wait_ge(S["moe_sig"], i * KE + (p + 1))
                        dve.tensor_tensor(gate_sb[:, p % 2, 0:CAP], ps[:, 2 * (p % 3) + 1, 0:CAP],
                                          gate_sb[:, p % 2, 0:CAP], ALU.mult).then_inc(S["moe_mul"], 1)
                    if p:
                        dve.wait_ge(S["moe_hid_high"], i * KE + p)
                        dve.tensor_tensor(hid_item_low[:, p - 1, :], gate_sb[:, (p - 1) % 2, 0:CAP],
                                          hid_item_high[:, p - 1, :].bitcast(F32), ALU.subtract)\
                           .then_inc(S["moe_hid"], 1)
                    if p in (5, 6):
                        take_sum(p - 5, i * 4 + (p - 4))
                    if p in (10, 11):
                        take_sum(p - 8, i * 4 + (p - 7))
                    for n in {KE - 3: (0,), KE - 2: (1, 2), KE: (3, 4)}.get(p, ()):
                        split_down(n)
                dve.wait_ge(S["wt_done"], i + 1)
                take_item()
                for j in range(4):
                    for n in moe_splits(j):
                        split_down(n)
            for n in range(4):
                take_sum(n, items * 4 + (n + 1))
            dve.wait_ge(S["moe_out"], items * 4 + 4)
            dve.memset(gap[:, :, 5:6], 0.0).then_inc(S["moe_all"], 1)
            norm(5, x, x, "final_g", SEQ, first_block=BOFF["w_in2"])
            norm(6, x, hn, "pre_g", SEQ, first_block=BOFF["w_in2"] + 2 * CH, low=in_low)
            for kv, name in enumerate(("pek", "pev")):
                step(dve.memset(windows[:, kv, 2, :], 0.0))
                step(dve.tensor_copy(windows[:, kv, 2, 0:32:2], vcol(name, 0, 16)))
            for p in range(24):
                split_weights((BOFF["w_in2"] + p * KD + KD - 1) // CH + LOOK)
                if taker2[p] != "dve":
                    continue
                dve.wait_ge(S["in2_done"], 2 * p + 2)
                b = 2 * (p % 3)
                if p >= 21:
                    c = p - 21
                    ins = dve.tensor_copy(vtok[:, :, c * WIDE:(c + 1) * WIDE], ps[:, b:b + 2, 0:SEQ])
                elif p in (2, 3):
                    dve.tensor_copy(windows[0:64, p - 2, 0:2, :], ps[0:64, b:b + 2, 0:SEQ])
                    ins = dve.tensor_copy(windows[64:P, p - 2, 0:2, 0:SEQ - 1], ps[64:P, b:b + 2, 1:SEQ])
                else:
                    dst, n = tiles2(p)
                    if n < KS or QB <= n < KB:
                        ins = dve.tensor_scalar(dst, ps[:, b:b + 2, 0:SEQ], 0.125, None, ALU.mult)
                    else:
                        ins = dve.tensor_copy(dst, ps[:, b:b + 2, 0:SEQ])
                ins.then_inc(S["in2_dve"], 1)
            for kv in range(2):
                dve.wait_ge(S["cmp_h_done"], kv + 1)
                dve.tensor_copy(cmp_pe[:, kv:kv + 1], ps[:, 2 * kv, 2 * CMP_N:2 * CMP_N + 1]).then_inc(S["cmp_pe_ready"], 1)
            dve.wait_ge(S["cmp_kv_done"], 1)
            dve.tensor_copy(cmp_k[:, 0:CMP_N], ps[:, 6, 64:64 + CMP_N]).then_inc(S["cmp_kv_ready"], 1)
            dve.tensor_copy(cmp_v[0:CMP_N, :], ps[0:CMP_N, 7, 0:P]).then_inc(S["cmp_kv_ready"], 1)
            dve.wait_ge(S["gates_ready"], 1)

            def biased(s):
                j, kind, i, g, br = subs[s]
                dve.wait_ge(S["score_done"], s + 1)
                if s >= 3:
                    dve.wait_ge(S["turn_done"], turns_before[s - 2])
                n = CMP_N if br == "cmp" else (i + 1) * P
                for p in range(4):
                    slope = moba_slope(4 * g + p) if kind == "moba" else nsa_slope(g, p)
                    bias = cbias[:, i, 0:CMP_N] if br == "cmp" else alibi[:, 2 * P - n:2 * P]
                    ins = dve.scalar_tensor_tensor(out=soft[:, s % 3, p, 0:n], in0=bias, scalar=slope,
                                                   in1=ps[:, 2 * (s % 2) + p % 2, (p // 2) * 256:(p // 2) * 256 + n],
                                                   op0=ALU.mult, op1=ALU.add)
                step(ins)
                step(dve.tensor_reduce(stats[:, s % 3, 0, :], soft[:, s % 3, :, 0:n], AX.X, ALU.max))
                dve.tensor_scalar(stats[:, s % 3, 1, :], stats[:, s % 3, 0, :], -1.0, 1.0e20, ALU.mult, ALU.min)\
                   .then_inc(S["s_ready"], 1)

            def scaled(s):
                j, kind, i, g, br = subs[s]
                dve.wait_ge(S["exp_ready"], s + 1)
                n = CMP_N if br == "cmp" else (i + 1) * P
                step(dve.tensor_scalar(stats[:, s % 3, 3, :], stats[:, s % 3, 2, :], 1.0e-30, None, ALU.max))
                step(dve.reciprocal(stats[:, s % 3, 3, :], stats[:, s % 3, 3, :]))
                if kind == "nsa":
                    col = i * 24 + ("cmp", "slc", "win").index(br) * 8 + g * 4
                    step(dve.tensor_tensor(stats[:, s % 3, 3, :], stats[:, s % 3, 3, :], gates[:, col:col + 4],
                                           ALU.mult))
                for p in range(4):
                    ins = dve.tensor_scalar(soft[:, s % 3, p, 0:n], soft[:, s % 3, p, 0:n],
                                            stats[:, s % 3, 3, p:p + 1], None, ALU.mult)
                ins.then_inc(S["prob_ready"], 1)

            def gated(j):
                kind, i, g = jobs[j]
                dve.wait_ge(S["pv_done"], j + 1)
                q = slice(i * P, (i + 1) * P)
                if kind == "nsa":
                    lo = 64 * g
                    ins = dve.tensor_tensor(sq256[lo:lo + 64, 0:4, q],
                                            ps[lo:lo + 64, 6 + j % 2, :].rearrange("p (a t) -> p a t", a=4),
                                            proj[lo:lo + 64, ZA:ZA + 4, q], ALU.mult)
                else:
                    ins = dve.tensor_tensor(sq256[:, 4 + 2 * g:6 + 2 * g, q],
                                            ps[:, 6 + j % 2, 0:2 * P].rearrange("p (a t) -> p a t", a=2),
                                            proj[:, ZB + 2 * g:ZB + 2 * g + 2, q], ALU.mult)
                ins.then_inc(S["y_ready"], 1)

            biased(0)
            biased(1)
            for s in range(len(subs)):
                scaled(s)
                if s + 2 < len(subs):
                    biased(s + 2)
                if s >= 1 and subs[s][0] != subs[s - 1][0]:
                    gated(subs[s - 1][0])
            gated(len(jobs) - 1)
            for m in range(KD):
                j, half = m // 2, m % 2
                dve.wait_ge(S["br_done"], j + 1)
                if m >= 2:
                    dve.wait_ge(S["br_ready"], m - 1)
                for br in range(2):
                    ins = dve.tensor_tensor(part[:, m % 2, br, :], ps[:, 4 * (j % 2) + 2 * br + half, 0:SEQ],
                                            proj[:, MG + 8 * br + m, :], ALU.mult)
                ins.then_inc(S["br_part"], 1)
            for m in range(KD):
                if m in (4, 6):
                    split_weights((BOFF["w_in3"] - 1) // CH + m - 2)
                dve.wait_ge(S["wo2_done"], m + 1)
                b = 2 * (m // 2 % 3) + m % 2
                dve.tensor_copy(zo[:, m, :], ps[:, b, 0:SEQ]).then_inc(S["wo2_ready"], 1)
            inverse_root(7, SEQ, EPS)
            for k in range(KD + 1):
                if k < KD:
                    steps[0] += 1
                    dve.scalar_tensor_tensor(out=zo[:, k, :], in0=zo[:, k, :], scalar=vcol("post_g", k),
                                             in1=rstd[:, 0:SEQ], op0=ALU.mult, op1=ALU.mult)\
                       .then_inc(S["dve_step"], 1)
                if k:
                    dve.wait_ge(S["dve_step"], steps[0] - (k < KD))
                    dve.tensor_tensor(x[:, k - 1, :], x[:, k - 1, :], zo[:, k - 1, :], ALU.add)\
                       .then_inc(S["normed"], 1)

            dve.memset(cpad, 0.0)
            norm(8, x, hn, "mix3_g", SEQ, low=in_low)

            def take3(p):
                dve.wait_ge(S["in3_done"], 2 * p + 2)
                b = 2 * (p % 3)
                if p >= 19:
                    ins = dve.tensor_copy(v3[:, :, (p - 19) * WIDE:(p - 18) * WIDE], ps[:, b:b + 2, 0:SEQ])
                elif 2 * p < L_G:
                    ins = dve.tensor_copy(cin[:, 2 * p:2 * p + 2, 3:3 + SEQ], ps[:, b:b + 2, 0:SEQ])
                elif 2 * p == S_Q:
                    ins = dve.tensor_scalar(proj[:, 2 * p:2 * p + 2, :], ps[:, b:b + 2, 0:SEQ], 0.125, None, ALU.mult)
                else:
                    ins = dve.tensor_copy(proj[:, 2 * p:2 * p + 2, :], ps[:, b:b + 2, 0:SEQ])
                ins.then_inc(S["in3_dve"], 1)

            def conv3(tiles, dst, done):
                for tap in range(4):
                    for n, j in enumerate(tiles):
                        u = cin[:, j, tap:tap + SEQ]
                        w = vcol("conv3", 4 * j + tap)
                        if tap == 0:
                            ins = dve.tensor_scalar(dst[:, n, :], u, w, None, ALU.mult)
                        else:
                            ins = dve.scalar_tensor_tensor(out=dst[:, n, :], in0=u, scalar=w, in1=dst[:, n, :],
                                                           op0=ALU.mult, op1=ALU.add)
                    if tap < 3:
                        step(ins)
                ins.then_inc(done, 1)

            for p in range(21):
                split_weights((BOFF["w_in3"] + p * KD + KD - 1) // CH + LOOK)
                if taker3[p] == "dve":
                    take3(p)
                if p == 7:
                    dve.wait_ge(S["in3_dve"], 3)
                    conv3((0, 1), xa, S["conv3_ready"])
                if p == 13:
                    dve.wait_ge(S["lam_exp"], 1)
                    e_, r_, r2, q_ = lam[:, 1, :], lam[:, 2, :], lam[:, 3, :], lam[:, 4, :]
                    step(dve.tensor_scalar(r_, e_, 2.0, None, ALU.add))
                    step(dve.reciprocal(r_, r_))
                    step(dve.tensor_tensor(r_, r_, e_, ALU.mult))
                    step(dve.tensor_tensor(r2, r_, r_, ALU.mult))
                    step(dve.tensor_scalar(q_, r2, 1.0 / 17, None, ALU.mult))
                    for odd in (15, 13, 11, 9, 7, 5, 3):
                        step(dve.scalar_tensor_tensor(out=q_, in0=q_, scalar=1.0 / odd, in1=r2, op0=ALU.add, op1=ALU.mult))
                    step(dve.scalar_tensor_tensor(out=q_, in0=q_, scalar=1.0, in1=r_, op0=ALU.add, op1=ALU.mult))
                    step(dve.tensor_scalar(r_, vcol("lru_lam", 0, 2), -1.0, 0.0, ALU.mult, ALU.max))
                    step(dve.scalar_tensor_tensor(out=q_, in0=q_, scalar=2.0, in1=r_, op0=ALU.mult, op1=ALU.add))
                    step(dve.tensor_scalar(q_, q_, -8.0, None, ALU.mult))
                if p in (9, 11):
                    conv3((2, 3) if p == 9 else (4, 5), qk3[:, 0:2] if p == 9 else qk3[:, 2:4], S["conv3_ready"])
            for hd in range(4):
                dve.wait_ge(S["sb_z_done"], hd + 1)
                dve.tensor_tensor(zs[:, hd, :], ps[:, hd, 0:3 * P], smask[:, :], ALU.add).then_inc(S["sb_zs"], 1)
            dve.wait_ge(S["if_done"], 1)
            dve.wait_ge(S["in3_act"], taker3.count("act"))
            dve.tensor_scalar(irow, ps[0:4, 6, 0:SEQ], vcol("ig_b", rows=4), None, ALU.add)
            dve.tensor_scalar(frow, ps[0:4, 6, SEQ:2 * SEQ], vcol("fg_b", rows=4), None, ALU.add)\
               .then_inc(S["gate_in"], 1)
            dve.wait_ge(S["lru_sig"], 2)
            for t in range(2):
                ins = dve.tensor_scalar(lru_t[:, 2, t, :], lru_t[:, 0, t, :], q_[:, t:t + 1], None, ALU.mult)
            ins.then_inc(S["lru_loga"], 1)
            step(dve.tensor_tensor(lru_t[:, 1, :, :], lru_t[:, 1, :, :], xa, ALU.mult))
            for hd in range(4):
                dve.wait_ge(S["sb_ln"], hd + 1)
                dve.scalar_tensor_tensor(out=sb_lk[:, hd, :], in0=zs[:, hd, :], scalar=0.0, in1=sb_lk[:, hd, :],
                                         op0=ALU.max, op1=ALU.add).then_inc(S["sb_lk"], 1)
            dve.wait_ge(S["gate_ln"], 1)
            step(dve.scalar_tensor_tensor(out=frow, in0=frow, scalar=0.0, in1=arow, op0=ALU.min, op1=ALU.subtract))
            step(dve.tensor_tensor_scan(brow, ones[0:4, :], frow, 0.0, ALU.mult, ALU.add))
            dve.tensor_tensor(crow, irow, brow, ALU.subtract).then_inc(S["c_ready"], 1)
            dve.wait_ge(S["c_ready"], 1)
            step(dve.tensor_tensor_scan(mrow, crow, crow, 0.0, ALU.max, ALU.max))
            step(dve.tensor_scalar(mrow, mrow, -1.0, None, ALU.mult))
            dve.tensor_tensor(floor, mrow, brow, ALU.subtract).then_inc(S["m_floor_in"], 1)
            dve.wait_ge(S["lru_a"], 2)
            step(dve.tensor_tensor(lru_t[:, 0, :, :], lru_t[:, 3, :, :], lru_t[:, 3, :, :], ALU.mult))
            dve.scalar_tensor_tensor(out=lru_t[:, 2, :, :], in0=lru_t[:, 0, :, :], scalar=1.0,
                                     in1=lru_t[:, 2, :, :], op0=ALU.add, op1=ALU.mult).then_inc(S["lru_f"], 1)
            for hd in range(4):
                dve.wait_ge(S["sb_r_done"], hd + 1)
                dve.tensor_tensor(sb_w[:, hd, :], zs[:, hd, :], ps[:, hd, 0:3 * P], ALU.subtract)\
                   .then_inc(S["sb_arg"], 1)
            dve.wait_ge(S["cT_done"], 1)
            dve.tensor_copy(ccol, ps[:, 7, 0:8]).then_inc(S["cT_ready"], 1)
            dve.wait_ge(S["lru_sqrt"], 1)
            step(dve.tensor_tensor(lru_t[:, 1, :, :], lru_t[:, 1, :, :], lru_t[:, 2, :, :], ALU.mult))
            for t in range(2):
                ins = dve.tensor_tensor_scan(lru_t[:, 0, t, :], lru_t[:, 3, t, :], lru_t[:, 1, t, :], 0.0,
                                             ALU.mult, ALU.add)
            step(ins)
            dve.tensor_tensor(y3[:, 0:2, :], lru_t[:, 0, :, :], proj[:, L_G:L_G + 2, :], ALU.mult)\
               .then_inc(S["lru_in"], 1)
            dve.wait_ge(S["mb_done"], 1)
            dve.wait_ge(S["sb_arg"], 4)
            for hd in range(4):
                nm = ps[:, hd // 2, (hd % 2) * SEQ:(hd % 2 + 1) * SEQ]
                dve.tensor_tensor(decay[:, hd, 0:SEQ], nm, tmask[:, 0:SEQ], ALU.add)
                dve.tensor_tensor(decay[:, hd, SEQ:3 * P], nm[:, P:SEQ], tmask[:, SEQ:3 * P], ALU.add)\
                   .then_inc(S["mb_ready"], 1)
            dve.wait_ge(S["sb_o_done"], 1)
            dve.tensor_copy(y3[:, 4:6, :], ps[:, 4, :].rearrange("p (k t) -> p k t", k=2)).then_inc(S["sb_y"], 1)
            for hd in range(4):
                dve.wait_ge(S["ml_exp"], hd + 1)
                dve.wait_ge(S["ml_s_done"], hd + 1)
                dve.scalar_tensor_tensor(out=sb_w[:, hd, :], in0=decay[:, hd, :], scalar=0.125,
                                         in1=ps[:, hd, 0:3 * P], op0=ALU.mult, op1=ALU.mult).then_inc(S["ml_p"], 1)
            dve.wait_ge(S["fl_ready"], 1)
            dve.wait_ge(S["fl_done"], 1)
            den = lru_t[:, 0, :, :]
            step(dve.tensor_tensor(den, ps[:, 5, :].rearrange("p (k t) -> p k t", k=2), den, ALU.max))
            step(dve.reciprocal(den, den))
            step(dve.tensor_tensor(den, ps[:, 6, :].rearrange("p (k t) -> p k t", k=2), den, ALU.mult))
            dve.tensor_tensor(y3[:, 2:4, :], den, proj[:, M_O:M_O + 2, :], ALU.mult).then_inc(S["mh_ready"], 1)
            dve.wait_ge(S["mh_ready"], 1)
            for m in range(KD):
                j, half = m // 2, m % 2
                dve.wait_ge(S["out3_done"], j + 1)
                if m >= 2:
                    dve.wait_ge(S["merged"], m - 1)
                for br in range(3):
                    ins = dve.tensor_tensor(part3[:, m % 2, br, :], ps[:, 3 * half + br, 0:SEQ],
                                            proj[:, G3 + 8 * br + m, :], ALU.mult)
                ins.then_inc(S["out3_part"], 1)
            for m in range(KD):
                if m in (4, 6):
                    split_weights((BOFF["ffn3_in"] - 1) // CH + m - 2)
                dve.wait_ge(S["wo3_done"], m + 1)
                b = 2 * (m // 2 % 3) + m % 2
                dve.tensor_tensor(x[:, m, :], ps[:, b, 0:SEQ], x[:, m, :], ALU.add).then_inc(S["x3_ready"], 1)
            ffn(1, 9, x, "ffn3_g", SEQ, in_low, hid_high, hid_low, BOFF["ffn3_in"], BOFF["ffn3_out"])
            norm(10, x, hn, "final3_g", SEQ)

        @block.gpsimd
        def _(pool):
            steps = [0]

            def step(ins):
                steps[0] += 1
                ins.then_inc(S["pool_step"], 1)
                pool.wait_ge(S["pool_step"], steps[0])

            pool.memset(ones[:, :], 1.0).then_inc(S["ones_ready"], 1)
            pool.wait_ge(S["ones_ready"], 1)
            step(pool.memset(ident[:, :], 0.0))
            step(pool.affine_select(out=ident[:, :], in_=ident[:, :], compare_op=ALU.not_equal, fill=1.0,
                                    base=0, pattern=[[-1, P]], channel_multiplier=1))
            step(pool.affine_select(out=tri[:, :], in_=ones[:, 0:P], compare_op=ALU.is_ge, fill=0.0,
                                    base=0, pattern=[[-1, P]], channel_multiplier=1))
            step(pool.memset(sel[:, :, :], 0.0))
            step(pool.affine_select(out=sel[:, :, :], in_=sel[:, :, :], compare_op=ALU.not_equal, fill=1.0,
                                    base=0, pattern=[[-1, 4], [0, P]], channel_multiplier=1))
            step(pool.iota(alibi[:, :], pattern=[[1, 2 * P]], base=-P, channel_multiplier=-1,
                           allow_small_or_imprecise_dtypes=True))
            step(pool.affine_select(out=alibi[:, :], in_=alibi[:, :], compare_op=ALU.is_ge, fill=NEG,
                                    base=P, pattern=[[-1, 2 * P]], channel_multiplier=1))
            for i in range(2):
                step(pool.iota(cbias[:, i, :], pattern=[[16, 16]], base=31 - i * P, channel_multiplier=-1,
                               allow_small_or_imprecise_dtypes=True))
                step(pool.affine_select(out=cbias[:, i, :], in_=cbias[:, i, :], compare_op=ALU.is_ge, fill=NEG,
                                        base=i * P - 31, pattern=[[-16, 16]], channel_multiplier=1))
            step(pool.memset(tmask[:, :], 0.0))
            step(pool.memset(smask[:, :], 0.0))
            for m, base in ((tmask, 0), (smask, -1)):
                for lo, hi in ((0, 2 * P), (2 * P, 3 * P)):
                    step(pool.affine_select(out=m[:, lo:hi], in_=m[:, lo:hi], compare_op=ALU.is_ge, fill=NEG,
                                            base=base, pattern=[[1, hi - lo]], channel_multiplier=-1))
            step(pool.affine_select(out=upto[:, :], in_=ones[:, 0:P], compare_op=ALU.is_ge, fill=0.0,
                                    base=0, pattern=[[1, P]], channel_multiplier=-1))
            step(pool.iota(iota_cap[:, :], pattern=[[1, CAP]], base=0, channel_multiplier=0,
                           allow_small_or_imprecise_dtypes=True))
            pool.iota(iota16[:, :], pattern=[[1, 16]], base=0, channel_multiplier=0,
                      allow_small_or_imprecise_dtypes=True).then_inc(S["consts_ready"], 1)
            pool.wait_ge(S["vec_landed"], 16)
            for j in range(8):
                if j >= 2:
                    pool.wait_ge(S["conv_done"], j - 1)
                for tap in range(PE_TAPS):
                    pool.tensor_scalar(diag[:, j % 2, tap, :], ident[:, :], vcol("w_dw", j * CONVW + tap), None,
                                       ALU.mult).then_inc(S["diag_ready"], 1)
            for m in range(KD):
                pool.wait_ge(S["br_part"], m + 1)
                pool.tensor_tensor(hn256[:, m, :], part[:, m % 2, 0, :], part[:, m % 2, 1, :], ALU.add)\
                    .then_inc(S["br_ready"], 1)
            for m in range(KD):
                pool.wait_ge(S["out3_part"], m + 1)
                step(pool.tensor_tensor(part3[:, m % 2, 0, :], part3[:, m % 2, 0, :], part3[:, m % 2, 1, :], ALU.add))
                pool.tensor_tensor(hn256[:, m, :], part3[:, m % 2, 0, :], part3[:, m % 2, 2, :], ALU.add)\
                    .then_inc(S["merged"], 1)


def _kernel_arrays(i):
    def blocks(w):
        k, n = w.shape
        return w.reshape(k // P, P, n // WIDE, WIDE).transpose(2, 0, 1, 3).reshape(-1, P, WIDE)

    def beside(a, b):
        k, n = a.shape
        return np.stack([a.reshape(k, n // P, P), b.reshape(k, n // P, P)], 2).reshape(k, 2 * n)

    def by_group(w, axis):
        s = w.shape
        if axis == 1:
            return w.reshape(s[0], 2, 4, 64).transpose(0, 2, 1, 3).reshape(s)
        return w.reshape(2, 4, 64, s[1]).transpose(1, 0, 2, 3).reshape(s)

    def both(w):
        return np.concatenate([w[:, 0:64], w[:, 0:64], w[:, 64:P], w[:, 64:P]], 1)

    def interleave(ws):
        bs = [blocks(w).reshape(4, -1, P, WIDE) for w in ws]
        return np.concatenate(bs, 1).reshape(-1, P, WIDE)

    a = {n: np.asarray(v) for n, v in i.items()}
    parts = [
        blocks(beside(a["conv_w_pw1"][0][:, :D], a["conv_w_pw1"][0][:, D:])),
        blocks(a["conv_w_pw2"][0]),
        blocks(beside(a["ffn_w_gate"][0], a["ffn_w_up"][0])),
        blocks(a["ffn_w_down"][0]),
        a["pool_w_group"][0].reshape(8, P, WIDE),
        np.zeros((4, P, WIDE), np.float32),
    ]
    for e in range(NE):
        parts += [blocks(beside(a["moe_w_gate"][0, e], a["moe_w_up"][0, e])), blocks(a["moe_w_down"][0, e])]
    w = a["w_in_2"][0]
    q_a, kv, g_a, z_a, qkv_b, z_b, merge = np.split(w, np.cumsum([512, 768, 24, 512, 1536, 512]), 1)
    kv = np.split(kv, 6, 1)
    parts.append(blocks(np.concatenate(
        [by_group(q_a, 1), both(kv[0]), both(kv[1]), kv[2], kv[4], by_group(z_a, 1), qkv_b[:, 0:1024], z_b, merge,
         kv[3], kv[5], qkv_b[:, 1024:1536]], 1)))
    for n in ("cmp_w1_k_2", "cmp_w1_v_2"):
        parts.append(a[n][0].reshape(8, 2, P, P).transpose(0, 2, 1, 3).reshape(8, P, WIDE))
    parts.append(interleave([by_group(a["w_branch_a_2"][0], 0), a["w_branch_b_2"][0]]))
    parts.append(blocks(a["w_o_2"][0]))
    w = a["w_in_3"][0]
    l_x, l_g, m_qk, m_v, m_o, m_if, s_qk, s_v, g3 = np.split(
        w, np.cumsum([256, 256, 512, 256, 256, 8, 512, 256]), 1)
    parts.append(blocks(np.concatenate([l_x, m_qk, l_g, m_o, s_qk, g3, m_v, s_v], 1)))
    parts.append(interleave([a["w_out_lru_3"][0], a["w_out_mlstm_3"][0], a["w_out_sb_3"][0]]))
    parts.append(blocks(a["w_o_3"][0]))
    parts.append(blocks(beside(a["w_ffn_in_3"][0][:, :FF], a["w_ffn_in_3"][0][:, FF:])))
    parts.append(blocks(a["w_ffn_out_3"][0]))
    stream = np.zeros((NCH, P, CH, WIDE), np.float32)
    at = 0
    for p in parts:
        done = 0
        while done < len(p):
            c, o = (at + done) // CH, (at + done) % CH
            if o == 0 and len(p) - done >= CH:
                n = (len(p) - done) // CH
                stream[c:c + n] = p[done:done + n * CH].reshape(n, CH, P, WIDE).transpose(0, 2, 1, 3)
                done += n * CH
            else:
                n = min(CH - o, len(p) - done)
                stream[c, :, o:o + n] = p[done:done + n].transpose(1, 0, 2)
                done += n
        at += len(p)
    assert at == NBLK

    def cols(v):
        return v.reshape(-1, P).T

    def taps(w):
        return w.reshape(w.shape[0], -1, P).transpose(2, 1, 0).reshape(P, -1)

    def tall(v):
        o = np.zeros((P, v.shape[1]), np.float32)
        o[:v.shape[0]] = v
        return o

    def rows(w):
        return w.reshape(-1, P, w.shape[1]).transpose(1, 0, 2).reshape(P, -1)

    vecs = {
        "b_pw1": cols(a["conv_b_pw1"][0]), "w_dw": taps(a["conv_w_dw"][0]), "b_dw": cols(a["conv_b_dw"][0]),
        "ln_g": cols(a["conv_ln_g"][0]), "ln_b": cols(a["conv_ln_b"][0]), "b_pw2": cols(a["conv_b_pw2"][0]),
        "pool_scale": cols(a["pool_scale"][0]), "mix_g0": cols(a["mix_norm_g"][0]), "mix_g1": cols(a["mix_norm_g"][1]),
        "ffn_g0": cols(a["ffn_norm_g"][0]), "ffn_g1": cols(a["ffn_norm_g"][1]), "final_g": cols(a["final_norm_g"]),
        "pre_g": cols(a["norm_pre_2"][0]), "post_g": cols(a["norm_post_2"][0]), "mix3_g": cols(a["norm_mix_g_3"][0]),
        "ffn3_g": cols(a["norm_ffn_g_3"][0]), "final3_g": cols(a["final_norm_g_3"]),
        "conv3": np.concatenate([taps(a["conv_lru_w_3"][0]), taps(a["conv_mlstm_w_3"][0])], 1),
        "lru_ba": cols(a["lru_ba_3"][0]), "lru_bx": cols(a["lru_bx_3"][0]), "lru_lam": cols(a["lru_lambda_3"][0]),
        "ig_b": tall(a["mlstm_ig_b_3"][0][:, None]), "fg_b": tall(a["mlstm_fg_b_3"][0][:, None]),
        "router": rows(a["moe_w_router"][0]), "w_gates": rows(g_a), "w_if": rows(m_if),
        "w2k": a["cmp_w2_k_2"][0], "w2v": a["cmp_w2_v_2"][0],
        "pek": a["cmp_pe_k_2"][0].reshape(16, P).T, "pev": a["cmp_pe_v_2"][0].reshape(16, P).T,
        "lru_wa": rows(a["lru_wa_3"][0].reshape(256, 64)), "lru_wx": rows(a["lru_wx_3"][0].reshape(256, 64)),
    }
    vec = np.concatenate([vecs[n] for n, _ in VECS], 1)
    assert vec.shape == (P, NV)
    h0 = np.concatenate([a["meta_tokens"], a["x"][0]], 0)
    h0 = h0.T.reshape(KD, P, T0).transpose(1, 0, 2)
    return {"w_stream": stream.reshape(NCH, P, CH * WIDE), "vec_in": np.ascontiguousarray(vec),
            "h_in": np.ascontiguousarray(h0)}


def kernel(**inputs):
    import concourse.bacc as _bacc
    from concourse.bass_utils import run_bass_kernel_spmd as _run

    arrays = _kernel_arrays(inputs)
    nc = _bacc.Bacc("TRN2", target_bir_lowering=False, num_devices=1)
    aps = [nc.dram_tensor(n, v.shape, F32, kind="ExternalInput").ap() for n, v in arrays.items()]
    out = nc.dram_tensor("out", (P, KD, SEQ), F32, kind="ExternalOutput").ap()
    program(nc, *aps, out)
    r = _run(nc, [arrays], core_ids=[0])
    got = np.asarray(r.results[0]["out"])
    return np.ascontiguousarray(got.transpose(2, 1, 0).reshape(1, SEQ, D))
```
